# Optimizing a Trainium2 kernel written in Bass

```python
import math
import jax, jax.numpy as jnp
from jax import lax
import numpy as np

D_MODEL = 1024
BATCH = 1
SEQ = 256
DEPTH = 2

N_A_LAYERS = DEPTH // 2
N_B_LAYERS = DEPTH - N_A_LAYERS
EPS = 1e-6
N_ADA = 6

MLSTM_HEADS = 4
MLSTM_QK_DIM = D_MODEL // (2 * MLSTM_HEADS)
MLSTM_V_DIM = D_MODEL // MLSTM_HEADS
MLSTM_CHUNK = 64
GATE_SOFTCAP = 15.0
MLSTM_QK_W = MLSTM_HEADS * MLSTM_QK_DIM
MLSTM_V_W = MLSTM_HEADS * MLSTM_V_DIM
MLSTM_PROJ = 2 * MLSTM_QK_W + MLSTM_V_W + D_MODEL + 2 * MLSTM_HEADS

FOX_HEADS = 8
FOX_HEAD_DIM = D_MODEL // FOX_HEADS
Q_BLOCK = 128

PEER_HEADS = 8
PEER_KEYS = 128
PEER_EXPERTS = PEER_KEYS * PEER_KEYS
PEER_QUERY_DIM = 256
PEER_HALF = PEER_QUERY_DIM // 2
PEER_TOPK = 16
PEER_TOKEN_CHUNK = 128

kernel_name = "yoco_mlstm_fox_peer_adaln"

F32 = jnp.float32

def _ada_rmsnorm(x, gain, shift, scale):
    xf = x.astype(F32)
    xf = xf * lax.rsqrt(jnp.mean(xf * xf, axis=-1, keepdims=True) + EPS) * gain.astype(F32)
    return (xf * (1.0 + scale[:, None, :]) + shift[:, None, :]).astype(x.dtype)

def _head_rms(t, gain):
    tf = t.astype(F32)
    tf = tf * lax.rsqrt(jnp.mean(tf * tf, axis=-1, keepdims=True) + EPS) * gain.astype(F32)
    return tf.astype(t.dtype)

def _softcap(z):
    return GATE_SOFTCAP * jnp.tanh(z / GATE_SOFTCAP)

def _mlstm_chunk_step(carry, inp):
    C, n, m = carry
    q, k, v, ig, lf = inp
    L = q.shape[2]
    causal = jnp.tril(jnp.ones((L, L), dtype=bool))
    b = jnp.cumsum(lf, axis=-1)
    d_log = jnp.where(causal, b[..., :, None] - b[..., None, :] + ig[..., None, :], -jnp.inf)
    inter = b + m[..., None]
    m_t = jnp.maximum(inter, jnp.max(d_log, axis=-1))
    w = jnp.exp(d_log - m_t[..., None])
    a_inter = jnp.exp(inter - m_t)
    s = jnp.einsum('bhtd,bhsd->bhts', q, k) * w
    num = a_inter[..., None] * jnp.einsum('bhtd,bhde->bhte', q, C) + jnp.einsum('bhts,bhse->bhte', s, v)
    den = a_inter * jnp.einsum('bhtd,bhd->bht', q, n) + jnp.sum(s, axis=-1)
    h = num / jnp.maximum(jnp.abs(den), jnp.exp(-m_t))[..., None]
    b_last = b[..., -1]
    g = b_last[..., None] - b + ig
    m_new = jnp.maximum(b_last + m, jnp.max(g, axis=-1))
    w_s = jnp.exp(g - m_new[..., None])
    decay = jnp.exp(b_last + m - m_new)
    C_new = decay[..., None, None] * C + jnp.einsum('bhs,bhsd,bhse->bhde', w_s, k, v)
    n_new = decay[..., None] * n + jnp.einsum('bhs,bhsd->bhd', w_s, k)
    return (C_new, n_new, m_new), h

def _mlstm(xn, w_in, b_i, b_f, h_gain, w_out):
    B, S, _ = xn.shape
    H, DQK, DV, L = MLSTM_HEADS, MLSTM_QK_DIM, MLSTM_V_DIM, MLSTM_CHUNK
    NC = S // L
    p = xn @ w_in
    o1 = MLSTM_QK_W
    o2 = o1 + MLSTM_QK_W
    o3 = o2 + MLSTM_V_W
    o4 = o3 + D_MODEL
    o5 = o4 + H
    q = p[..., :o1].reshape(B, S, H, DQK).astype(F32) * (DQK ** -0.5)
    k = p[..., o1:o2].reshape(B, S, H, DQK).astype(F32)
    v = p[..., o2:o3].reshape(B, S, H, DV).astype(F32)
    o_gate = jax.nn.sigmoid(p[..., o3:o4])
    ig = _softcap(p[..., o4:o5].astype(F32) + b_i.astype(F32))
    lf = jax.nn.log_sigmoid(_softcap(p[..., o5:].astype(F32) + b_f.astype(F32)))

    def to_chunks(t):
        return t.reshape(B, NC, L, H, t.shape[-1]).transpose(1, 0, 3, 2, 4)

    def gate_chunks(t):
        return t.reshape(B, NC, L, H).transpose(1, 0, 3, 2)

    init = (jnp.zeros((B, H, DQK, DV), F32), jnp.zeros((B, H, DQK), F32), jnp.zeros((B, H), F32))
    _, h = lax.scan(_mlstm_chunk_step, init,
                    (to_chunks(q), to_chunks(k), to_chunks(v), gate_chunks(ig), gate_chunks(lf)))
    h = h.transpose(1, 0, 3, 2, 4).reshape(B, S, H, DV)
    h = _head_rms(h, h_gain.reshape(H, DV)).reshape(B, S, D_MODEL).astype(xn.dtype)
    return (o_gate * h) @ w_out

def _shared_kv(x, cs, ada_w, ada_b, norm_g, w_kv, b_f, k_gain):
    B, S, _ = x.shape
    mod = cs @ ada_w.astype(F32) + ada_b.astype(F32)
    sh, sc = jnp.split(mod, 2, axis=-1)
    xn = _ada_rmsnorm(x, norm_g, sh, sc)
    p = xn @ w_kv
    k = _head_rms(p[..., :D_MODEL].reshape(B, S, FOX_HEADS, FOX_HEAD_DIM), k_gain)
    v = p[..., D_MODEL:2 * D_MODEL].reshape(B, S, FOX_HEADS, FOX_HEAD_DIM)
    log_f = jax.nn.log_sigmoid(p[..., 2 * D_MODEL:].astype(F32) + b_f.astype(F32))
    f_cum = jnp.cumsum(log_f, axis=1).transpose(0, 2, 1)
    return k.transpose(0, 2, 1, 3), v.transpose(0, 2, 1, 3), f_cum

def _fox(xn, w_qo, q_gain, w_out, k, v, f_cum):
    B, S, _ = xn.shape
    p = xn @ w_qo
    q = _head_rms(p[..., :D_MODEL].reshape(B, S, FOX_HEADS, FOX_HEAD_DIM), q_gain).transpose(0, 2, 1, 3)
    o_gate = jax.nn.sigmoid(p[..., D_MODEL:])
    scale = FOX_HEAD_DIM ** -0.5
    outs = []
    for blk in range(S // Q_BLOCK):
        lo, hi = blk * Q_BLOCK, (blk + 1) * Q_BLOCK
        logits = jnp.einsum('bhqd,bhkd->bhqk', q[:, :, lo:hi], k[:, :, :hi]).astype(F32) * scale
        logits = logits + f_cum[:, :, lo:hi, None] - f_cum[:, :, None, :hi]
        mask = jnp.arange(hi)[None, :] <= jnp.arange(lo, hi)[:, None]
        probs = jax.nn.softmax(jnp.where(mask, logits, -jnp.inf), axis=-1)
        outs.append(jnp.einsum('bhqk,bhkd->bhqd', probs.astype(v.dtype), v[:, :, :hi]))
    att = jnp.concatenate(outs, axis=2).transpose(0, 2, 1, 3).reshape(B, S, D_MODEL)
    return (o_gate * att) @ w_out

def _peer(xn, wq, subkeys, u, v):
    B, S, D = xn.shape
    tokens = xn.reshape(B * S // PEER_TOKEN_CHUNK, PEER_TOKEN_CHUNK, D)
    K = PEER_TOPK

    def chunk(xc):
        T = xc.shape[0]
        q = (xc @ wq).reshape(T, PEER_HEADS, 2, PEER_HALF)
        s = jnp.einsum('thpd,pkd->thpk', q, subkeys).astype(F32)
        s_top, i_top = lax.top_k(s, K)
        cand_s = (s_top[:, :, 0, :, None] + s_top[:, :, 1, None, :]).reshape(T, PEER_HEADS, K * K)
        cand_i = (i_top[:, :, 0, :, None] * PEER_KEYS + i_top[:, :, 1, None, :]).reshape(T, PEER_HEADS, K * K)
        best_s, pos = lax.top_k(cand_s, K)
        idx = jnp.take_along_axis(cand_i, pos, axis=-1)
        gate = jax.nn.softmax(best_s, axis=-1)
        u_sel = jnp.take(u, idx, axis=0)
        act = jax.nn.gelu(jnp.einsum('thkd,td->thk', u_sel, xc).astype(F32), approximate=False)
        v_sel = jnp.take(v, idx, axis=0)
        return jnp.einsum('thk,thkd->td', (gate * act).astype(v.dtype), v_sel)

    return lax.map(chunk, tokens).reshape(B, S, D)

def setup_inputs(seed: int = 0) -> dict:
    key = jax.random.key(seed)
    ks = jax.random.split(key, 26)
    D = D_MODEL
    s = D ** -0.5

    def nrm(k, shape, scale):
        return jax.random.normal(k, shape, F32) * scale

    def gain(k, shape):
        return 1.0 + 0.02 * jax.random.normal(k, shape, F32)

    return {
        "x": nrm(ks[0], (BATCH, SEQ, D), 1.0),
        "c": nrm(ks[1], (BATCH, D), 1.0),
        "ada_w": nrm(ks[2], (DEPTH, D, N_ADA * D), s),
        "ada_b": nrm(ks[3], (DEPTH, N_ADA * D), 0.02),
        "mix_norm": gain(ks[4], (DEPTH, D)),
        "ffn_norm": gain(ks[5], (DEPTH, D)),
        "a_w_in": nrm(ks[6], (N_A_LAYERS, D, MLSTM_PROJ), s),
        "a_b_i": nrm(ks[7], (N_A_LAYERS, MLSTM_HEADS), 0.1),
        "a_b_f": 3.0 + 3.0 * jax.random.uniform(ks[8], (N_A_LAYERS, MLSTM_HEADS), F32),
        "a_h_norm": gain(ks[9], (N_A_LAYERS, D)),
        "a_w_out": nrm(ks[10], (N_A_LAYERS, D, D), s),
        "kv_ada_w": nrm(ks[11], (D, 2 * D), s),
        "kv_ada_b": nrm(ks[12], (2 * D,), 0.02),
        "kv_norm": gain(ks[13], (D,)),
        "kv_w": nrm(ks[14], (D, 2 * D + FOX_HEADS), s),
        "kv_b_f": 2.0 + 0.5 * jax.random.normal(ks[15], (FOX_HEADS,), F32),
        "kv_k_norm": gain(ks[16], (FOX_HEAD_DIM,)),
        "b_w_qo": nrm(ks[17], (N_B_LAYERS, D, 2 * D), s),
        "b_q_norm": gain(ks[18], (N_B_LAYERS, FOX_HEAD_DIM)),
        "b_w_out": nrm(ks[19], (N_B_LAYERS, D, D), s),
        "peer_wq": nrm(ks[20], (DEPTH, D, PEER_HEADS * PEER_QUERY_DIM), s),
        "peer_subkeys": nrm(ks[21], (DEPTH, 2, PEER_KEYS, PEER_HALF), PEER_HALF ** -0.5),
        "peer_u": nrm(ks[22], (DEPTH, PEER_EXPERTS, D), s),
        "peer_v": nrm(ks[23], (DEPTH, PEER_EXPERTS, D), PEER_HEADS ** -0.5),
    }

def reference(x, c, ada_w, ada_b, mix_norm, ffn_norm, a_w_in, a_b_i, a_b_f, a_h_norm, a_w_out,
              kv_ada_w, kv_ada_b, kv_norm, kv_w, kv_b_f, kv_k_norm, b_w_qo, b_q_norm, b_w_out,
              peer_wq, peer_subkeys, peer_u, peer_v):
    cs = jax.nn.silu(c.astype(F32))
    k_sh = v_sh = f_cum = None
    for l in range(DEPTH):
        mod = cs @ ada_w[l].astype(F32) + ada_b[l].astype(F32)
        sh1, sc1, g1, sh2, sc2, g2 = jnp.split(mod, N_ADA, axis=-1)
        xn = _ada_rmsnorm(x, mix_norm[l], sh1, sc1)
        if l < N_A_LAYERS:
            y = _mlstm(xn, a_w_in[l], a_b_i[l], a_b_f[l], a_h_norm[l], a_w_out[l])
        else:
            j = l - N_A_LAYERS
            y = _fox(xn, b_w_qo[j], b_q_norm[j], b_w_out[j], k_sh, v_sh, f_cum)
        x = x + (g1[:, None, :] * y.astype(F32)).astype(x.dtype)
        xn = _ada_rmsnorm(x, ffn_norm[l], sh2, sc2)
        y = _peer(xn, peer_wq[l], peer_subkeys[l], peer_u[l], peer_v[l])
        x = x + (g2[:, None, :] * y.astype(F32)).astype(x.dtype)
        if l == N_A_LAYERS - 1:
            k_sh, v_sh, f_cum = _shared_kv(x, cs, kv_ada_w, kv_ada_b, kv_norm, kv_w, kv_b_f, kv_k_norm)
    return x


_drawn_inputs = setup_inputs


def setup_inputs(seed=0):
    import zlib

    import numpy as np

    out = dict(_drawn_inputs(seed))
    spreads = {}
    factors = {'a_b_i': 8.0,
     'a_h_norm': 3.208,
     'kv_ada_b': 4.393,
     'kv_norm': 6.573,
     'kv_k_norm': 7.718,
     'b_q_norm': 8.0}
    for name, (base, spread) in spreads.items():
        noise = np.random.default_rng([zlib.crc32(name.encode()), seed]).standard_normal(out[name].shape)
        drawn = base * np.exp(spread * noise) if base else spread * noise
        out[name] = __import__('jax').numpy.asarray(drawn.astype(out[name].dtype))
    for name, factor in factors.items():
        out[name] = (out[name] * factor).astype(out[name].dtype)
    return out
```

```python
from contextlib import ExitStack

import concourse.bass as bass
from concourse import mybir

F32 = mybir.dt.float32
F32R = mybir.dt.float32r
U32 = mybir.dt.uint32
ALU = mybir.AluOpType
ACT = mybir.ActivationFunctionType
AX = mybir.AxisListType

P = 128
D = 1024
DC = D // P
T = 256
G = T // P
EPS = 1e-6
NEG = -1e30
LOWEST = -3.0e38
N_ADA = 6

ML_H = 4
ML_DK = D // (2 * ML_H)
ML_DV = D // ML_H
CAP = 15.0

FX_H = 8
FX_D = D // FX_H

PR_H = 8
PR_KEYS = 128
PR_EXPERTS = PR_KEYS * PR_KEYS
PR_K = 16
PR_ROWS = 2 * PR_H
SEL = PR_H * PR_K

WCOLS = 512
MODS = 2 * N_ADA * DC + 2 * DC

def mod_col(layer, what):
    return (layer * N_ADA + what) * DC
SH1, SC1, G1, SH2, SC2, G2 = range(N_ADA)
KV_SH = 2 * N_ADA * DC
KV_SC = KV_SH + DC
MIX_NORM, FFN_NORM, KV_NORM, H_NORM, K_NORM, Q_NORM = 0, 2 * DC, 4 * DC, 5 * DC, 6 * DC, 6 * DC + 1
GAINS = 6 * DC + 2


class Count:

    def __init__(self):
        self.n = 0

    def up(self):
        self.n += 1
        return self.n


class Chip:

    def __init__(self, nc, ctx):
        self.nc = nc
        sb = lambda name, shape, dt=F32: ctx.enter_context(nc.sbuf_tensor(name, shape, dt))
        self.x = sb("x_res", [P, G, D])
        self.mod = sb("mod", [P, MODS])
        self.gains = sb("gains", [P, GAINS])
        self.ident = sb("ident", [P, P])
        self.ones = sb("ones", [P, P])
        self.minus_half = sb("minus_half", [P, 1])
        self.iota = sb("iota", [P, P])
        self.bank = [ctx.enter_context(nc.psum_tensor(f"bank{k}", [P, 512], F32)) for k in range(8)]


class Phase:

    def __init__(self, nc, ctx, tag):
        self.nc, self.ctx, self.tag = nc, ctx, tag
        self.sems = []
        ctx.callback(self.close)

    def close(self):
        if self.sems:
            self.nc.clear_and_free_semaphores(self.sems)
            self.nc.all_engine_barrier()

    def sb(self, name, shape, dt=F32):
        return self.ctx.enter_context(self.nc.sbuf_tensor(f"{self.tag}_{name}", shape, dt))

    def sem(self, name):
        self.sems.append(self.nc.alloc_semaphore(f"{self.tag}_{name}"))
        return self.sems[-1]



def adaln_vectors(nc, chip, a):
    with ExitStack() as ctx:
        ph = Phase(nc, ctx, "ada")
        NW = 3
        wide = N_ADA * D
        wst = [ph.sb(f"w{k}", [P, wide]) for k in range(NW)]
        acc = [ph.sb(f"acc{k}", [P, wide]) for k in range(2)]
        cs = ph.sb("cs", [P, DC])
        sig = ph.sb("sig", [P, DC])
        vb = ph.sb("vb", [MODS, P])
        vg = ph.sb("vg", [GAINS, P])
        c_in, rows_in, x_in = ph.sem("c_in"), ph.sem("rows_in"), ph.sem("x_in")
        w_in = [ph.sem(f"w_in{k}") for k in range(NW)]
        const_done, sig_done, cs_done = ph.sem("const_done"), ph.sem("sig_done"), ph.sem("cs_done")
        summed, mod_ps, vec_ps, mod_done = ph.sem("summed"), ph.sem("mod_ps"), ph.sem("vec_ps"), ph.sem("mod_done")
        bias_done = ph.sem("bias_done")
        pool_step = ph.sem("pool_step")
        mats = [(a["ada_w"][0], wide), (a["ada_w"][1], wide), (a["kv_ada_w"], 2 * D)]
        steps = [(m, k) for m in range(3) for k in range(DC)]
        bank = chip.bank
        mps, bps, gps = bank[0], bank[1], bank[2]
        block = ctx.enter_context(nc.Block())

        @block.sync
        def _(eng):
            eng.dma_start(cs[:, :], a["c"].rearrange("o (p k) -> (o p) k", k=DC)).then_inc(c_in, 16)
            for n, (m, k) in enumerate(steps):
                w, width = mats[m]
                if n >= NW:
                    eng.wait_ge(summed, n - NW + 1)
                eng.dma_start(wst[n % NW][:, 0:width],
                              w.rearrange("(p k) n -> p k n", k=DC)[:, k, :]).then_inc(w_in[n % NW], 16)

        @block.scalar
        def _(eng):
            rows = [(vb, a["ada_b"].rearrange("l (j p) -> (l j) p", p=P), 0, 2 * N_ADA * DC),
                    (vb, a["kv_ada_b"].rearrange("(j p) -> j p", p=P), KV_SH, 2 * DC),
                    (vg, a["mix_norm"].rearrange("l (j p) -> (l j) p", p=P), MIX_NORM, 2 * DC),
                    (vg, a["ffn_norm"].rearrange("l (j p) -> (l j) p", p=P), FFN_NORM, 2 * DC),
                    (vg, a["kv_norm"].rearrange("(j p) -> j p", p=P), KV_NORM, DC),
                    (vg, a["a_h_norm"].rearrange("l (j p) -> (l j) p", p=P), H_NORM, DC),
                    (vg, a["kv_k_norm"].rearrange("(j p) -> j p", p=P), K_NORM, 1),
                    (vg, a["b_q_norm"].rearrange("l (j p) -> (l j) p", p=P), Q_NORM, 1)]
            for dst, src, at, n in rows:
                eng.dma_start(dst[at:at + n, :], src).then_inc(rows_in, 16)
            for g in range(G):
                eng.dma_start(chip.x[:, g, :], a["x"][g * P:(g + 1) * P, :]).then_inc(x_in, 16)
            eng.wait_ge(c_in, 16)
            eng.activation(sig[:, :], cs[:, :], ACT.Sigmoid).then_inc(sig_done, 1)
            eng.wait_ge(vec_ps, 2)
            eng.activation(chip.gains[:, :], gps[:, 0:GAINS], ACT.Copy).then_inc(bias_done, 1)
            eng.wait_ge(bias_done, 1)
            eng.wait_ge(x_in, 16 * G)

        @block.gpsimd
        def _(eng):
            eng.memset(chip.ident[:, :], 0.0).then_inc(pool_step, 1)
            eng.memset(chip.ones[:, :], 1.0).then_inc(const_done, 1)
            eng.memset(chip.minus_half[:, :], -0.5).then_inc(const_done, 1)
            eng.wait_ge(pool_step, 1)
            eng.affine_select(out=chip.ident[:, :], in_=chip.ident[:, :], compare_op=ALU.not_equal, fill=1.0,
                              base=0, pattern=[[-1, P]], channel_multiplier=1).then_inc(const_done, 1)
            eng.iota(chip.iota[:, :], [[1, P]], base=0, channel_multiplier=0,
                     allow_small_or_imprecise_dtypes=True).then_inc(const_done, 1)

        @block.vector
        def _(eng):
            eng.wait_ge(sig_done, 1)
            eng.tensor_tensor(cs[:, :], cs[:, :], sig[:, :], ALU.mult).then_inc(cs_done, 1)
            eng.wait_ge(cs_done, 1)
            for n, (m, k) in enumerate(steps):
                width = mats[m][1]
                eng.wait_ge(w_in[n % NW], 16 * (n // NW + 1))
                dst = acc[m % 2][:, 0:width]
                if k == 0:
                    if m == 2:
                        eng.wait_ge(mod_ps, 1)
                    eng.tensor_scalar(dst, wst[n % NW][:, 0:width], cs[:, k:k + 1], None, ALU.mult).then_inc(summed, 1)
                else:
                    eng.wait_ge(summed, n)
                    eng.scalar_tensor_tensor(out=dst, in0=wst[n % NW][:, 0:width], scalar=cs[:, k:k + 1], in1=dst,
                                             op0=ALU.mult, op1=ALU.add).then_inc(summed, 1)
            eng.wait_ge(mod_ps, 3)
            eng.wait_ge(vec_ps, 1)
            eng.tensor_copy(chip.mod[:, :], bps[:, 0:MODS]).then_inc(mod_done, 1)
            eng.wait_ge(mod_done, 1)
            eng.tensor_tensor(chip.mod[:, :], chip.mod[:, :], mps[:, 0:MODS], ALU.add).then_inc(mod_done, 1)
            eng.wait_ge(mod_done, 2)

        @block.tensor
        def _(eng):
            eng.wait_ge(const_done, 4)
            eng.wait_ge(rows_in, 16 * 8)
            eng.transpose(bps[:, 0:MODS], vb[:, :], chip.ident[0:MODS, 0:MODS]).then_inc(vec_ps, 1)
            eng.transpose(gps[:, 0:GAINS], vg[:, :], chip.ident[0:GAINS, 0:GAINS]).then_inc(vec_ps, 1)
            at = 0
            for m in range(3):
                eng.wait_ge(summed, DC * (m + 1))
                for j in range(mats[m][1] // P):
                    mm = eng.matmul(mps[:, at:at + 1], acc[m % 2][:, j * P:(j + 1) * P], chip.ones[:, 0:1],
                                    start=True, stop=True)
                    at += 1
                mm.then_inc(mod_ps, 1)



class Norm:

    def __init__(self, ph, chip, shift, scale, gain, tag=""):
        self.chip, self.shift, self.scale, self.gain = chip, shift, scale, gain
        self.xs = ph.sb(f"xs{tag}", [P, G, D])
        self.xnT = ph.sb(f"xnT{tag}", [P, DC, T])
        self.ss = ph.sb(f"ss{tag}", [P, G])
        self.coef = ph.sb(f"coef{tag}", [P, DC])
        self.squared, self.scaled, self.turned, self.done = (
            ph.sem(f"norm_{n}{tag}") for n in ("squared", "scaled", "turned", "done"))
        self.step, self.mean, self.root = (ph.sem(f"norm_{n}{tag}") for n in ("step", "mean", "root"))

    def act(self, eng):
        for g in range(G):
            eng.activation(self.xs[:, g, :], self.chip.x[:, g, :], ACT.Square,
                           accum_out=self.ss[:, g:g + 1]).then_inc(self.squared, 1)

    def dve(self, eng):
        n = Count()
        chip = self.chip
        eng.scalar_tensor_tensor(out=self.coef[:, :], in0=chip.mod[:, self.scale:self.scale + DC], scalar=1.0,
                                 in1=chip.gains[:, self.gain:self.gain + DC], op0=ALU.add, op1=ALU.mult
                                 ).then_inc(self.step, 1)
        eng.wait_ge(self.step, n.up())
        eng.wait_ge(self.squared, G)
        eng.tensor_scalar(self.ss[:, :], self.ss[:, :], 1.0 / D, EPS, ALU.mult, ALU.add).then_inc(self.mean, 1)
        eng.wait_ge(self.root, 1)
        for g in range(G):
            eng.tensor_scalar(self.xs[:, g, :], chip.x[:, g, :], self.ss[:, g:g + 1], None,
                              ALU.mult).then_inc(self.scaled, 1)
        for c in range(DC):
            eng.wait_ge(self.turned, c // 2 + 1)
            at = (c % 2) * T
            eng.tensor_scalar(self.xnT[:, c, :], chip.bank[c // 2][:, at:at + T], self.coef[:, c:c + 1],
                              chip.mod[:, self.shift + c:self.shift + c + 1], ALU.mult, ALU.add
                              ).then_inc(self.done, 1)

    def pool(self, eng):
        eng.wait_ge(self.mean, 1)
        rsqrt(eng, self.chip, self.ss[:, :], [P, G]).then_inc(self.root, 1)

    def pe(self, eng):
        eng.wait_ge(self.scaled, G)
        turn_to_features(eng, self.chip, self.xs, self.turned)


def rsqrt(eng, chip, values, shape):
    return eng.tensor_tensor(values, values, chip.minus_half[:, 0:1].to_broadcast(shape), ALU.pow)


def turn_to_features(eng, chip, src, turned):
    for c in range(DC):
        for g in range(G):
            at = (c % 2) * T + g * P
            mm = eng.transpose(chip.bank[c // 2][:, at:at + P], src[:, g, c * P:(c + 1) * P], chip.ident[:, :])
        if c % 2:
            mm.then_inc(turned, 1)


class Project:

    SLOTS = 3

    def __init__(self, ph, blocks, tag="", slots=None):
        self.blocks = blocks
        self.slots = slots or [ph.sb(f"wst{tag}{k}", [P, DC, WCOLS]) for k in range(self.SLOTS)]
        self.loaded = [ph.sem(f"w_loaded{tag}{k}") for k in range(self.SLOTS)]
        self.done = ph.sem(f"projected{tag}")
        self.units, self.last = [], []
        for b, (_, _, width, fm) in enumerate(blocks):
            self.units += [(b, n) for n in range(width // T if fm else G)]
            self.last.append(len(self.units))

    def load(self, eng):
        for b, (w, col, width, _) in enumerate(self.blocks):
            if b >= self.SLOTS:
                eng.wait_ge(self.done, self.last[b - self.SLOTS])
            eng.dma_start(self.slots[b % self.SLOTS][:, :, 0:width],
                          w.rearrange("(c p) n -> p c n", p=P)[:, :, col:col + width]
                          ).then_inc(self.loaded[b % self.SLOTS], 16)

    def unit(self, eng, u, out, xT):
        b, n = self.units[u]
        _, _, width, fm = self.blocks[b]
        w = self.slots[b % self.SLOTS]
        eng.wait_ge(self.loaded[b % self.SLOTS], 16 * (b // self.SLOTS + 1))
        if fm:
            for half in range(2):
                f = n * T + half * P
                for c in range(DC):
                    mm = eng.matmul(out[:, half * T:(half + 1) * T], w[:, c, f:f + P], xT[:, c, :],
                                    start=(c == 0), stop=(c == DC - 1))
        else:
            for c in range(DC):
                mm = eng.matmul(out[:, 0:width], xT[:, c, n * P:(n + 1) * P], w[:, c, 0:width],
                                start=(c == 0), stop=(c == DC - 1))
        mm.then_inc(self.done, 1)


class Residual:

    def __init__(self, ph, chip, gate, banks, diag=None, row=None):
        self.chip, self.gate, self.banks = chip, gate, banks
        self.diag = diag if diag is not None else ph.sb("gate_diag", [P, D])
        self.row = row if row is not None else ph.sb("gate_row", [P, D])
        self.diag_done, self.spread, self.row_done, self.step = (
            ph.sem(n) for n in ("gate_diag_done", "gate_spread", "gate_row_done", "residual_step"))

    def dve_diag(self, eng):
        for c in range(DC):
            eng.tensor_scalar(self.diag[:, c * P:(c + 1) * P], self.chip.ident[:, :],
                              self.chip.mod[:, self.gate + c:self.gate + c + 1], None, ALU.mult
                              ).then_inc(self.diag_done, 1)

    def pe(self, eng):
        eng.wait_ge(self.diag_done, DC)
        for half in range(2):
            eng.matmul(self.banks[half][:, :], self.chip.ones[:, :], self.diag[:, half * 512:(half + 1) * 512],
                       start=True, stop=True).then_inc(self.spread, 1)

    def act(self, eng):
        for half in range(2):
            eng.wait_ge(self.spread, half + 1)
            eng.activation(self.row[:, half * 512:(half + 1) * 512], self.banks[half][:, :], ACT.Copy
                           ).then_inc(self.row_done, 1)

    def dve_add(self, eng, y_banks, wait_for_y):
        n = Count()
        for g in range(G):
            for half in range(2):
                cols = slice(half * 512, (half + 1) * 512)
                if g == 0:
                    eng.wait_ge(self.row_done, half + 1)
                wait_for_y(g, half)
                tmp = self.diag[:, cols] if g == 0 else self.diag[:, cols]
                eng.tensor_tensor(tmp, y_banks[g][half][:, :], self.row[:, cols], ALU.mult).then_inc(self.step, 1)
                eng.wait_ge(self.step, n.up())
                eng.tensor_tensor(self.chip.x[:, g, cols], self.chip.x[:, g, cols], tmp, ALU.add
                                  ).then_inc(self.step, 1)
                eng.wait_ge(self.step, n.up())



def mlstm(nc, chip, a):
    with ExitStack() as ctx:
        ph = Phase(nc, ctx, "ml")
        bank = chip.bank
        w = a["a_w_in"][0]
        qk, vw = ML_H * ML_DK, ML_H * ML_DV
        norm = Norm(ph, chip, mod_col(0, SH1), mod_col(0, SC1), MIX_NORM)
        GATES = 2 * qk + vw + D
        blocks = [(w, GATES, 2 * ML_H, None), (w, 0, WCOLS, True), (w, qk, WCOLS, True)]
        blocks += [(w, 2 * qk + n * WCOLS, WCOLS, False) for n in range(4)]
        blocks += [(a["a_w_out"][0], n * WCOLS, WCOLS, False) for n in range(2)]
        pj = Project(ph, blocks)
        pj.units = [(b, n) for b, n in pj.units if not (b == 0 and n == 1)]
        pj.last = [n - 1 for n in pj.last]
        U_Q, U_K, U_V, U_O, U_OUT = 1, 3, 5, 9, 13
        qT = ph.sb("qT", [P, ML_H, T])
        kT = ph.sb("kT", [P, ML_H, T])
        vx = ph.sb("vx", [P, G, ML_H, ML_DV + 1])
        so = ph.sb("so", [P, G, D])
        num = ph.sb("num", [P, G, ML_H, ML_DV + 1])
        y = ph.sb("y", [P, G, D])
        yT = ph.sb("yT", [P, DC, T])
        bi, bf = ph.sb("bi", [ML_H, 1]), ph.sb("bf", [ML_H, 1])
        ti, tf = ph.sb("ti", [ML_H, T]), ph.sb("tf", [ML_H, T])
        soft = ph.sb("soft", [ML_H, T])
        B, ai, M, em = (ph.sb(n, [ML_H, T]) for n in ("B", "ai", "M", "em"))
        sel = ph.sb("sel", [ML_H, ML_H, P])
        tri = ph.sb("tri", [P, P])
        acol = ph.sb("acol", [P, G, ML_H])
        ecol = ph.sb("ecol", [P, G, ML_H])
        arg = [ph.sb(f"arg{k}", [P, G, P]) for k in range(2)]
        pw = [ph.sb(f"pw{k}", [P, 3, P]) for k in range(2)]
        sd = [ph.sb(f"sd{k}", [P, 3, P]) for k in range(2)]
        junk = ph.sb("junk", [P, ML_DV])
        ssq, den, rr = (ph.sb(n, [P, G, ML_H]) for n in ("ssq", "den", "rr"))
        res = Residual(ph, chip, mod_col(0, G1), [bank[2], bank[3]])

        b_in, bias_ready, const_done = ph.sem("b_in"), ph.sem("bias_ready"), ph.sem("const_done")
        pool_step, dve_step, act_step = ph.sem("pool_step"), ph.sem("dve_step"), ph.sem("act_step")
        evac = ph.sem("evacuated")
        tanh_done, logf_done = ph.sem("tanh_done"), ph.sem("logf_done")
        m_done, em_done, cols_ps, cols_done = ph.sem("m_done"), ph.sem("em_done"), ph.sem("cols_ps"), ph.sem("cols_done")
        em_arg, mean_done, root_done = ph.sem("em_arg"), ph.sem("mean_done"), ph.sem("root_done")
        row_ps, score_ps, arg_done, pw_done, sd_done = (
            ph.sem(n) for n in ("row_ps", "score_ps", "arg_done", "pw_done", "sd_done"))
        num_ps, num_done, y_done, turned, yT_done = (
            ph.sem(n) for n in ("num_ps", "num_done", "y_done", "turned", "yT_done"))
        block = ctx.enter_context(nc.Block())

        def unit_bank(u):
            return bank[(4 + u) % 8]

        @block.sync
        def _(eng):
            eng.dma_start(bi[:, :], a["a_b_i"].rearrange("o h -> h o")).then_inc(b_in, 16)
            eng.dma_start(bf[:, :], a["a_b_f"].rearrange("o h -> h o")).then_inc(b_in, 16)
            pj.load(eng)

        @block.gpsimd
        def _(eng):
            eng.memset(sel[:, :, :], 0.0).then_inc(pool_step, 1)
            eng.memset(tri[:, :], 0.0).then_inc(pool_step, 1)
            eng.memset(vx[:, :, :, ML_DV:ML_DV + 1], 1.0).then_inc(const_done, 1)
            eng.wait_ge(pool_step, 2)
            eng.affine_select(out=sel[:, :, :], in_=sel[:, :, :], compare_op=ALU.not_equal, fill=1.0, base=0,
                              pattern=[[-1, ML_H], [0, P]], channel_multiplier=1).then_inc(const_done, 1)
            eng.affine_select(out=tri[:, :], in_=tri[:, :], compare_op=ALU.is_ge, fill=NEG, base=0,
                              pattern=[[1, P]], channel_multiplier=-1).then_inc(const_done, 1)
            norm.pool(eng)
            eng.wait_ge(mean_done, 1)
            rsqrt(eng, chip, rr[:, :, :].rearrange("p g h -> p (g h)"), [P, G * ML_H]).then_inc(root_done, 1)

        @block.tensor
        def _(eng):
            norm.pe(eng)
            eng.wait_ge(norm.done, DC)
            eng.wait_ge(pj.loaded[0], 16)
            for n in range(2):
                for c in range(DC):
                    mm = eng.matmul(unit_bank(0)[0:ML_H, n * T:(n + 1) * T],
                                    pj.slots[0][:, c, n * ML_H:(n + 1) * ML_H], norm.xnT[:, c, :],
                                    start=(c == 0), stop=(c == DC - 1))
            mm.then_inc(pj.done, 1)
            for u in range(U_Q, U_OUT):
                if u >= 8:
                    eng.wait_ge(evac, u - 8 + 1)
                pj.unit(eng, u, unit_bank(u), norm.xnT)
            eng.wait_ge(evac, U_OUT)
            eng.wait_ge(em_done, 1)
            for n, src in enumerate((ai, em)):
                for g in range(G):
                    at = (n * G + g) * ML_H
                    mm = eng.transpose(bank[4][:, at:at + ML_H], src[:, g * P:(g + 1) * P],
                                       chip.ident[0:ML_H, 0:ML_H])
            mm.then_inc(cols_ps, 1)
            eng.wait_ge(cols_done, 2)
            eng.wait_ge(const_done, 3)

            def scores(h):
                base = (h % 2) * 4
                if h >= 2:
                    eng.wait_ge(sd_done, h - 1)
                    eng.wait_ge(pw_done, h - 1)
                eng.matmul(bank[base][:, 0:T], sel[:, h, :], M[:, :], start=True, stop=True).then_inc(row_ps, 1)
                eng.matmul(bank[base + 1][:, 0:T], kT[:, h, 0:P], qT[:, h, :], start=True, stop=True)
                eng.matmul(bank[base + 1][:, T:T + P], kT[:, h, P:T], qT[:, h, P:T], start=True, stop=True
                           ).then_inc(score_ps, 1)

            def sums(h):
                base = (h % 2) * 4
                if h >= 2:
                    eng.wait_ge(num_done, G * (h - 1))
                eng.wait_ge(sd_done, h + 1)
                s = sd[h % 2]
                eng.matmul(bank[base + 2][:, 0:ML_DV + 1], s[:, 0, :], vx[:, 0, h, :], start=True, stop=True
                           ).then_inc(num_ps, 1)
                eng.matmul(bank[base + 3][:, 0:ML_DV + 1], s[:, 1, :], vx[:, 0, h, :], start=True, stop=False)
                eng.matmul(bank[base + 3][:, 0:ML_DV + 1], s[:, 2, :], vx[:, 1, h, :], start=False, stop=True
                           ).then_inc(num_ps, 1)

            for h in range(ML_H + 1):
                if h < ML_H:
                    scores(h)
                if h >= 1:
                    sums(h - 1)
            eng.wait_ge(num_done, G * ML_H)
            eng.wait_ge(y_done, G * ML_H)
            turn_to_features(eng, chip, y, turned)
            eng.wait_ge(yT_done, DC)
            for n in range(2 * G):
                pj.unit(eng, U_OUT + n, bank[4 + n], yT)
            res.pe(eng)

        @block.scalar
        def _(eng):
            norm.act(eng)
            eng.wait_ge(bias_ready, 2)
            eng.wait_ge(pj.done, 1)
            eng.activation(ti[:, :], unit_bank(0)[0:ML_H, 0:T], ACT.Tanh, bias=bi[:, 0:1], scale=1.0 / CAP
                           ).then_inc(tanh_done, 1)
            eng.activation(tf[:, :], unit_bank(0)[0:ML_H, T:2 * T], ACT.Tanh, bias=bf[:, 0:1], scale=1.0 / CAP
                           ).then_inc(evac, 1)
            eng.wait_ge(evac, 1)
            eng.activation(soft[:, :], tf[:, :], ACT.Exp, scale=-CAP).then_inc(act_step, 1)
            eng.wait_ge(act_step, 1)
            eng.activation(soft[:, :], soft[:, :], ACT.Ln, bias=1.0).then_inc(logf_done, 1)
            for u in range(U_Q, U_OUT):
                eng.wait_ge(pj.done, u + 1)
                ps = unit_bank(u)
                if u < U_K:
                    i = 2 * (u - U_Q)
                    eng.activation(qT[:, i:i + 2, :], ps[:, :], ACT.Copy).then_inc(evac, 1)
                elif u < U_V:
                    i = 2 * (u - U_K)
                    eng.activation(kT[:, i:i + 2, :], ps[:, :], ACT.Copy).then_inc(evac, 1)
                elif u < U_O:
                    b, g = divmod(u - U_V, G)
                    eng.activation(vx[:, g, 2 * b:2 * b + 2, 0:ML_DV],
                                   ps[:, :].rearrange("p (h d) -> p h d", h=2), ACT.Copy).then_inc(evac, 1)
                else:
                    b, g = divmod(u - U_O, G)
                    eng.activation(so[:, g, b * WCOLS:(b + 1) * WCOLS], ps[:, :], ACT.Sigmoid).then_inc(evac, 1)
            eng.wait_ge(em_arg, 1)
            eng.activation(em[:, :], em[:, :], ACT.Exp, scale=-1.0).then_inc(em_done, 1)
            eng.wait_ge(cols_done, 2)

            def weights(h):
                k = h % 2
                if h >= 2:
                    eng.wait_ge(sd_done, h - 1)
                eng.wait_ge(arg_done, h + 1)
                eng.activation(pw[k][:, 0, :], arg[k][:, 0, :], ACT.Exp, bias=acol[:, 0, h:h + 1])
                eng.activation(pw[k][:, 1, :], bank[(h % 2) * 4][:, P:T], ACT.Exp, bias=acol[:, 0, h:h + 1],
                               scale=-1.0)
                eng.activation(pw[k][:, 2, :], arg[k][:, 1, :], ACT.Exp, bias=acol[:, 1, h:h + 1]
                               ).then_inc(pw_done, 1)

            def take(h):
                for g in range(G):
                    ps = bank[(h % 2) * 4 + 2 + g]
                    eng.wait_ge(num_ps, G * h + g + 1)
                    if h + g:
                        eng.wait_ge(num_done, G * h + g)
                    eng.activation(junk[:, :], ps[:, 0:ML_DV], ACT.Square, accum_out=ssq[:, g, h:h + 1])
                    eng.activation(num[:, g, h, :], ps[:, 0:ML_DV + 1], ACT.Copy).then_inc(num_done, 1)

            for h in range(ML_H + 1):
                if h < ML_H:
                    weights(h)
                if h >= 1:
                    take(h - 1)
            for c in range(DC):
                eng.wait_ge(turned, c // 2 + 1)
                at = (c % 2) * T
                eng.activation(yT[:, c, :], bank[c // 2][:, at:at + T], ACT.Copy,
                               scale=chip.gains[:, H_NORM + c:H_NORM + c + 1]).then_inc(yT_done, 1)
            res.act(eng)

        @block.vector
        def _(eng):
            n = Count()
            eng.wait_ge(b_in, 32)
            eng.tensor_scalar(bi[:, :], bi[:, :], 1.0 / CAP, None, ALU.mult).then_inc(bias_ready, 1)
            eng.tensor_scalar(bf[:, :], bf[:, :], 1.0 / CAP, None, ALU.mult).then_inc(bias_ready, 1)
            norm.dve(eng)
            eng.wait_ge(logf_done, 1)
            eng.tensor_tensor_scan(B[:, :], chip_ones(chip, ML_H), soft[:, :], 0.0, ALU.mult, ALU.subtract
                                   ).then_inc(dve_step, 1)
            eng.wait_ge(dve_step, n.up())
            eng.wait_ge(tanh_done, 1)
            eng.scalar_tensor_tensor(out=ai[:, :], in0=ti[:, :], scalar=CAP, in1=B[:, :], op0=ALU.mult,
                                     op1=ALU.subtract).then_inc(dve_step, 1)
            eng.wait_ge(dve_step, n.up())
            eng.tensor_tensor_scan(M[:, :], chip_ones(chip, ML_H), ai[:, :], 0.0, ALU.mult, ALU.max
                                   ).then_inc(dve_step, 1)
            eng.wait_ge(dve_step, n.up())
            eng.tensor_tensor(em[:, :], B[:, :], M[:, :], ALU.add).then_inc(em_arg, 1)
            res.dve_diag(eng)
            eng.wait_ge(cols_ps, 1)
            eng.tensor_copy(acol[:, :, :], bank[4][:, 0:G * ML_H]).then_inc(cols_done, 1)
            eng.tensor_copy(ecol[:, :, :], bank[4][:, G * ML_H:2 * G * ML_H]).then_inc(cols_done, 1)

            def args(h):
                k = h % 2
                if h >= 2:
                    eng.wait_ge(pw_done, h - 1)
                eng.wait_ge(row_ps, h + 1)
                eng.tensor_tensor(arg[k][:, :, :], tri[:, :].unsqueeze(1).to_broadcast([P, G, P]),
                                  bank[k * 4][:, 0:T].rearrange("p (g t) -> p g t", g=G), ALU.subtract
                                  ).then_inc(arg_done, 1)

            def weigh(h):
                k = h % 2
                if h >= 2:
                    eng.wait_ge(num_ps, G * (h - 1))
                eng.wait_ge(score_ps, h + 1)
                eng.wait_ge(pw_done, h + 1)
                eng.scalar_tensor_tensor(out=sd[k][:, :, :], in0=bank[k * 4 + 1][:, 0:3 * P].rearrange("p (a t) -> p a t", a=3),
                                         scalar=ML_DK ** -0.5, in1=pw[k][:, :, :], op0=ALU.mult, op1=ALU.mult
                                         ).then_inc(sd_done, 1)

            for h in range(ML_H + 1):
                if h < ML_H:
                    args(h)
                if h >= 1:
                    weigh(h - 1)
            eng.wait_ge(num_done, G * ML_H)
            d = num[:, :, :, ML_DV:ML_DV + 1].rearrange("p g h o -> p g (h o)")
            eng.scalar_tensor_tensor(out=den[:, :, :], in0=d, scalar=-1.0, in1=d, op0=ALU.mult,
                                     op1=ALU.max).then_inc(dve_step, 1)
            eng.wait_ge(dve_step, n.up())
            eng.tensor_tensor(den[:, :, :], den[:, :, :], ecol[:, :, :], ALU.max).then_inc(dve_step, 1)
            eng.wait_ge(dve_step, n.up())
            eng.reciprocal(den[:, :, :], den[:, :, :]).then_inc(dve_step, 1)
            eng.wait_ge(dve_step, n.up())
            eng.tensor_tensor(rr[:, :, :], ssq[:, :, :], den[:, :, :], ALU.mult).then_inc(dve_step, 1)
            eng.wait_ge(dve_step, n.up())
            eng.tensor_tensor(rr[:, :, :], rr[:, :, :], den[:, :, :], ALU.mult).then_inc(dve_step, 1)
            eng.wait_ge(dve_step, n.up())
            eng.tensor_scalar(rr[:, :, :], rr[:, :, :], 1.0 / ML_DV, EPS, ALU.mult, ALU.add).then_inc(mean_done, 1)
            eng.wait_ge(root_done, 1)
            eng.tensor_tensor(rr[:, :, :], rr[:, :, :], den[:, :, :], ALU.mult).then_inc(dve_step, 1)
            eng.wait_ge(dve_step, n.up())
            for g in range(G):
                for h in range(ML_H):
                    cols = slice(h * ML_DV, (h + 1) * ML_DV)
                    eng.scalar_tensor_tensor(out=y[:, g, cols], in0=num[:, g, h, 0:ML_DV], scalar=rr[:, g, h:h + 1],
                                             in1=so[:, g, cols], op0=ALU.mult, op1=ALU.mult).then_inc(y_done, 1)

            def wait_for_y(g, half):
                eng.wait_ge(pj.done, U_OUT + half * G + g + 1)

            res.dve_add(eng, [[bank[4 + half * G + g] for half in range(2)] for g in range(G)], wait_for_y)


def chip_ones(chip, rows):
    return chip.ones[0:rows, 0:1].to_broadcast([rows, T])



def fox(nc, chip, a):
    with ExitStack() as ctx:
        ph = Phase(nc, ctx, "fx")
        bank = chip.bank
        norm_kv = Norm(ph, chip, KV_SH, KV_SC, KV_NORM, "kv")
        norm_q = Norm(ph, chip, mod_col(1, SH1), mod_col(1, SC1), MIX_NORM + DC, "q")
        wk, wq = a["kv_w"], a["b_w_qo"][0]
        blocks = [(wk, 2 * D, FX_H, None), (wk, 0, WCOLS, True), (wk, WCOLS, WCOLS, True),
                  (wk, D, WCOLS, False), (wk, D + WCOLS, WCOLS, False),
                  (wq, 0, WCOLS, True), (wq, WCOLS, WCOLS, True),
                  (wq, D, WCOLS, False), (wq, D + WCOLS, WCOLS, False)]
        blocks += [(a["b_w_out"][0], n * WCOLS, WCOLS, False) for n in range(2)]
        pj = Project(ph, blocks)
        pj.units = [(b, n) for b, n in pj.units if not (b == 0 and n == 1)]
        pj.last = [n - 1 for n in pj.last]
        U_K, U_V, U_Q, U_O, U_OUT = 1, 5, 9, 13, 17
        kT = ph.sb("kT", [P, FX_H, T])
        qT = ph.sb("qT", [P, FX_H, T])
        v = ph.sb("v", [P, G, D])
        so = ph.sb("so", [P, G, D])
        y = norm_kv.xs
        yT = norm_kv.xnT
        bf = ph.sb("bf", [FX_H, 1])
        az, lf, mn = (ph.sb(n, [FX_H, T]) for n in ("az", "lf", "mn"))
        F3 = ph.sb("F3", [FX_H, 3, P])
        F = ph.sb("F", [FX_H, T])
        Fcol = ph.sb("Fcol", [P, G, FX_H])
        sel = ph.sb("sel", [FX_H, FX_H, P])
        mask = ph.sb("mask", [P, 3, P])
        sq = [ph.sb(f"sq{k}", [P, 4, P]) for k in range(2)]
        rcol = [ph.sb(f"rcol{k}", [P, 4]) for k in range(2)]
        rdiag = [ph.sb(f"rdiag{k}", [P, 4, P]) for k in range(2)]
        rb = [ph.sb(f"rb{k}", [P, 512]) for k in range(2)]
        bias = [ph.sb(f"bias{k}", [P, 3, P]) for k in range(2)]
        lg = [ph.sb(f"lg{k}", [P, 3 * P]) for k in range(2)]
        pr = [ph.sb(f"pr{k}", [P, 3 * P]) for k in range(2)]
        pT = [ph.sb(f"pT{k}", [P, 3 * P]) for k in range(2)]
        nmax = ph.sb("nmax", [P, FX_H, G])
        rsum = ph.sb("rsum", [P, FX_H, G])
        res = Residual(ph, chip, mod_col(1, G1), [bank[2], bank[3]])

        b_in, const_done, pool_step, dve_step, act_step = (
            ph.sem(n) for n in ("b_in", "const_done", "pool_step", "dve_step", "act_step"))
        evac, sq_done, ss_ps, logf_done, gate_read = (
            ph.sem(n) for n in ("evacuated", "sq_done", "ss_ps", "logf_done", "gate_read"))
        mean_done, root_done = ph.sem("mean_done"), ph.sem("root_done")
        rdiag_done, spread, rb_done = ph.sem("rdiag_done"), ph.sem("rms_spread"), ph.sem("rb_done")
        F_done, cols_ps, cols_done = ph.sem("F_done"), ph.sem("cols_ps"), ph.sem("cols_done")
        dve_evac = ph.sem("dve_evac")
        row_ps, bias_done, score_ps, lg_done, max_done, pr_done, pT_ps, pT_done, att_ps, y_done = (
            ph.sem(n) for n in ("row_ps", "bias_done", "score_ps", "lg_done", "max_done", "pr_done",
                                "pT_ps", "pT_done", "att_ps", "y_done"))
        turned, yT_done = ph.sem("turned"), ph.sem("yT_done")
        block = ctx.enter_context(nc.Block())

        head_units = list(range(U_K, U_V)) + list(range(U_Q, U_O))
        plain_units = [0] + list(range(U_V, U_Q)) + list(range(U_O, U_OUT))

        def unit_bank(u):
            if u in head_units:
                return bank[4 + head_units.index(u) % 3]
            return bank[plain_units.index(u) % 3]

        def wait_left(eng, u):
            if u in head_units:
                i = head_units.index(u)
                if i >= 3:
                    eng.wait_ge(dve_evac, i - 2)
            else:
                i = plain_units.index(u)
                if i >= 3:
                    eng.wait_ge(evac, i - 2)

        @block.sync
        def _(eng):
            eng.dma_start(bf[:, :], a["kv_b_f"].rearrange("(h o) -> h o", o=1)).then_inc(b_in, 16)
            pj.load(eng)

        @block.gpsimd
        def _(eng):
            eng.memset(sel[:, :, :], 0.0).then_inc(pool_step, 1)
            eng.memset(mask[:, :, :], 0.0).then_inc(pool_step, 1)
            eng.wait_ge(pool_step, 2)
            eng.affine_select(out=sel[:, :, :], in_=sel[:, :, :], compare_op=ALU.not_equal, fill=1.0, base=0,
                              pattern=[[-1, FX_H], [0, P]], channel_multiplier=1).then_inc(const_done, 1)
            for n in (0, 2):
                eng.affine_select(out=mask[:, n, :], in_=mask[:, n, :], compare_op=ALU.is_ge, fill=-NEG, base=0,
                                  pattern=[[-1, P]], channel_multiplier=1).then_inc(const_done, 1)

            def root(i):
                eng.wait_ge(mean_done, i + 1)
                rsqrt(eng, chip, rcol[i % 2][:, :], [P, 4]).then_inc(root_done, 1)

            norm_kv.pool(eng)
            for i in range(len(head_units) // 2):
                root(i)
            norm_q.pool(eng)
            for i in range(len(head_units) // 2, len(head_units)):
                root(i)

        @block.tensor
        def _(eng):
            norm_kv.pe(eng)
            eng.wait_ge(norm_kv.done, DC)
            eng.wait_ge(pj.loaded[0], 16)
            for c in range(DC):
                mm = eng.matmul(unit_bank(0)[0:FX_H, 0:T], pj.slots[0][:, c, 0:FX_H], norm_kv.xnT[:, c, :],
                                start=(c == 0), stop=(c == DC - 1))
            mm.then_inc(pj.done, 1)

            def squares(u):
                i = head_units.index(u)
                eng.wait_ge(sq_done, i + 1)
                if i >= 1:
                    eng.wait_ge(mean_done, i)
                for n in range(4):
                    mm = eng.matmul(bank[3][:, n:n + 1], sq[i % 2][:, n, :], chip.ones[:, 0:1], start=True, stop=True)
                mm.then_inc(ss_ps, 1)

            def spread_rms(u):
                i = head_units.index(u)
                eng.wait_ge(rdiag_done, 4 * (i + 1))
                if i >= 1:
                    eng.wait_ge(rb_done, i)
                eng.matmul(bank[7][:, :], chip.ones[:, :], rdiag[i % 2][:, :, :], start=True, stop=True
                           ).then_inc(spread, 1)

            def rms_behind(u):
                if u - 1 in head_units:
                    squares(u - 1)
                if u - 2 in head_units:
                    spread_rms(u - 2)

            for u in range(U_K, U_Q):
                wait_left(eng, u)
                pj.unit(eng, u, unit_bank(u), norm_kv.xnT)
                rms_behind(u)
            eng.wait_ge(evac, 1 + U_Q - U_V)
            norm_q.pe(eng)
            eng.wait_ge(norm_q.done, DC)
            for u in range(U_Q, U_OUT):
                wait_left(eng, u)
                pj.unit(eng, u, unit_bank(u), norm_q.xnT)
                rms_behind(u)
            eng.wait_ge(F_done, 1)
            eng.wait_ge(evac, len(plain_units))
            eng.wait_ge(dve_evac, len(head_units))
            for g in range(G):
                mm = eng.transpose(bank[0][:, g * FX_H:(g + 1) * FX_H], F[:, g * P:(g + 1) * P],
                                   chip.ident[0:FX_H, 0:FX_H])
            mm.then_inc(cols_ps, 1)
            eng.wait_ge(cols_done, 1)
            eng.wait_ge(const_done, 3)

            def scores(h):
                base = (h % 2) * 4
                if h >= 2:
                    eng.wait_ge(lg_done, h - 1)
                eng.matmul(bank[base][:, 0:3 * P], sel[:, h, :], F3[:, :, :], start=True, stop=True
                           ).then_inc(row_ps, 1)
                eng.matmul(bank[base + 1][:, 0:P], qT[:, h, 0:P], kT[:, h, 0:P], start=True, stop=True)
                eng.matmul(bank[base + 1][:, P:3 * P], qT[:, h, P:T], kT[:, h, :], start=True, stop=True
                           ).then_inc(score_ps, 1)

            def turn(h):
                base = (h % 2) * 4
                eng.wait_ge(pr_done, G * (h + 1))
                if h >= 2:
                    eng.wait_ge(pT_done, h - 1)
                for n in range(3):
                    mm = eng.transpose(bank[base + 2][:, n * P:(n + 1) * P], pr[h % 2][:, n * P:(n + 1) * P],
                                       chip.ident[:, :])
                mm.then_inc(pT_ps, 1)

            def attend(h):
                base = (h % 2) * 4
                cols = slice(h * FX_D, (h + 1) * FX_D)
                eng.wait_ge(pT_done, h + 1)
                if h >= 2:
                    eng.wait_ge(y_done, G * (h - 1))
                p = pT[h % 2]
                eng.matmul(bank[base + 3][:, 0:FX_D], p[:, 0:P], v[:, 0, cols], start=True, stop=True)
                eng.matmul(bank[base + 3][:, FX_D:2 * FX_D], p[:, P:2 * P], v[:, 0, cols], start=True, stop=False)
                eng.matmul(bank[base + 3][:, FX_D:2 * FX_D], p[:, 2 * P:3 * P], v[:, 1, cols], start=False,
                           stop=True).then_inc(att_ps, 1)

            for h in range(FX_H + 2):
                if h < FX_H:
                    scores(h)
                if 1 <= h <= FX_H:
                    turn(h - 1)
                if h >= 2:
                    attend(h - 2)
            eng.wait_ge(y_done, G * FX_H)
            turn_to_features(eng, chip, y, turned)
            eng.wait_ge(yT_done, DC)
            for n in range(2 * G):
                pj.unit(eng, U_OUT + n, bank[4 + n], yT)
            res.pe(eng)

        @block.scalar
        def _(eng):
            norm_kv.act(eng)
            norm_q.act(eng)
            eng.wait_ge(b_in, 16)
            eng.wait_ge(pj.done, 1)
            eng.activation(az[:, :], unit_bank(0)[0:FX_H, 0:T], ACT.Abs, bias=bf[:, 0:1]).then_inc(act_step, 1)
            eng.wait_ge(act_step, 1)
            eng.activation(az[:, :], az[:, :], ACT.Exp, scale=-1.0).then_inc(act_step, 1)
            eng.wait_ge(act_step, 2)
            eng.activation(az[:, :], az[:, :], ACT.Ln, bias=1.0).then_inc(logf_done, 1)
            eng.wait_ge(gate_read, 1)
            eng.sem_inc(evac, 1)
            for u in range(U_K, U_OUT):
                eng.wait_ge(pj.done, u + 1)
                ps = unit_bank(u)
                if u in head_units:
                    i = head_units.index(u)
                    if i >= 2:
                        eng.wait_ge(ss_ps, i - 1)
                    eng.activation(sq[i % 2][:, :, :], ps[:, :], ACT.Square).then_inc(sq_done, 1)
                elif u < U_Q:
                    b, g = divmod(u - U_V, G)
                    eng.activation(v[:, g, b * WCOLS:(b + 1) * WCOLS], ps[:, :], ACT.Copy).then_inc(evac, 1)
                else:
                    b, g = divmod(u - U_O, G)
                    eng.activation(so[:, g, b * WCOLS:(b + 1) * WCOLS], ps[:, :], ACT.Sigmoid).then_inc(evac, 1)
                if u - 2 in head_units:
                    i = head_units.index(u - 2)
                    eng.wait_ge(spread, i + 1)
                    if i >= 2:
                        eng.wait_ge(dve_evac, i - 1)
                    eng.activation(rb[i % 2][:, :], bank[7][:, :], ACT.Copy).then_inc(rb_done, 1)

            def soft(h):
                k = h % 2
                eng.wait_ge(max_done, G * (h + 1))
                if h >= 2:
                    eng.wait_ge(pT_ps, h - 1)
                eng.activation(pr[k][:, 0:P], lg[k][:, 0:P], ACT.Exp, bias=nmax[:, h, 0:1],
                               accum_out=rsum[:, h, 0:1]).then_inc(pr_done, 1)
                eng.activation(pr[k][:, P:3 * P], lg[k][:, P:3 * P], ACT.Exp, bias=nmax[:, h, 1:2],
                               accum_out=rsum[:, h, 1:2]).then_inc(pr_done, 1)

            def take(h):
                k = h % 2
                eng.wait_ge(pT_ps, h + 1)
                if h >= 2:
                    eng.wait_ge(att_ps, h - 1)
                eng.activation(pT[k][:, :], bank[k * 4 + 2][:, 0:3 * P], ACT.Copy).then_inc(pT_done, 1)

            for h in range(FX_H + 1):
                if h < FX_H:
                    soft(h)
                if h >= 1:
                    take(h - 1)
            for c in range(DC):
                eng.wait_ge(turned, c // 2 + 1)
                at = (c % 2) * T
                eng.activation(yT[:, c, :], bank[c // 2][:, at:at + T], ACT.Copy).then_inc(yT_done, 1)
            res.act(eng)

        @block.vector
        def _(eng):
            n = Count()
            norm_kv.dve(eng)
            eng.wait_ge(act_step, 1)
            eng.tensor_scalar(mn[:, :], unit_bank(0)[0:FX_H, 0:T], bf[:, 0:1], 0.0, ALU.add, ALU.min
                              ).then_inc(gate_read, 1)
            eng.wait_ge(gate_read, 1)
            eng.wait_ge(logf_done, 1)
            eng.tensor_tensor(lf[:, :], mn[:, :], az[:, :], ALU.subtract).then_inc(dve_step, 1)
            eng.wait_ge(dve_step, n.up())
            eng.tensor_tensor_scan(F[:, :], chip_ones(chip, FX_H), lf[:, :], 0.0, ALU.mult, ALU.add
                                   ).then_inc(dve_step, 1)
            eng.wait_ge(dve_step, n.up())
            eng.tensor_copy(F3[:, 0, :], F[:, 0:P])
            eng.tensor_copy(F3[:, 1:3, :], F[:, :].rearrange("h (g t) -> h g t", g=G)).then_inc(F_done, 1)
            res.dve_diag(eng)

            def rms_diag(i):
                k = i % 2
                eng.wait_ge(ss_ps, i + 1)
                eng.tensor_scalar(rcol[k][:, :], bank[3][:, 0:4], 1.0 / FX_D, EPS, ALU.mult, ALU.add
                                  ).then_inc(mean_done, 1)
                eng.wait_ge(root_done, i + 1)
                if i >= 2:
                    eng.wait_ge(spread, i - 1)
                for m in range(4):
                    eng.tensor_scalar(rdiag[k][:, m, :], chip.ident[:, :], rcol[k][:, m:m + 1], None, ALU.mult
                                      ).then_inc(rdiag_done, 1)

            def normalise(i):
                u = head_units[i]
                gain, dst, at = (K_NORM, kT, 2 * (u - U_K)) if u < U_V else (Q_NORM, qT, 2 * (u - U_Q))
                eng.wait_ge(rb_done, i + 1)
                eng.scalar_tensor_tensor(out=dst[:, at:at + 2, :],
                                         in0=unit_bank(u)[:, :].rearrange("p (h t) -> p h t", h=2),
                                         scalar=chip.gains[:, gain:gain + 1],
                                         in1=rb[i % 2][:, :].rearrange("p (h t) -> p h t", h=2),
                                         op0=ALU.mult, op1=ALU.mult).then_inc(dve_evac, 1)

            half_units = len(head_units) // 2
            for first in (0, half_units):
                if first:
                    norm_q.dve(eng)
                for i in range(first, first + half_units):
                    rms_diag(i)
                    if i > first:
                        normalise(i - 1)
                normalise(first + half_units - 1)
            eng.wait_ge(cols_ps, 1)
            eng.tensor_copy(Fcol[:, :, :], bank[0][:, 0:G * FX_H]).then_inc(cols_done, 1)
            eng.wait_ge(cols_done, 1)

            def logits(h):
                k = h % 2
                ps, sc = bank[k * 4], bank[k * 4 + 1]
                eng.wait_ge(row_ps, h + 1)
                eng.scalar_tensor_tensor(out=bias[k][:, 0, :], in0=ps[:, 0:P], scalar=Fcol[:, 0, h:h + 1],
                                         in1=mask[:, 0, :], op0=ALU.subtract, op1=ALU.add).then_inc(bias_done, 1)
                eng.scalar_tensor_tensor(out=bias[k][:, 1:3, :], in0=ps[:, P:3 * P].rearrange("p (a s) -> p a s", a=2),
                                         scalar=Fcol[:, 1, h:h + 1], in1=mask[:, 1:3, :],
                                         op0=ALU.subtract, op1=ALU.add).then_inc(bias_done, 1)
                eng.wait_ge(bias_done, 2 * (h + 1))
                eng.wait_ge(score_ps, h + 1)
                if h >= 2:
                    eng.wait_ge(pr_done, G * (h - 1))
                eng.scalar_tensor_tensor(out=lg[k][:, :], in0=sc[:, 0:3 * P], scalar=FX_D ** -0.5,
                                         in1=bias[k][:, :, :].rearrange("p a s -> p (a s)"),
                                         op0=ALU.mult, op1=ALU.subtract).then_inc(lg_done, 1)
                eng.wait_ge(lg_done, h + 1)
                eng.tensor_reduce(nmax[:, h, 0:1], lg[k][:, 0:P], AX.X, ALU.max, negate=True).then_inc(max_done, 1)
                eng.tensor_reduce(nmax[:, h, 1:2], lg[k][:, P:3 * P], AX.X, ALU.max, negate=True
                                  ).then_inc(max_done, 1)

            def gate(h):
                k = h % 2
                cols = slice(h * FX_D, (h + 1) * FX_D)
                eng.wait_ge(att_ps, h + 1)
                eng.reciprocal(rsum[:, h, :], rsum[:, h, :]).then_inc(dve_step, 1)
                eng.wait_ge(dve_step, n.up())
                for g in range(G):
                    eng.scalar_tensor_tensor(out=y[:, g, cols], in0=bank[k * 4 + 3][:, g * FX_D:(g + 1) * FX_D],
                                             scalar=rsum[:, h, g:g + 1], in1=so[:, g, cols],
                                             op0=ALU.mult, op1=ALU.mult).then_inc(y_done, 1)

            for h in range(FX_H + 2):
                if h < FX_H:
                    logits(h)
                if h >= 2:
                    gate(h - 2)

            def wait_for_y(g, half):
                eng.wait_ge(pj.done, U_OUT + half * G + g + 1)

            res.dve_add(eng, [[bank[4 + half * G + g] for half in range(2)] for g in range(G)], wait_for_y)



class PeerState:

    def __init__(self, ph):
        self.xhl = ph.sb("xhl", [P, DC, 2, T], F32R)
        self.iT = ph.sb("iT", [SEL, T])
        self.jT = ph.sb("jT", [SEL, T])
        self.gT = ph.sb("gT", [SEL, T])


def peer_route(nc, chip, a, layer, st):
    with ExitStack() as ctx:
        ph = Phase(nc, ctx, f"rt{layer}")
        bank = chip.bank
        norm = Norm(ph, chip, mod_col(layer, SH2), mod_col(layer, SC2), FFN_NORM + layer * DC)
        pj = Project(ph, [(a["peer_wq"][layer], n * WCOLS, WCOLS, True) for n in range(4)])
        sk = ph.sb("sk", [PR_KEYS, 2, P])
        skT = ph.sb("skT", [P, 2, PR_KEYS])
        qT = [ph.sb(f"qT{k}", [P, 4, T]) for k in range(2)]
        sc = ph.sb("sc", [P, G, PR_ROWS, PR_KEYS])
        left = ph.sb("left", [P, 2, T])
        top = ph.sb("top", [P, G, PR_ROWS, PR_K])
        topi = ph.sb("topi", [P, G, PR_ROWS, PR_K], U32)
        topf = ph.sb("topf", [P, G, PR_ROWS, PR_K])
        cand = ph.sb("cand", [P, PR_H, PR_K, PR_K])
        eq = ph.sb("eq", [P, PR_H, PR_K, PR_K])
        best = ph.sb("best", [P, G, PR_H, PR_K])
        pos = ph.sb("pos", [P, G, PR_H, PR_K], U32)
        posk = ph.sb("posk", [P, 2, PR_H, PR_K], U32)
        posf = ph.sb("posf", [P, 2, PR_H, PR_K])
        key = ph.sb("key", [P, G, 2, SEL])
        gate = ph.sb("gate", [P, G, SEL])
        gsum = ph.sb("gsum", [P, G, PR_H])

        sk_in, sk_ps, sk_done = ph.sem("sk_in"), ph.sem("sk_ps"), ph.sem("sk_done")
        hi_done, dve_step = ph.sem("hi_done"), ph.sem("dve_step")
        q_done, sc_ps, sc_done = ph.sem("q_done"), ph.sem("sc_ps"), ph.sem("sc_done")
        diff_done, exp_done, sel_done, turned, taken = (
            ph.sem(n) for n in ("diff_done", "exp_done", "sel_done", "turned", "taken"))
        block = ctx.enter_context(nc.Block())

        @block.sync
        def _(eng):
            eng.dma_start(sk[:, :, :], a["peer_subkeys"][layer].rearrange("h k d -> k h d")).then_inc(sk_in, 16)
            pj.load(eng)

        @block.gpsimd
        def _(eng):
            norm.pool(eng)

        @block.tensor
        def _(eng):
            eng.wait_ge(sk_in, 16)
            for n in range(2):
                mm = eng.transpose(bank[4][:, n * P:(n + 1) * P], sk[:, n, :], chip.ident[:, :])
            mm.then_inc(sk_ps, 1)
            norm.pe(eng)
            eng.wait_ge(norm.done, DC)
            eng.wait_ge(sk_done, 1)

            def queries(b):
                if b >= 2:
                    eng.wait_ge(q_done, 2 * (b - 1))
                for n in range(2):
                    pj.unit(eng, 2 * b + n, bank[4 + (2 * b + n) % 4], norm.xnT)

            def scores(b):
                eng.wait_ge(q_done, 2 * (b + 1))
                for g in range(G):
                    if b >= 2:
                        eng.wait_ge(sc_done, G * (b - 2) + g + 1)
                    for j in range(4):
                        mm = eng.matmul(bank[(G * b + g) % 4][:, j * P:(j + 1) * P], qT[b % 2][:, j, g * P:(g + 1) * P],
                                        skT[:, j % 2, :], start=True, stop=True)
                    mm.then_inc(sc_ps, 1)

            for b in range(5):
                if b < 4:
                    queries(b)
                if b >= 1:
                    scores(b - 1)
            eng.wait_ge(sc_done, 4 * G)
            for g in range(G):
                eng.wait_ge(sel_done, g + 1)
                for n in range(3):
                    src = gate[:, g, :] if n == 2 else key[:, g, n, :]
                    mm = eng.transpose(bank[g][:, n * P:(n + 1) * P], src, chip.ident[:, :])
                mm.then_inc(turned, 1)

        @block.scalar
        def _(eng):
            norm.act(eng)
            eng.wait_ge(sk_ps, 1)
            eng.activation(skT[:, :, :], bank[4][:, 0:2 * P], ACT.Copy).then_inc(sk_done, 1)
            eng.wait_ge(norm.done, DC)
            eng.activation(st.xhl[:, :, 0, :], norm.xnT[:, :, :], ACT.Copy).then_inc(hi_done, 1)

            def take_q(b):
                for n in range(2):
                    eng.wait_ge(pj.done, 2 * b + n + 1)
                    if b >= 2:
                        eng.wait_ge(sc_ps, G * (b - 1))
                    eng.activation(qT[b % 2][:, 2 * n:2 * n + 2, :], bank[4 + (2 * b + n) % 4][:, :], ACT.Copy
                                   ).then_inc(q_done, 1)

            def take_s(b):
                for g in range(G):
                    eng.wait_ge(sc_ps, G * b + g + 1)
                    eng.activation(sc[:, g, 4 * b:4 * b + 4, :], bank[(G * b + g) % 4][:, :], ACT.Copy
                                   ).then_inc(sc_done, 1)

            for b in range(5):
                if b < 4:
                    take_q(b)
                if b >= 1:
                    take_s(b - 1)
            for g in range(G):
                eng.wait_ge(diff_done, g + 1)
                eng.activation(gate[:, g, :], gate[:, g, :], ACT.Exp).then_inc(exp_done, 1)
            for g in range(G):
                eng.wait_ge(turned, g + 1)
                for n, dst in enumerate((st.iT, st.jT, st.gT)):
                    eng.activation(dst[:, g * P:(g + 1) * P], bank[g][:, n * P:(n + 1) * P], ACT.Copy
                                   ).then_inc(taken, 1)
            eng.wait_ge(taken, 3 * G)

        @block.vector
        def _(eng):
            n = Count()
            norm.dve(eng)
            eng.wait_ge(hi_done, 1)
            eng.tensor_tensor(st.xhl[:, :, 1, :], norm.xnT[:, :, :], st.xhl[:, :, 0, :].bitcast(F32), ALU.subtract)

            def top16(values, out, index, spare):
                eng.max(out[..., 0:8], values).then_inc(dve_step, 1)
                eng.wait_ge(dve_step, n.up())
                eng.max_index(index[..., 0:8], out[..., 0:8], values)
                eng.match_replace(spare, out[..., 0:8], values, LOWEST).then_inc(dve_step, 1)
                eng.wait_ge(dve_step, n.up())
                eng.max(out[..., 8:16], spare).then_inc(dve_step, 1)
                eng.wait_ge(dve_step, n.up())
                eng.max_index(index[..., 8:16], out[..., 8:16], spare).then_inc(dve_step, 1)
                n.up()

            for b in range(4):
                for g in range(G):
                    eng.wait_ge(sc_done, G * b + g + 1)
                    for r in range(4 * b, 4 * b + 4):
                        top16(sc[:, g, r, :], top[:, g, r, :], topi[:, g, r, :], left[:, r % 2, 0:PR_KEYS])
            for g in range(G):
                eng.wait_ge(dve_step, n.n)
                eng.tensor_copy(topf[:, g, :, :], topi[:, g, :, :])
                pair = top[:, g, :, :].rearrange("p (h two) k -> p h two k", two=2)
                eng.tensor_tensor(cand[:, :, :, :],
                                  pair[:, :, 0, :].unsqueeze(3).to_broadcast([P, PR_H, PR_K, PR_K]),
                                  pair[:, :, 1, :].unsqueeze(2).to_broadcast([P, PR_H, PR_K, PR_K]), ALU.add
                                  ).then_inc(dve_step, 1)
                eng.wait_ge(dve_step, n.up())
                for h in range(PR_H):
                    top16(cand[:, h, :, :].rearrange("p a b -> p (a b)"), best[:, g, h, :], pos[:, g, h, :],
                          left[:, h % 2, :])
                eng.wait_ge(dve_step, n.n)
                eng.tensor_tensor(gate[:, g, :].rearrange("p (h k) -> p h k", h=PR_H), best[:, g, :, :],
                                  best[:, g, :, 0:1].to_broadcast([P, PR_H, PR_K]), ALU.subtract
                                  ).then_inc(diff_done, 1)
                eng.tensor_scalar(posk[:, 0, :, :], pos[:, g, :, :], 4, None, ALU.logical_shift_right
                                  ).then_inc(dve_step, 1)
                eng.wait_ge(dve_step, n.up())
                eng.tensor_scalar(posk[:, 1, :, :], pos[:, g, :, :], 15, None, ALU.bitwise_and).then_inc(dve_step, 1)
                eng.wait_ge(dve_step, n.up())
                eng.tensor_copy(posf[:, :, :, :], posk[:, :, :, :]).then_inc(dve_step, 1)
                eng.wait_ge(dve_step, n.up())
                for half in range(2):
                    wide = [P, PR_H, PR_K, PR_K]
                    eng.tensor_tensor(eq[:, :, :, :], posf[:, half, :, :].unsqueeze(3).to_broadcast(wide),
                                      chip.iota[:, 0:PR_K].unsqueeze(1).unsqueeze(1).to_broadcast(wide), ALU.is_equal
                                      ).then_inc(dve_step, 1)
                    eng.wait_ge(dve_step, n.up())
                    tf = topf[:, g, :, :].rearrange("p (h two) k -> p h two k", two=2)[:, :, half, :]
                    eng.tensor_tensor(eq[:, :, :, :], eq[:, :, :, :], tf.unsqueeze(2).to_broadcast(wide), ALU.mult
                                      ).then_inc(dve_step, 1)
                    eng.wait_ge(dve_step, n.up())
                    eng.tensor_reduce(key[:, g, half, :].rearrange("p (h k) -> p h k", h=PR_H), eq[:, :, :, :],
                                      AX.X, ALU.add).then_inc(dve_step, 1)
                    eng.wait_ge(dve_step, n.up())
                eng.wait_ge(exp_done, g + 1)
                gv = gate[:, g, :].rearrange("p (h k) -> p h k", h=PR_H)
                eng.tensor_reduce(gsum[:, g, :], gv, AX.X, ALU.add).then_inc(dve_step, 1)
                eng.wait_ge(dve_step, n.up())
                eng.reciprocal(gsum[:, g, :], gsum[:, g, :]).then_inc(dve_step, 1)
                eng.wait_ge(dve_step, n.up())
                eng.tensor_tensor(gv, gv, gsum[:, g, :].unsqueeze(2).to_broadcast([P, PR_H, PR_K]), ALU.mult
                                  ).then_inc(sel_done, 1)
                eng.wait_ge(sel_done, g + 1)



def peer_experts(nc, chip, a, layer, st):
    TILES = PR_EXPERTS // P
    SLOTS = 4
    TOK = 4
    with ExitStack() as ctx:
        ph = Phase(nc, ctx, f"ex{layer}")
        bank = chip.bank
        act = ph.sb("act", [P, TILES, T])
        stream = [ph.sb(f"stream{k}", [P, D]) for k in range(SLOTS)]
        hi = [ph.sb(f"hi{k}", [P, D], F32R) for k in range(2)]
        lo = [ph.sb(f"lo{k}", [P, D], F32R) for k in range(2)]
        whi = [ph.sb(f"whi{k}", [P, T], F32R) for k in range(2)]
        wlo = [ph.sb(f"wlo{k}", [P, T], F32R) for k in range(2)]
        oj = [ph.sb(f"oj{k}", [SEL, TOK, P]) for k in range(2)]
        oi = [ph.sb(f"oi{k}", [SEL, TOK, P]) for k in range(2)]
        res = Residual(ph, chip, mod_col(layer, G2), [bank[4], bank[5]], diag=stream[0], row=stream[1])

        loaded = [ph.sem(f"loaded{k}") for k in range(SLOTS)]
        slot_free = ph.sem("slot_free")
        turned = ph.sem("turned")
        hi_done, lo_done = ph.sem("hi_done"), ph.sem("lo_done")
        half_free = ph.sem("half_free")
        parts_free = ph.sem("parts_free")
        dot_ps, dot_free = ph.sem("dot_ps"), ph.sem("dot_free")
        dj_done, abs_done, oj_done, oi_done, hot_free, gate_ps, gate_free = (
            ph.sem(n) for n in ("dj_done", "abs_done", "oj_done", "oi_done", "hot_free", "gate_ps", "gate_free"))
        vhi, vlo, wparts, wl_done, v_free = (ph.sem(n) for n in ("vhi", "vlo", "wparts", "wl_done", "v_free"))
        y_ps = ph.sem("y_ps")
        block = ctx.enter_context(nc.Block())

        def tiles(eng, body, ahead=None, skip=0):
            if ahead:
                ahead(0, 0)
            first = skip
            for k in range(first):
                if ahead:
                    ahead(k + 1, (k + 1) % SLOTS)
                body(k, k % SLOTS)
            with eng.Fori(first // SLOTS, TILES // SLOTS - 1) as i:
                for k in range(SLOTS):
                    t = i * SLOTS + k
                    if ahead:
                        ahead(i * SLOTS + (k + 1), (k + 1) % SLOTS)
                    body(t, k)
            for k in range(SLOTS):
                t = TILES - SLOTS + k
                if ahead and k < SLOTS - 1:
                    ahead(t + 1, k + 1)
                body(t, k)

        @block.sync
        def _(eng):
            def load_u(t, k):
                eng.wait_ge(slot_free, t + 1)
                eng.dma_start(stream[k][:, :], a["peer_u"][layer][bass.ds(t * P, P), :]).then_inc(loaded[k], 16)

            def load_v(t, k):
                eng.wait_ge(slot_free, t + (TILES + 1))
                eng.dma_start(stream[k][:, :], a["peer_v"][layer][bass.ds(t * P, P), :]).then_inc(loaded[k], 16)

            tiles(eng, load_u)
            tiles(eng, load_v)

        @block.tensor
        def _(eng):
            eng.sem_inc(slot_free, SLOTS)

            def turn(t, k):
                p = k % 2
                eng.wait_ge(loaded[k], (t - k) * (16 // SLOTS) + 16)
                for half in range(2):
                    eng.wait_ge(half_free, t * 2 + (half + 1))
                    for c in range(4):
                        col = half * 512 + c * P
                        mm = eng.transpose(bank[2 * p + half][:, c * P:(c + 1) * P], stream[k][:, col:col + P],
                                           chip.ident[:, :])
                    mm.then_inc(turned, 1)

            def dots(t, k):
                p = k % 2
                eng.wait_ge(lo_done, t * 2 + 2)
                eng.wait_ge(dot_free, t + 1)
                out = bank[4 + p][:, 0:T]
                for c in range(DC):
                    col = slice(c * P, (c + 1) * P)
                    eng.matmul(out, hi[p][:, col], st.xhl[:, c, 0, :], start=(c == 0), stop=False)
                    eng.matmul(out, hi[p][:, col], st.xhl[:, c, 1, :], start=False, stop=False)
                    mm = eng.matmul(out, lo[p][:, col], st.xhl[:, c, 0, :], start=False, stop=(c == DC - 1))
                mm.then_inc(dot_ps, 1)

            tiles(eng, dots, ahead=turn)

            def gates(q, k):
                eng.wait_ge(oj_done, q + 1)
                eng.wait_ge(oi_done, q + 1)
                eng.wait_ge(gate_free, q + 1)
                for n in range(TOK):
                    mm = eng.matmul(bank[6 + k][:, n * P:(n + 1) * P], oj[k][:, n, :], oi[k][:, n, :],
                                    start=True, stop=True)
                mm.then_inc(gate_ps, 1)

            with eng.Fori(0, T // TOK // 2) as i:
                for k in range(2):
                    gates(i * 2 + k, k)

            def sums(t, k, first=False, last=False):
                p = k % 2
                eng.wait_ge(vlo, t + 1)
                eng.wait_ge(wl_done, t + 1)
                for g in range(G):
                    tok = slice(g * P, (g + 1) * P)
                    for n, (w, v) in enumerate(((whi, hi), (whi, lo), (wlo, hi))):
                        for half in range(2):
                            mm = eng.matmul(bank[2 * g + half][:, :], w[p][:, tok], v[p][:, half * 512:(half + 1) * 512],
                                            start=(first and n == 0), stop=(last and n == 2))
                mm.then_inc(v_free, 1)

            for k in range(SLOTS):
                sums(k, k, first=(k == 0))
            with eng.Fori(1, TILES // SLOTS - 1) as i:
                for k in range(SLOTS):
                    sums(i * SLOTS + k, k)
            for k in range(SLOTS):
                sums(TILES - SLOTS + k, k, last=(k == SLOTS - 1))
            res.pe(eng)

        @block.scalar
        def _(eng):
            nc.scalar.preload_act_table(ACT.Gelu)

            def split(t, k):
                p = k % 2
                for half in range(2):
                    eng.wait_ge(turned, t * 2 + (half + 1))
                    if half == 0:
                        eng.wait_ge(dot_ps, t + 1)
                    eng.activation(hi[p][:, half * 512:(half + 1) * 512], bank[2 * p + half][:, :], ACT.Copy
                                   ).then_inc(hi_done, 1)

            def gelu(t, k):
                eng.wait_ge(dot_ps, t + 3)
                eng.activation(act[:, bass.ds(t, 1), :], bank[4 + k % 2][:, 0:T], ACT.Gelu).then_inc(dot_free, 1)

            eng.sem_inc(dot_ps, 2)
            eng.sem_inc(dot_free, 2)
            tiles(eng, gelu, ahead=split)

            def parts(t, k):
                p = k % 2
                eng.wait_ge(loaded[k], (t - k) * (16 // SLOTS) + (16 + 16 * TILES // SLOTS))
                eng.wait_ge(v_free, t + 1)
                eng.activation(hi[p][:, :], stream[k][:, :], ACT.Copy).then_inc(vhi, 1)
                eng.activation(whi[p][:, :], act[:, bass.ds(t, 1), :], ACT.Copy).then_inc(wparts, 1)

            def hot(q, k):
                eng.wait_ge(dj_done, q + 1)
                eng.activation(oj[k][:, :, :], oj[k][:, :, :], ACT.Abs).then_inc(abs_done, 1)
                eng.wait_ge(abs_done, q + 1)
                eng.activation(oj[k][:, :, :], oj[k][:, :, :], ACT.Relu, bias=1.0, scale=-1.0).then_inc(oj_done, 1)

            with eng.Fori(0, T // TOK // 2) as i:
                for k in range(2):
                    hot(i * 2 + k, k)

            eng.sem_inc(v_free, 2)
            eng.wait_ge(gate_free, T // TOK + 2)
            tiles(eng, parts)
            res.act(eng)

        @block.gpsimd
        def _(eng):
            def hot(q, k):
                eng.wait_ge(hot_free, q + 1)
                eng.tensor_tensor(oj[k][:, :, :], chip.iota[:, :].unsqueeze(1).to_broadcast([SEL, TOK, P]),
                                  st.jT[:, bass.ds(q * TOK, TOK)].unsqueeze(2).to_broadcast([SEL, TOK, P]),
                                  ALU.subtract).then_inc(dj_done, 1)

            with eng.Fori(0, T // TOK // 2) as i:
                for k in range(2):
                    hot(i * 2 + k, k)

        @block.vector
        def _(eng):
            eng.sem_inc(half_free, 4)

            def low(t, k):
                p = k % 2
                for half in range(2):
                    cols = slice(half * 512, (half + 1) * 512)
                    eng.wait_ge(hi_done, t * 2 + (half + 1))
                    eng.tensor_tensor(lo[p][:, cols], bank[2 * p + half][:, :], hi[p][:, cols].bitcast(F32),
                                      ALU.subtract).then_inc(lo_done, 1)
                    eng.wait_ge(lo_done, t * 2 + (half + 1))
                    eng.sem_inc(half_free, 1)
                eng.sem_inc(slot_free, 1)

            with eng.Fori(0, TILES // SLOTS) as i:
                for k in range(SLOTS):
                    low(i * SLOTS + k, k)

            eng.sem_inc(hot_free, 2)
            eng.sem_inc(gate_free, 2)

            def hot(q, k):
                eng.wait_ge(gate_ps, q + 1)
                for n in range(TOK):
                    t = q * TOK + n
                    mm = eng.tensor_scalar(oi[k][:, n, :], chip.iota[:, :], st.iT[:, bass.ds(t, 1)],
                                           st.gT[:, bass.ds(t, 1)], ALU.is_equal, ALU.mult)
                mm.then_inc(oi_done, 1)

            def apply(q, k):
                eng.wait_ge(gate_ps, q + 3)
                eng.sem_inc(hot_free, 1)
                cell = act[:, :, bass.ds(q * TOK, TOK)]
                eng.tensor_tensor(cell, bank[6 + k][:, :].rearrange("p (t i) -> p i t", t=TOK), cell, ALU.mult
                                  ).then_inc(gate_free, 1)

            eng.sem_inc(gate_ps, 2)
            eng.wait_ge(dot_free, TILES + 2)
            hot(0, 0)
            with eng.Fori(0, T // TOK // 2 - 1) as i:
                for k in range(2):
                    hot(i * 2 + (k + 1), (k + 1) % 2)
                    apply(i * 2 + k, k)
            last = T // TOK
            hot(last - 1, 1)
            apply(last - 2, 0)
            apply(last - 1, 1)

            def low_parts(t, k):
                p = k % 2
                eng.wait_ge(vhi, t + 1)
                eng.tensor_tensor(lo[p][:, :], stream[k][:, :], hi[p][:, :].bitcast(F32), ALU.subtract
                                  ).then_inc(vlo, 1)
                eng.wait_ge(wparts, t + 1)
                eng.tensor_tensor(wlo[p][:, :], act[:, bass.ds(t, 1), :], whi[p][:, :].bitcast(F32), ALU.subtract
                                  ).then_inc(wl_done, 1)
                eng.wait_ge(vlo, t + 1)
                eng.sem_inc(slot_free, 1)

            eng.wait_ge(gate_free, last + 2)
            with eng.Fori(0, TILES // SLOTS) as i:
                for k in range(SLOTS):
                    low_parts(i * SLOTS + k, k)

            res.dve_diag(eng)

            def wait_for_y(g, half):
                eng.wait_ge(v_free, TILES + 2)

            res.dve_add(eng, [[bank[2 * g + half] for half in range(2)] for g in range(G)], wait_for_y)


def store(nc, chip, out):
    with ExitStack() as ctx:
        stored = ctx.enter_context(nc.semaphore("stored"))
        block = ctx.enter_context(nc.Block())

        @block.sync
        def _(eng):
            for g in range(G):
                eng.dma_start(out[g * P:(g + 1) * P, :], chip.x[:, g, :]).then_inc(stored, 16)
            eng.wait_ge(stored, 16 * G)


def program(nc, a, out):
    with ExitStack() as ctx:
        chip = Chip(nc, ctx)
        adaln_vectors(nc, chip, a)
        mixers = (mlstm, fox)
        for layer, mixer in enumerate(mixers):
            mixer(nc, chip, a)
            with ExitStack() as inner:
                st = PeerState(Phase(nc, inner, f"peer{layer}"))
                peer_route(nc, chip, a, layer, st)
                peer_experts(nc, chip, a, layer, st)
        store(nc, chip, out)


_INS = ["x", "c", "ada_w", "ada_b", "mix_norm", "ffn_norm", "a_w_in", "a_b_i", "a_b_f", "a_h_norm", "a_w_out",
        "kv_ada_w", "kv_ada_b", "kv_norm", "kv_w", "kv_b_f", "kv_k_norm", "b_w_qo", "b_q_norm", "b_w_out",
        "peer_wq", "peer_subkeys", "peer_u", "peer_v"]


def kernel(**inputs):
    import numpy as np
    import concourse.bacc as bacc
    from concourse.bass_utils import run_bass_kernel_spmd

    nc = bacc.Bacc("TRN2", target_bir_lowering=False, num_devices=1)
    arrays, args = {}, {}
    for name in _INS:
        v = np.ascontiguousarray(inputs[name])
        if name == "x":
            v = v.reshape(T, D)
        arrays[f"in_{name}"] = v
        args[name] = nc.dram_tensor(f"in_{name}", v.shape, mybir.dt.from_np(v.dtype), kind="ExternalInput").ap()
    out = nc.dram_tensor("out_x", (T, D), F32, kind="ExternalOutput").ap()
    program(nc, args, out)
    r = run_bass_kernel_spmd(nc, [arrays], core_ids=[0])
    return r.results[0]["out_x"].reshape(1, T, D)
```

```python
from contextlib import ExitStack

import concourse.bass as bass
from concourse import mybir

F32 = mybir.dt.float32
F32R = mybir.dt.float32r
U32 = mybir.dt.uint32
ALU = mybir.AluOpType
ACT = mybir.ActivationFunctionType
AX = mybir.AxisListType

P = 128
D = 1024
DC = D // P
T = 256
G = T // P
EPS = 1e-6
NEG = -1e30
LOWEST = -3.0e38
N_ADA = 6

ML_H = 4
ML_DK = D // (2 * ML_H)
ML_DV = D // ML_H
CAP = 15.0

FX_H = 8
FX_D = D // FX_H

PR_H = 8
PR_KEYS = 128
PR_EXPERTS = PR_KEYS * PR_KEYS
PR_K = 16
PR_ROWS = 2 * PR_H
SEL = PR_H * PR_K

WCOLS = 512
MODS = 2 * N_ADA * DC + 2 * DC

def mod_col(layer, what):
    return (layer * N_ADA + what) * DC
SH1, SC1, G1, SH2, SC2, G2 = range(N_ADA)
KV_SH = 2 * N_ADA * DC
KV_SC = KV_SH + DC
MIX_NORM, FFN_NORM, KV_NORM, H_NORM, K_NORM, Q_NORM = 0, 2 * DC, 4 * DC, 5 * DC, 6 * DC, 6 * DC + 1
GAINS = 6 * DC + 2


class Count:

    def __init__(self):
        self.n = 0

    def up(self):
        self.n += 1
        return self.n


class Chip:

    def __init__(self, nc, ctx):
        self.nc = nc
        sb = lambda name, shape, dt=F32: ctx.enter_context(nc.sbuf_tensor(name, shape, dt))
        self.x = sb("x_res", [P, G, D])
        self.mod = sb("mod", [P, MODS])
        self.gains = sb("gains", [P, GAINS])
        self.ident = sb("ident", [P, P])
        self.ones = sb("ones", [P, P])
        self.cs = sb("silu_c", [P, DC])
        self.minus_half = sb("minus_half", [P, 1])
        self.iota = sb("iota", [P, P])
        self.bank = [ctx.enter_context(nc.psum_tensor(f"bank{k}", [P, 512], F32)) for k in range(8)]


class Phase:

    def __init__(self, nc, ctx, tag):
        self.nc, self.ctx, self.tag = nc, ctx, tag
        self.sems = []
        ctx.callback(self.close)

    def close(self):
        if self.sems:
            self.nc.clear_and_free_semaphores(self.sems)
            self.nc.all_engine_barrier()

    def sb(self, name, shape, dt=F32):
        return self.ctx.enter_context(self.nc.sbuf_tensor(f"{self.tag}_{name}", shape, dt))

    def sem(self, name):
        self.sems.append(self.nc.alloc_semaphore(f"{self.tag}_{name}"))
        return self.sems[-1]



class AdaSum:

    WIDE = 2 * D

    def __init__(self, ph, chip, mats, slots=3):
        self.chip, self.mats, self.n_slots = chip, mats, slots
        self.slots = [ph.sb(f"ada_w{k}", [P, self.WIDE]) for k in range(self.n_slots)]
        self.acc = [ph.sb(f"ada_acc{m}", [P, cols]) for m, (_, _, cols, _) in enumerate(mats)]
        self.loaded = [ph.sem(f"ada_loaded{k}") for k in range(self.n_slots)]
        self.added, self.reduced = ph.sem("ada_added"), ph.sem("ada_reduced")
        self.pieces, self.last = [], []
        for m, (_, _, cols, _) in enumerate(mats):
            width = min(self.WIDE, cols)
            self.pieces += [(m, k, col, width) for k in range(DC) for col in range(0, cols, width)]
            self.last.append(len(self.pieces))

    def load(self, eng, first_piece=0, pieces=None):
        for n in range(first_piece, len(self.pieces))[:pieces]:
            m, k, col, width = self.pieces[n]
            if n >= self.n_slots:
                eng.wait_ge(self.added, n - self.n_slots + 1)
            w, first = self.mats[m][0:2]
            eng.dma_start(self.slots[n % self.n_slots][:, 0:width],
                          w.rearrange("(p k) n -> p k n", k=DC)[:, k, first + col:first + col + width]
                          ).then_inc(self.loaded[n % self.n_slots], 16)

    def dve(self, eng, first_piece=0, pieces=None):
        for n in range(first_piece, len(self.pieces))[:pieces]:
            m, k, col, width = self.pieces[n]
            src, dst = self.slots[n % self.n_slots][:, 0:width], self.acc[m][:, col:col + width]
            factor = self.chip.cs[:, k:k + 1]
            eng.wait_ge(self.loaded[n % self.n_slots], 16 * (n // self.n_slots + 1))
            if k == 0:
                eng.tensor_scalar(dst, src, factor, None, ALU.mult).then_inc(self.added, 1)
            else:
                eng.wait_ge(self.added, n - self.mats[m][2] // width + 1)
                eng.scalar_tensor_tensor(out=dst, in0=src, scalar=factor, in1=dst, op0=ALU.mult, op1=ALU.add
                                         ).then_inc(self.added, 1)

    def pe(self, eng, ps):
        at = 0
        for m, (_, _, cols, _) in enumerate(self.mats):
            eng.wait_ge(self.added, self.last[m])
            for j in range(cols // P):
                mm = eng.matmul(ps[:, at:at + 1], self.acc[m][:, j * P:(j + 1) * P], self.chip.ones[:, 0:1],
                                start=True, stop=True)
                at += 1
        mm.then_inc(self.reduced, 1)

    def dve_finish(self, eng, ps, done):
        eng.wait_ge(self.reduced, 1)
        at = 0
        for _, _, cols, col in self.mats:
            n = cols // P
            eng.tensor_tensor(self.chip.mod[:, col:col + n], self.chip.mod[:, col:col + n], ps[:, at:at + n],
                              ALU.add).then_inc(done, 1)
            at += n


def adaln_vectors(nc, chip, a):
    with ExitStack() as ctx:
        ph = Phase(nc, ctx, "ada")
        ada = AdaSum(ph, chip, [(a["ada_w"][0], 0, 2 * D, mod_col(0, SH1))])
        cs = chip.cs
        sig = ph.sb("sig", [P, DC])
        vb = ph.sb("vb", [MODS, P])
        vg = ph.sb("vg", [GAINS, P])
        c_in, rows_in, x_in = ph.sem("c_in"), ph.sem("rows_in"), ph.sem("x_in")
        const_done, sig_done, cs_done = ph.sem("const_done"), ph.sem("sig_done"), ph.sem("cs_done")
        vec_ps, mod_done, gains_done, pool_step = (
            ph.sem(n) for n in ("vec_ps", "mod_done", "gains_done", "pool_step"))
        mps, bps, gps = chip.bank[0], chip.bank[1], chip.bank[2]
        block = ctx.enter_context(nc.Block())

        @block.sync
        def _(eng):
            eng.dma_start(cs[:, :], a["c"].rearrange("o (p k) -> (o p) k", k=DC)).then_inc(c_in, 16)
            ada.load(eng)
            eng.wait_ge(x_in, 16 * G)

        @block.scalar
        def _(eng):
            rows = [(vb, a["ada_b"].rearrange("l (j p) -> (l j) p", p=P), 0, 2 * N_ADA * DC),
                    (vb, a["kv_ada_b"].rearrange("(j p) -> j p", p=P), KV_SH, 2 * DC),
                    (vg, a["mix_norm"].rearrange("l (j p) -> (l j) p", p=P), MIX_NORM, 2 * DC),
                    (vg, a["ffn_norm"].rearrange("l (j p) -> (l j) p", p=P), FFN_NORM, 2 * DC),
                    (vg, a["kv_norm"].rearrange("(j p) -> j p", p=P), KV_NORM, DC),
                    (vg, a["a_h_norm"].rearrange("l (j p) -> (l j) p", p=P), H_NORM, DC),
                    (vg, a["kv_k_norm"].rearrange("(j p) -> j p", p=P), K_NORM, 1),
                    (vg, a["b_q_norm"].rearrange("l (j p) -> (l j) p", p=P), Q_NORM, 1)]
            for dst, src, at, n in rows:
                eng.dma_start(dst[at:at + n, :], src).then_inc(rows_in, 16)
            for g in range(G):
                eng.dma_start(chip.x[:, g, :], a["x"][g * P:(g + 1) * P, :]).then_inc(x_in, 16)
            eng.wait_ge(c_in, 16)
            eng.activation(sig[:, :], cs[:, :], ACT.Sigmoid).then_inc(sig_done, 1)
            eng.wait_ge(vec_ps, 2)
            eng.activation(chip.gains[:, :], gps[:, 0:GAINS], ACT.Copy).then_inc(gains_done, 1)
            eng.wait_ge(gains_done, 1)

        @block.gpsimd
        def _(eng):
            eng.memset(chip.ident[:, :], 0.0).then_inc(pool_step, 1)
            eng.memset(chip.ones[:, :], 1.0).then_inc(const_done, 1)
            eng.memset(chip.minus_half[:, :], -0.5).then_inc(const_done, 1)
            eng.wait_ge(pool_step, 1)
            eng.affine_select(out=chip.ident[:, :], in_=chip.ident[:, :], compare_op=ALU.not_equal, fill=1.0,
                              base=0, pattern=[[-1, P]], channel_multiplier=1).then_inc(const_done, 1)
            eng.iota(chip.iota[:, :], [[1, P]], base=0, channel_multiplier=0,
                     allow_small_or_imprecise_dtypes=True).then_inc(const_done, 1)

        @block.vector
        def _(eng):
            eng.wait_ge(sig_done, 1)
            eng.tensor_tensor(cs[:, :], cs[:, :], sig[:, :], ALU.mult).then_inc(cs_done, 1)
            eng.wait_ge(cs_done, 1)
            ada.dve(eng)
            eng.wait_ge(vec_ps, 1)
            eng.tensor_copy(chip.mod[:, :], bps[:, 0:MODS]).then_inc(mod_done, 1)
            eng.wait_ge(mod_done, 1)
            ada.dve_finish(eng, mps, mod_done)
            eng.wait_ge(mod_done, 2)

        @block.tensor
        def _(eng):
            eng.wait_ge(const_done, 4)
            eng.wait_ge(rows_in, 16 * 8)
            eng.transpose(bps[:, 0:MODS], vb[:, :], chip.ident[0:MODS, 0:MODS]).then_inc(vec_ps, 1)
            eng.transpose(gps[:, 0:GAINS], vg[:, :], chip.ident[0:GAINS, 0:GAINS]).then_inc(vec_ps, 1)
            ada.pe(eng, mps)



class Norm:

    def __init__(self, ph, chip, shift, scale, gain, tag="", xhl=None, like=None):
        self.chip, self.shift, self.scale, self.gain, self.like = chip, shift, scale, gain, like
        self.xs = like.xs if like else ph.sb(f"xs{tag}", [P, G, D])
        self.xnT = like.xnT if like else ph.sb(f"xnT{tag}", [P, DC, T])
        self.xhl = xhl
        if xhl is not None:
            self.hi, self.lo = ph.sem(f"norm_hi{tag}"), ph.sem(f"norm_lo{tag}")
        self.ss = ph.sb(f"ss{tag}", [P, G])
        self.coef = ph.sb(f"coef{tag}", [P, DC])
        self.squared, self.scaled, self.turned, self.done = (
            ph.sem(f"norm_{n}{tag}") for n in ("squared", "scaled", "turned", "done"))
        self.step, self.mean, self.root = (ph.sem(f"norm_{n}{tag}") for n in ("step", "mean", "root"))

    def act(self, eng):
        for g in range(G):
            eng.activation(self.xs[:, g, :], self.chip.x[:, g, :], ACT.Square,
                           accum_out=self.ss[:, g:g + 1]).then_inc(self.squared, 1)

    def act_hi(self, eng):
        split_hi(eng, self.xnT, self.xhl, self.done, self.hi)

    def dve_lo(self, eng):
        split_lo(eng, self.xnT, self.xhl, self.hi, self.lo)

    def dve(self, eng):
        n = Count()
        chip = self.chip
        eng.scalar_tensor_tensor(out=self.coef[:, :], in0=chip.mod[:, self.scale:self.scale + DC], scalar=1.0,
                                 in1=chip.gains[:, self.gain:self.gain + DC], op0=ALU.add, op1=ALU.mult
                                 ).then_inc(self.step, 1)
        eng.wait_ge(self.step, n.up())
        if not self.like:
            eng.wait_ge(self.squared, G)
            eng.tensor_scalar(self.ss[:, :], self.ss[:, :], 1.0 / D, EPS, ALU.mult, ALU.add).then_inc(self.mean, 1)
            eng.wait_ge(self.root, 1)
            for g in range(G):
                eng.tensor_scalar(self.xs[:, g, :], chip.x[:, g, :], self.ss[:, g:g + 1], None,
                                  ALU.mult).then_inc(self.scaled, 1)
        for c in range(DC):
            eng.wait_ge(self.turned, c // 2 + 1)
            at = (c % 2) * T
            eng.tensor_scalar(self.xnT[:, c, :], chip.bank[c // 2][:, at:at + T], self.coef[:, c:c + 1],
                              chip.mod[:, self.shift + c:self.shift + c + 1], ALU.mult, ALU.add
                              ).then_inc(self.done, 1)

    def pool(self, eng):
        eng.wait_ge(self.mean, 1)
        rsqrt(eng, self.chip, self.ss[:, :], [P, G]).then_inc(self.root, 1)

    def pe(self, eng):
        if not self.like:
            eng.wait_ge(self.scaled, G)
        turn_to_features(eng, self.chip, self.xs, self.turned)


def split_hi(eng, src, parts, ready, hi_done):
    for half in range(2):
        c = slice(half * DC // 2, (half + 1) * DC // 2)
        eng.wait_ge(ready, (half + 1) * DC // 2)
        eng.activation(parts[:, c, 0, :], src[:, c, :], ACT.Copy).then_inc(hi_done, 1)


def split_lo(eng, src, parts, hi_done, lo_done):
    for half in range(2):
        c = slice(half * DC // 2, (half + 1) * DC // 2)
        eng.wait_ge(hi_done, half + 1)
        eng.tensor_tensor(parts[:, c, 1, :], src[:, c, :], parts[:, c, 0, :].bitcast(F32), ALU.subtract
                          ).then_inc(lo_done, 1)


def rsqrt(eng, chip, values, shape):
    return eng.tensor_tensor(values, values, chip.minus_half[:, 0:1].to_broadcast(shape), ALU.pow)


def turn_to_features(eng, chip, src, turned):
    for c in range(DC):
        for g in range(G):
            at = (c % 2) * T + g * P
            mm = eng.transpose(chip.bank[c // 2][:, at:at + P], src[:, g, c * P:(c + 1) * P], chip.ident[:, :])
        if c % 2:
            mm.then_inc(turned, 1)


VECTOR = "vector"


class Project:

    SLOTS = 3

    def __init__(self, ph, blocks, tag="", slots=None):
        self.blocks = blocks
        self.slots = slots or [ph.sb(f"wst{tag}{k}", [P, DC, WCOLS]) for k in range(self.SLOTS)]
        self.loaded = [ph.sem(f"w_loaded{tag}{k}") for k in range(self.SLOTS)]
        self.done = ph.sem(f"projected{tag}")
        self.units, self.last = [], []
        for b, (_, _, width, fm) in enumerate(blocks):
            self.units += [(b, n) for n in range(1 if fm == VECTOR else width // T if fm else G)]
            self.last.append(len(self.units))

    def load(self, eng):
        for b, (w, col, width, fm) in enumerate(self.blocks):
            if b >= self.SLOTS:
                eng.wait_ge(self.done, self.last[b - self.SLOTS])
            rows = "(p c) n -> p c n" if fm == VECTOR else "(c p) n -> p c n"
            eng.dma_start(self.slots[b % self.SLOTS][:, :, 0:width],
                          w.rearrange(rows, p=P)[:, :, col:col + width]
                          ).then_inc(self.loaded[b % self.SLOTS], 16)

    def unit(self, eng, u, out, xT):
        b, n = self.units[u]
        _, _, width, fm = self.blocks[b]
        w = self.slots[b % self.SLOTS]
        eng.wait_ge(self.loaded[b % self.SLOTS], 16 * (b // self.SLOTS + 1))
        if fm == VECTOR:
            for c in range(DC):
                mm = eng.matmul(out[0:1, 0:width], xT[:, c:c + 1], w[:, c, 0:width],
                                start=(c == 0), stop=(c == DC - 1))
        elif fm:
            for half in range(2):
                f = n * T + half * P
                for c in range(DC):
                    mm = eng.matmul(out[:, half * T:(half + 1) * T], w[:, c, f:f + P], xT[:, c, :],
                                    start=(c == 0), stop=(c == DC - 1))
        else:
            for c in range(DC):
                mm = eng.matmul(out[:, 0:width], xT[:, c, n * P:(n + 1) * P], w[:, c, 0:width],
                                start=(c == 0), stop=(c == DC - 1))
        mm.then_inc(self.done, 1)


class SplitProject:

    def __init__(self, ph, blocks, slots=3):
        self.blocks, self.n_slots = blocks, slots
        self.slots = [ph.sb(f"wst{k}", [P, DC, WCOLS]) for k in range(slots)]
        self.wh = [ph.sb(f"w_hi{k}", [P, DC, T], F32R) for k in range(2)]
        self.wl = [ph.sb(f"w_lo{k}", [P, DC, T], F32R) for k in range(2)]
        self.loaded = [ph.sem(f"w_loaded{k}") for k in range(slots)]
        self.hi, self.lo, self.done = ph.sem("w_hi_done"), ph.sem("w_lo_done"), ph.sem("projected")
        self.units = 2 * len(blocks)

    def load(self, eng, first_block=0, blocks=None):
        for b in range(first_block, len(self.blocks))[:blocks]:
            w, col, _ = self.blocks[b]
            if b >= self.n_slots:
                eng.wait_ge(self.lo, 2 * (b - self.n_slots + 1))
            eng.dma_start(self.slots[b % self.n_slots][:, :, :],
                          w.rearrange("(c p) n -> p c n", p=P)[:, :, col:col + WCOLS]
                          ).then_inc(self.loaded[b % self.n_slots], 16)

    def source(self, u):
        return self.slots[u // 2 % self.n_slots][:, :, u % 2 * T:(u % 2 + 1) * T]

    def act(self, eng, u):
        if u >= self.units:
            return
        b = u // 2
        eng.wait_ge(self.loaded[b % self.n_slots], 16 * (b // self.n_slots + 1))
        if u >= 2:
            eng.wait_ge(self.done, u - 1)
        eng.activation(self.wh[u % 2][:, :, :], self.source(u), ACT.Copy).then_inc(self.hi, 1)

    def dve(self, eng, u):
        if u >= self.units:
            return
        eng.wait_ge(self.hi, u + 1)
        eng.tensor_tensor(self.wl[u % 2][:, :, :], self.source(u), self.wh[u % 2][:, :, :].bitcast(F32),
                          ALU.subtract).then_inc(self.lo, 1)

    def pe(self, eng, u, out, xhl):
        wh, wl = self.wh[u % 2], self.wl[u % 2]
        eng.wait_ge(self.lo, u + 1)
        for n in range(2):
            at = slice(n * P, (n + 1) * P)
            dst = out[:, n * T:(n + 1) * T]
            for c in range(DC):
                if self.blocks[u // 2][2]:
                    terms = ((wh[:, c, at], xhl[:, c, 0, :]), (wh[:, c, at], xhl[:, c, 1, :]),
                             (wl[:, c, at], xhl[:, c, 0, :]))
                else:
                    terms = ((xhl[:, c, 0, at], wh[:, c, :]), (xhl[:, c, 0, at], wl[:, c, :]),
                             (xhl[:, c, 1, at], wh[:, c, :]))
                for i, (lhsT, rhs) in enumerate(terms):
                    mm = eng.matmul(dst, lhsT, rhs, start=(c == 0 and i == 0), stop=(c == DC - 1 and i == 2))
        mm.then_inc(self.done, 1)


class Residual:

    def __init__(self, ph, chip, gate, banks, diag=None, row=None):
        self.chip, self.gate, self.banks = chip, gate, banks
        self.diag = diag if diag is not None else ph.sb("gate_diag", [P, D])
        self.row = row if row is not None else ph.sb("gate_row", [P, D])
        self.diag_done, self.spread, self.row_done, self.step = (
            ph.sem(n) for n in ("gate_diag_done", "gate_spread", "gate_row_done", "residual_step"))

    def dve_diag(self, eng):
        for c in range(DC):
            eng.tensor_scalar(self.diag[:, c * P:(c + 1) * P], self.chip.ident[:, :],
                              self.chip.mod[:, self.gate + c:self.gate + c + 1], None, ALU.mult
                              ).then_inc(self.diag_done, 1)

    def pe(self, eng):
        eng.wait_ge(self.diag_done, DC)
        for half in range(2):
            eng.matmul(self.banks[half][:, :], self.chip.ones[:, :], self.diag[:, half * 512:(half + 1) * 512],
                       start=True, stop=True).then_inc(self.spread, 1)

    def act(self, eng):
        for half in range(2):
            eng.wait_ge(self.spread, half + 1)
            eng.activation(self.row[:, half * 512:(half + 1) * 512], self.banks[half][:, :], ACT.Copy
                           ).then_inc(self.row_done, 1)

    def dve_add(self, eng, pieces):
        n = Count()
        eng.wait_ge(self.row_done, 2)
        for wait, y, g, groups, col, width in pieces:
            wait()
            shape = [P, groups, width]
            row = self.row[:, col:col + width].unsqueeze(1).to_broadcast(shape)
            tmp = self.diag[:, 0:groups * width].rearrange("p (g d) -> p g d", g=groups)
            eng.tensor_tensor(tmp, y.rearrange("p (g d) -> p g d", g=groups), row, ALU.mult).then_inc(self.step, 1)
            eng.wait_ge(self.step, n.up())
            x = self.chip.x[:, g:g + groups, col:col + width]
            eng.tensor_tensor(x, x, tmp, ALU.add).then_inc(self.step, 1)
            eng.wait_ge(self.step, n.up())



def mlstm(nc, chip, a):
    with ExitStack() as ctx:
        ph = Phase(nc, ctx, "ml")
        bank = chip.bank
        w = a["a_w_in"][0]
        qk, vw = ML_H * ML_DK, ML_H * ML_DV
        norm = Norm(ph, chip, mod_col(0, SH1), mod_col(0, SC1), MIX_NORM)
        GATES = 2 * qk + vw + D
        blocks = [(w, GATES, 2 * ML_H, None), (w, 0, WCOLS, True), (w, qk, WCOLS, True)]
        blocks += [(w, 2 * qk + n * WCOLS, WCOLS, False) for n in range(4)]
        blocks += [(a["a_w_out"][0], n * WCOLS, WCOLS, False) for n in range(2)]
        pj = Project(ph, blocks)
        pj.units = [(b, n) for b, n in pj.units if not (b == 0 and n == 1)]
        pj.last = [n - 1 for n in pj.last]
        U_Q, U_K, U_V, U_O, U_OUT = 1, 3, 5, 9, 13
        qT = ph.sb("qT", [P, ML_H, T])
        kT = ph.sb("kT", [P, ML_H, T])
        vx = ph.sb("vx", [P, G, ML_H, ML_DV + 1])
        so = ph.sb("so", [P, G, D])
        num = ph.sb("num", [P, G, ML_H, ML_DV + 1])
        y, yT = norm.xs, norm.xnT
        bi, bf = ph.sb("bi", [ML_H, 1]), ph.sb("bf", [ML_H, 1])
        ti, tf = ph.sb("ti", [ML_H, T]), ph.sb("tf", [ML_H, T])
        soft = ph.sb("soft", [ML_H, T])
        B, ai, M, em = (ph.sb(n, [ML_H, T]) for n in ("B", "ai", "M", "em"))
        sel = ph.sb("sel", [ML_H, ML_H, P])
        tri = ph.sb("tri", [P, P])
        acol = ph.sb("acol", [P, G, ML_H])
        ecol = ph.sb("ecol", [P, G, ML_H])
        arg = [ph.sb(f"arg{k}", [P, G, P]) for k in range(2)]
        pw = [ph.sb(f"pw{k}", [P, 3, P]) for k in range(2)]
        sd = [ph.sb(f"sd{k}", [P, 3, P]) for k in range(2)]
        junk = ph.sb("junk", [P, ML_DV])
        ssq, den, rr = (ph.sb(n, [P, G, ML_H]) for n in ("ssq", "den", "rr"))
        res = Residual(ph, chip, mod_col(0, G1), [bank[2], bank[3]])
        ada = AdaSum(ph, chip, [(a["ada_w"][0], 2 * D, 4 * D, mod_col(0, G1))])
        mod_done = ph.sem("mod_done")

        b_in, bias_ready, const_done = ph.sem("b_in"), ph.sem("bias_ready"), ph.sem("const_done")
        pool_step, dve_step, act_step = ph.sem("pool_step"), ph.sem("dve_step"), ph.sem("act_step")
        evac = ph.sem("evacuated")
        tanh_done, logf_done = ph.sem("tanh_done"), ph.sem("logf_done")
        m_done, em_done, cols_ps, cols_done = ph.sem("m_done"), ph.sem("em_done"), ph.sem("cols_ps"), ph.sem("cols_done")
        em_arg, mean_done, root_done = ph.sem("em_arg"), ph.sem("mean_done"), ph.sem("root_done")
        row_ps, score_ps, arg_done, pw_done, sd_done = (
            ph.sem(n) for n in ("row_ps", "score_ps", "arg_done", "pw_done", "sd_done"))
        num_ps, num_done, y_done, turned, yT_done = (
            ph.sem(n) for n in ("num_ps", "num_done", "y_done", "turned", "yT_done"))
        block = ctx.enter_context(nc.Block())

        def unit_bank(u):
            return bank[(4 + u) % 8]

        @block.sync
        def _(eng):
            eng.dma_start(bi[:, :], a["a_b_i"].rearrange("o h -> h o")).then_inc(b_in, 16)
            eng.dma_start(bf[:, :], a["a_b_f"].rearrange("o h -> h o")).then_inc(b_in, 16)
            pj.load(eng)

        @block.gpsimd
        def _(eng):
            eng.memset(sel[:, :, :], 0.0).then_inc(pool_step, 1)
            eng.memset(tri[:, :], 0.0).then_inc(pool_step, 1)
            eng.memset(vx[:, :, :, ML_DV:ML_DV + 1], 1.0).then_inc(const_done, 1)
            eng.wait_ge(pool_step, 2)
            eng.affine_select(out=sel[:, :, :], in_=sel[:, :, :], compare_op=ALU.not_equal, fill=1.0, base=0,
                              pattern=[[-1, ML_H], [0, P]], channel_multiplier=1).then_inc(const_done, 1)
            eng.affine_select(out=tri[:, :], in_=tri[:, :], compare_op=ALU.is_ge, fill=NEG, base=0,
                              pattern=[[1, P]], channel_multiplier=-1).then_inc(const_done, 1)
            norm.pool(eng)
            ada.load(eng)
            eng.wait_ge(mean_done, 1)
            rsqrt(eng, chip, rr[:, :, :].rearrange("p g h -> p (g h)"), [P, G * ML_H]).then_inc(root_done, 1)

        @block.tensor
        def _(eng):
            norm.pe(eng)
            eng.wait_ge(norm.done, DC)
            eng.wait_ge(pj.loaded[0], 16)
            for n in range(2):
                for c in range(DC):
                    mm = eng.matmul(unit_bank(0)[0:ML_H, n * T:(n + 1) * T],
                                    pj.slots[0][:, c, n * ML_H:(n + 1) * ML_H], norm.xnT[:, c, :],
                                    start=(c == 0), stop=(c == DC - 1))
            mm.then_inc(pj.done, 1)
            for u in range(U_Q, U_OUT):
                if u >= 8:
                    eng.wait_ge(evac, u - 8 + 1)
                pj.unit(eng, u, unit_bank(u), norm.xnT)
            eng.wait_ge(evac, U_OUT)
            eng.wait_ge(em_done, 1)
            for n, src in enumerate((ai, em)):
                for g in range(G):
                    at = (n * G + g) * ML_H
                    mm = eng.transpose(bank[4][:, at:at + ML_H], src[:, g * P:(g + 1) * P],
                                       chip.ident[0:ML_H, 0:ML_H])
            mm.then_inc(cols_ps, 1)
            eng.wait_ge(cols_done, 2)
            eng.wait_ge(const_done, 3)

            def scores(h):
                base = (h % 2) * 4
                if h >= 2:
                    eng.wait_ge(sd_done, h - 1)
                    eng.wait_ge(pw_done, h - 1)
                eng.matmul(bank[base][:, 0:T], sel[:, h, :], M[:, :], start=True, stop=True).then_inc(row_ps, 1)
                eng.matmul(bank[base + 1][:, 0:T], kT[:, h, 0:P], qT[:, h, :], start=True, stop=True)
                eng.matmul(bank[base + 1][:, T:T + P], kT[:, h, P:T], qT[:, h, P:T], start=True, stop=True
                           ).then_inc(score_ps, 1)

            def sums(h):
                base = (h % 2) * 4
                if h >= 2:
                    eng.wait_ge(num_done, G * (h - 1))
                eng.wait_ge(sd_done, h + 1)
                s = sd[h % 2]
                eng.matmul(bank[base + 2][:, 0:ML_DV + 1], s[:, 0, :], vx[:, 0, h, :], start=True, stop=True
                           ).then_inc(num_ps, 1)
                eng.matmul(bank[base + 3][:, 0:ML_DV + 1], s[:, 1, :], vx[:, 0, h, :], start=True, stop=False)
                eng.matmul(bank[base + 3][:, 0:ML_DV + 1], s[:, 2, :], vx[:, 1, h, :], start=False, stop=True
                           ).then_inc(num_ps, 1)

            for h in range(ML_H + 1):
                if h < ML_H:
                    scores(h)
                if h >= 1:
                    sums(h - 1)
            eng.wait_ge(num_done, G * ML_H)
            ada.pe(eng, bank[4])
            eng.wait_ge(y_done, G * ML_H)
            turn_to_features(eng, chip, y, turned)
            eng.wait_ge(yT_done, DC)
            for n in range(2 * G):
                pj.unit(eng, U_OUT + n, bank[4 + n], yT)
            res.pe(eng)

        @block.scalar
        def _(eng):
            norm.act(eng)
            eng.wait_ge(bias_ready, 2)
            eng.wait_ge(pj.done, 1)
            eng.activation(ti[:, :], unit_bank(0)[0:ML_H, 0:T], ACT.Tanh, bias=bi[:, 0:1], scale=1.0 / CAP
                           ).then_inc(tanh_done, 1)
            eng.activation(tf[:, :], unit_bank(0)[0:ML_H, T:2 * T], ACT.Tanh, bias=bf[:, 0:1], scale=1.0 / CAP
                           ).then_inc(evac, 1)
            eng.wait_ge(evac, 1)
            eng.activation(soft[:, :], tf[:, :], ACT.Exp, scale=-CAP).then_inc(act_step, 1)
            eng.wait_ge(act_step, 1)
            eng.activation(soft[:, :], soft[:, :], ACT.Ln, bias=1.0).then_inc(logf_done, 1)
            for u in range(U_Q, U_OUT):
                eng.wait_ge(pj.done, u + 1)
                ps = unit_bank(u)
                if u < U_K:
                    i = 2 * (u - U_Q)
                    eng.activation(qT[:, i:i + 2, :], ps[:, :], ACT.Copy).then_inc(evac, 1)
                elif u < U_V:
                    i = 2 * (u - U_K)
                    eng.activation(kT[:, i:i + 2, :], ps[:, :], ACT.Copy).then_inc(evac, 1)
                elif u < U_O:
                    b, g = divmod(u - U_V, G)
                    eng.activation(vx[:, g, 2 * b:2 * b + 2, 0:ML_DV],
                                   ps[:, :].rearrange("p (h d) -> p h d", h=2), ACT.Copy).then_inc(evac, 1)
                else:
                    b, g = divmod(u - U_O, G)
                    eng.activation(so[:, g, b * WCOLS:(b + 1) * WCOLS], ps[:, :], ACT.Sigmoid).then_inc(evac, 1)
            eng.wait_ge(em_arg, 1)
            eng.activation(em[:, :], em[:, :], ACT.Exp, scale=-1.0).then_inc(em_done, 1)
            eng.wait_ge(cols_done, 2)

            def weights(h):
                k = h % 2
                if h >= 2:
                    eng.wait_ge(sd_done, h - 1)
                eng.wait_ge(arg_done, h + 1)
                eng.activation(pw[k][:, 0, :], arg[k][:, 0, :], ACT.Exp, bias=acol[:, 0, h:h + 1])
                eng.activation(pw[k][:, 1, :], bank[(h % 2) * 4][:, P:T], ACT.Exp, bias=acol[:, 0, h:h + 1],
                               scale=-1.0)
                eng.activation(pw[k][:, 2, :], arg[k][:, 1, :], ACT.Exp, bias=acol[:, 1, h:h + 1]
                               ).then_inc(pw_done, 1)

            def take(h):
                for g in range(G):
                    ps = bank[(h % 2) * 4 + 2 + g]
                    eng.wait_ge(num_ps, G * h + g + 1)
                    if h + g:
                        eng.wait_ge(num_done, G * h + g)
                    eng.activation(junk[:, :], ps[:, 0:ML_DV], ACT.Square, accum_out=ssq[:, g, h:h + 1])
                    eng.activation(num[:, g, h, :], ps[:, 0:ML_DV + 1], ACT.Copy).then_inc(num_done, 1)

            for h in range(ML_H + 1):
                if h < ML_H:
                    weights(h)
                if h >= 1:
                    take(h - 1)
            for c in range(DC):
                eng.wait_ge(turned, c // 2 + 1)
                at = (c % 2) * T
                eng.activation(yT[:, c, :], bank[c // 2][:, at:at + T], ACT.Copy,
                               scale=chip.gains[:, H_NORM + c:H_NORM + c + 1]).then_inc(yT_done, 1)
            res.act(eng)

        @block.vector
        def _(eng):
            n = Count()
            eng.wait_ge(b_in, 32)
            eng.tensor_scalar(bi[:, :], bi[:, :], 1.0 / CAP, None, ALU.mult).then_inc(bias_ready, 1)
            eng.tensor_scalar(bf[:, :], bf[:, :], 1.0 / CAP, None, ALU.mult).then_inc(bias_ready, 1)
            norm.dve(eng)
            eng.wait_ge(logf_done, 1)
            eng.tensor_tensor_scan(B[:, :], chip_ones(chip, ML_H), soft[:, :], 0.0, ALU.mult, ALU.subtract
                                   ).then_inc(dve_step, 1)
            eng.wait_ge(dve_step, n.up())
            eng.wait_ge(tanh_done, 1)
            eng.scalar_tensor_tensor(out=ai[:, :], in0=ti[:, :], scalar=CAP, in1=B[:, :], op0=ALU.mult,
                                     op1=ALU.subtract).then_inc(dve_step, 1)
            eng.wait_ge(dve_step, n.up())
            eng.tensor_tensor_scan(M[:, :], chip_ones(chip, ML_H), ai[:, :], 0.0, ALU.mult, ALU.max
                                   ).then_inc(dve_step, 1)
            eng.wait_ge(dve_step, n.up())
            eng.tensor_tensor(em[:, :], B[:, :], M[:, :], ALU.add).then_inc(em_arg, 1)
            ada.dve(eng)
            eng.wait_ge(cols_ps, 1)
            eng.tensor_copy(acol[:, :, :], bank[4][:, 0:G * ML_H]).then_inc(cols_done, 1)
            eng.tensor_copy(ecol[:, :, :], bank[4][:, G * ML_H:2 * G * ML_H]).then_inc(cols_done, 1)

            def args(h):
                k = h % 2
                if h >= 2:
                    eng.wait_ge(pw_done, h - 1)
                eng.wait_ge(row_ps, h + 1)
                eng.tensor_tensor(arg[k][:, :, :], tri[:, :].unsqueeze(1).to_broadcast([P, G, P]),
                                  bank[k * 4][:, 0:T].rearrange("p (g t) -> p g t", g=G), ALU.subtract
                                  ).then_inc(arg_done, 1)

            def weigh(h):
                k = h % 2
                if h >= 2:
                    eng.wait_ge(num_ps, G * (h - 1))
                eng.wait_ge(score_ps, h + 1)
                eng.wait_ge(pw_done, h + 1)
                eng.scalar_tensor_tensor(out=sd[k][:, :, :], in0=bank[k * 4 + 1][:, 0:3 * P].rearrange("p (a t) -> p a t", a=3),
                                         scalar=ML_DK ** -0.5, in1=pw[k][:, :, :], op0=ALU.mult, op1=ALU.mult
                                         ).then_inc(sd_done, 1)

            for h in range(ML_H + 1):
                if h < ML_H:
                    args(h)
                if h >= 1:
                    weigh(h - 1)
            ada.dve_finish(eng, bank[4], mod_done)
            eng.wait_ge(mod_done, 1)
            res.dve_diag(eng)
            eng.wait_ge(num_done, G * ML_H)
            d = num[:, :, :, ML_DV:ML_DV + 1].rearrange("p g h o -> p g (h o)")
            eng.scalar_tensor_tensor(out=den[:, :, :], in0=d, scalar=-1.0, in1=d, op0=ALU.mult,
                                     op1=ALU.max).then_inc(dve_step, 1)
            eng.wait_ge(dve_step, n.up())
            eng.tensor_tensor(den[:, :, :], den[:, :, :], ecol[:, :, :], ALU.max).then_inc(dve_step, 1)
            eng.wait_ge(dve_step, n.up())
            eng.reciprocal(den[:, :, :], den[:, :, :]).then_inc(dve_step, 1)
            eng.wait_ge(dve_step, n.up())
            eng.tensor_tensor(rr[:, :, :], ssq[:, :, :], den[:, :, :], ALU.mult).then_inc(dve_step, 1)
            eng.wait_ge(dve_step, n.up())
            eng.tensor_tensor(rr[:, :, :], rr[:, :, :], den[:, :, :], ALU.mult).then_inc(dve_step, 1)
            eng.wait_ge(dve_step, n.up())
            eng.tensor_scalar(rr[:, :, :], rr[:, :, :], 1.0 / ML_DV, EPS, ALU.mult, ALU.add).then_inc(mean_done, 1)
            eng.wait_ge(root_done, 1)
            eng.tensor_tensor(rr[:, :, :], rr[:, :, :], den[:, :, :], ALU.mult).then_inc(dve_step, 1)
            eng.wait_ge(dve_step, n.up())
            for g in range(G):
                for h in range(ML_H):
                    cols = slice(h * ML_DV, (h + 1) * ML_DV)
                    eng.scalar_tensor_tensor(out=y[:, g, cols], in0=num[:, g, h, 0:ML_DV], scalar=rr[:, g, h:h + 1],
                                             in1=so[:, g, cols], op0=ALU.mult, op1=ALU.mult).then_inc(y_done, 1)
            res.dve_add(eng, [(lambda n=n: eng.wait_ge(pj.done, U_OUT + n + 1), bank[4 + n][:, :], n % G, 1,
                               n // G * WCOLS, WCOLS) for n in range(2 * G)])


def chip_ones(chip, rows):
    return chip.ones[0:rows, 0:1].to_broadcast([rows, T])



def fox(nc, chip, a):
    with ExitStack() as ctx:
        ph = Phase(nc, ctx, "fx")
        bank = chip.bank
        xhl = ph.sb("xhl", [P, DC, 2, T], F32R)
        norm_kv = Norm(ph, chip, KV_SH, KV_SC, KV_NORM, "kv", xhl=xhl)
        norm_q = Norm(ph, chip, mod_col(1, SH1), mod_col(1, SC1), MIX_NORM + DC, "q", xhl=xhl, like=norm_kv)
        wk, wq = a["kv_w"], a["b_w_qo"][0]
        wf = ph.sb("wf", [P, DC, FX_H])
        blocks = [(wk, 0, True), (wk, WCOLS, True), (wk, D, False), (wk, D + WCOLS, False),
                  (wq, 0, True), (wq, WCOLS, True), (wq, D, False), (wq, D + WCOLS, False),
                  (a["b_w_out"][0], 0, False), (a["b_w_out"][0], WCOLS, False)]
        pj = SplitProject(ph, blocks, slots=2)
        U_K, U_V, U_Q, U_O, U_OUT = 0, 4, 8, 12, 16
        ada = AdaSum(ph, chip, [(a["ada_w"][1], 2 * D, 4 * D, mod_col(1, G1))], slots=2)
        kT = ph.sb("kT", [P, FX_H, T])
        qT = ph.sb("qT", [P, FX_H, T])
        v = ph.sb("v", [P, G, D])
        so = ph.sb("so", [P, G, D])
        y = norm_kv.xs
        yT = norm_kv.xnT
        bf = ph.sb("bf", [FX_H, 1])
        az, lf, mn = (ph.sb(n, [FX_H, T]) for n in ("az", "lf", "mn"))
        F3 = ph.sb("F3", [FX_H, 3, P])
        F = ph.sb("F", [FX_H, T])
        Fcol = ph.sb("Fcol", [P, G, FX_H])
        sel = ph.sb("sel", [FX_H, FX_H, P])
        mask = ph.sb("mask", [P, 3, P])
        sq = [ph.sb(f"sq{k}", [P, 4, P]) for k in range(2)]
        rcol = [ph.sb(f"rcol{k}", [P, 4]) for k in range(2)]
        rdiag = [ph.sb(f"rdiag{k}", [P, 4, P]) for k in range(2)]
        rb = [ph.sb(f"rb{k}", [P, 512]) for k in range(2)]
        bias = [ph.sb(f"bias{k}", [P, 3, P]) for k in range(2)]
        lg = [ph.sb(f"lg{k}", [P, 3 * P]) for k in range(2)]
        pr = [ph.sb(f"pr{k}", [P, 3 * P]) for k in range(2)]
        pT = [ph.sb(f"pT{k}", [P, 3 * P]) for k in range(2)]
        nmax = ph.sb("nmax", [P, FX_H, G])
        rsum = ph.sb("rsum", [P, FX_H, G])
        res = Residual(ph, chip, mod_col(1, G1), [bank[2], bank[3]], diag=so[:, 0, :], row=so[:, 1, :])

        f_ps, mod_done = ph.sem("f_ps"), ph.sem("mod_done")
        yT_hi, yT_lo = ph.sem("yT_hi"), ph.sem("yT_lo")
        b_in, const_done, pool_step, dve_step, act_step = (
            ph.sem(n) for n in ("b_in", "const_done", "pool_step", "dve_step", "act_step"))
        evac, sq_done, ss_ps, logf_done, gate_read = (
            ph.sem(n) for n in ("evacuated", "sq_done", "ss_ps", "logf_done", "gate_read"))
        mean_done, root_done = ph.sem("mean_done"), ph.sem("root_done")
        rdiag_done, spread, rb_done = ph.sem("rdiag_done"), ph.sem("rms_spread"), ph.sem("rb_done")
        F_done, cols_ps, cols_done = ph.sem("F_done"), ph.sem("cols_ps"), ph.sem("cols_done")
        dve_evac = ph.sem("dve_evac")
        row_ps, bias_done, score_ps, lg_done, max_done, pr_done, pT_ps, pT_done, att_ps, y_done = (
            ph.sem(n) for n in ("row_ps", "bias_done", "score_ps", "lg_done", "max_done", "pr_done",
                                "pT_ps", "pT_done", "att_ps", "y_done"))
        turned, yT_done = ph.sem("turned"), ph.sem("yT_done")
        block = ctx.enter_context(nc.Block())

        head_units = list(range(U_K, U_V)) + list(range(U_Q, U_O))
        plain_units = list(range(U_V, U_Q)) + list(range(U_O, U_OUT))

        def unit_bank(u):
            if u in head_units:
                return bank[4 + head_units.index(u) % 3]
            return bank[plain_units.index(u) % 3]

        def wait_left(eng, u):
            if u in head_units:
                i = head_units.index(u)
                if i >= 3:
                    eng.wait_ge(dve_evac, i - 2)
            else:
                i = plain_units.index(u)
                if i >= 3:
                    eng.wait_ge(evac, i - 2)
                else:
                    eng.wait_ge(gate_read, 1)

        @block.sync
        def _(eng):
            pj.load(eng, 0, 1)
            eng.dma_start(bf[:, :], a["kv_b_f"].rearrange("(h o) -> h o", o=1)).then_inc(b_in, 16)
            eng.dma_start(wf[:, :, :], wk.rearrange("(c p) n -> p c n", p=P)[:, :, 2 * D:2 * D + FX_H]
                          ).then_inc(b_in, 16)
            pj.load(eng, 1, 1)
            for b in range(2, len(blocks)):
                ada.load(eng, 2 * (b - 2), 2)
                pj.load(eng, b, 1)

        @block.gpsimd
        def _(eng):
            eng.memset(sel[:, :, :], 0.0).then_inc(pool_step, 1)
            eng.memset(mask[:, :, :], 0.0).then_inc(pool_step, 1)
            eng.wait_ge(pool_step, 2)
            eng.affine_select(out=sel[:, :, :], in_=sel[:, :, :], compare_op=ALU.not_equal, fill=1.0, base=0,
                              pattern=[[-1, FX_H], [0, P]], channel_multiplier=1).then_inc(const_done, 1)
            for n in (0, 2):
                eng.affine_select(out=mask[:, n, :], in_=mask[:, n, :], compare_op=ALU.is_ge, fill=-NEG, base=0,
                                  pattern=[[-1, P]], channel_multiplier=1).then_inc(const_done, 1)

            def root(i):
                eng.wait_ge(mean_done, i + 1)
                rsqrt(eng, chip, rcol[i % 2][:, :], [P, 4]).then_inc(root_done, 1)

            norm_kv.pool(eng)
            for i in range(len(head_units)):
                root(i)

        @block.tensor
        def _(eng):
            norm_kv.pe(eng)
            eng.wait_ge(norm_kv.done, DC)
            eng.wait_ge(b_in, 32)
            for c in range(DC):
                mm = eng.matmul(bank[0][0:FX_H, 0:T], wf[:, c, :], norm_kv.xnT[:, c, :],
                                start=(c == 0), stop=(c == DC - 1))
            mm.then_inc(f_ps, 1)
            eng.wait_ge(norm_kv.lo, 2)

            def squares(u):
                i = head_units.index(u)
                eng.wait_ge(sq_done, i + 1)
                if i >= 1:
                    eng.wait_ge(mean_done, i)
                for n in range(4):
                    mm = eng.matmul(bank[3][:, n:n + 1], sq[i % 2][:, n, :], chip.ones[:, 0:1], start=True, stop=True)
                mm.then_inc(ss_ps, 1)

            def spread_rms(u):
                i = head_units.index(u)
                eng.wait_ge(rdiag_done, 4 * (i + 1))
                if i >= 1:
                    eng.wait_ge(rb_done, i)
                eng.matmul(bank[7][:, :], chip.ones[:, :], rdiag[i % 2][:, :, :], start=True, stop=True
                           ).then_inc(spread, 1)

            def rms_behind(u):
                if u - 1 in head_units:
                    squares(u - 1)
                if u - 2 in head_units:
                    spread_rms(u - 2)

            for u in range(U_K, U_Q):
                wait_left(eng, u)
                pj.pe(eng, u, unit_bank(u), xhl)
                rms_behind(u)
            eng.wait_ge(evac, U_Q - U_V)
            norm_q.pe(eng)
            eng.wait_ge(norm_q.lo, 2)
            for u in range(U_Q, U_OUT):
                wait_left(eng, u)
                pj.pe(eng, u, unit_bank(u), xhl)
                rms_behind(u)
            eng.wait_ge(F_done, 1)
            eng.wait_ge(evac, len(plain_units))
            eng.wait_ge(dve_evac, len(head_units))
            for g in range(G):
                mm = eng.transpose(bank[0][:, g * FX_H:(g + 1) * FX_H], F[:, g * P:(g + 1) * P],
                                   chip.ident[0:FX_H, 0:FX_H])
            mm.then_inc(cols_ps, 1)
            eng.wait_ge(cols_done, 1)
            eng.wait_ge(const_done, 3)

            def scores(h):
                base = (h % 2) * 4
                if h >= 2:
                    eng.wait_ge(lg_done, h - 1)
                eng.matmul(bank[base][:, 0:3 * P], sel[:, h, :], F3[:, :, :], start=True, stop=True
                           ).then_inc(row_ps, 1)
                eng.matmul(bank[base + 1][:, 0:P], qT[:, h, 0:P], kT[:, h, 0:P], start=True, stop=True)
                eng.matmul(bank[base + 1][:, P:3 * P], qT[:, h, P:T], kT[:, h, :], start=True, stop=True
                           ).then_inc(score_ps, 1)

            def turn(h):
                base = (h % 2) * 4
                eng.wait_ge(pr_done, G * (h + 1))
                if h >= 2:
                    eng.wait_ge(pT_done, h - 1)
                for n in range(3):
                    mm = eng.transpose(bank[base + 2][:, n * P:(n + 1) * P], pr[h % 2][:, n * P:(n + 1) * P],
                                       chip.ident[:, :])
                mm.then_inc(pT_ps, 1)

            def attend(h):
                base = (h % 2) * 4
                cols = slice(h * FX_D, (h + 1) * FX_D)
                eng.wait_ge(pT_done, h + 1)
                if h >= 2:
                    eng.wait_ge(y_done, G * (h - 1))
                p = pT[h % 2]
                eng.matmul(bank[base + 3][:, 0:FX_D], p[:, 0:P], v[:, 0, cols], start=True, stop=True)
                eng.matmul(bank[base + 3][:, FX_D:2 * FX_D], p[:, P:2 * P], v[:, 0, cols], start=True, stop=False)
                eng.matmul(bank[base + 3][:, FX_D:2 * FX_D], p[:, 2 * P:3 * P], v[:, 1, cols], start=False,
                           stop=True).then_inc(att_ps, 1)

            for h in range(FX_H + 2):
                if h < FX_H:
                    scores(h)
                if 1 <= h <= FX_H:
                    turn(h - 1)
                if h >= 2:
                    attend(h - 2)
            eng.wait_ge(y_done, G * FX_H)
            ada.pe(eng, bank[4])
            turn_to_features(eng, chip, y, turned)
            eng.wait_ge(yT_lo, 2)
            for n in range(4):
                pj.pe(eng, U_OUT + n, bank[4 + n], xhl)
            res.pe(eng)

        @block.scalar
        def _(eng):
            norm_kv.act(eng)
            pj.act(eng, 0)
            pj.act(eng, 1)
            norm_kv.act_hi(eng)
            eng.wait_ge(f_ps, 1)
            eng.wait_ge(b_in, 32)
            eng.activation(az[:, :], bank[0][0:FX_H, 0:T], ACT.Abs, bias=bf[:, 0:1]).then_inc(act_step, 1)
            eng.wait_ge(act_step, 1)
            eng.activation(az[:, :], az[:, :], ACT.Exp, scale=-1.0).then_inc(act_step, 1)
            eng.wait_ge(act_step, 2)
            eng.activation(az[:, :], az[:, :], ACT.Ln, bias=1.0).then_inc(logf_done, 1)
            for u in range(U_K, U_OUT):
                if u == U_Q:
                    norm_q.act_hi(eng)
                pj.act(eng, u + 2)
                eng.wait_ge(pj.done, u + 1)
                ps = unit_bank(u)
                if u in head_units:
                    i = head_units.index(u)
                    if i >= 2:
                        eng.wait_ge(ss_ps, i - 1)
                    eng.activation(sq[i % 2][:, :, :], ps[:, :], ACT.Square).then_inc(sq_done, 1)
                elif u < U_Q:
                    cols = slice((u - U_V) * T, (u - U_V + 1) * T)
                    eng.activation(v[:, :, cols], ps[:, :].rearrange("p (g d) -> p g d", g=G), ACT.Copy
                                   ).then_inc(evac, 1)
                else:
                    cols = slice((u - U_O) * T, (u - U_O + 1) * T)
                    eng.activation(so[:, :, cols], ps[:, :].rearrange("p (g d) -> p g d", g=G), ACT.Sigmoid
                                   ).then_inc(evac, 1)
                if u - 2 in head_units:
                    i = head_units.index(u - 2)
                    eng.wait_ge(spread, i + 1)
                    if i >= 2:
                        eng.wait_ge(dve_evac, i - 1)
                    eng.activation(rb[i % 2][:, :], bank[7][:, :], ACT.Copy).then_inc(rb_done, 1)

            def soft(h):
                k = h % 2
                eng.wait_ge(max_done, G * (h + 1))
                if h >= 2:
                    eng.wait_ge(pT_ps, h - 1)
                eng.activation(pr[k][:, 0:P], lg[k][:, 0:P], ACT.Exp, bias=nmax[:, h, 0:1],
                               accum_out=rsum[:, h, 0:1]).then_inc(pr_done, 1)
                eng.activation(pr[k][:, P:3 * P], lg[k][:, P:3 * P], ACT.Exp, bias=nmax[:, h, 1:2],
                               accum_out=rsum[:, h, 1:2]).then_inc(pr_done, 1)

            def take(h):
                k = h % 2
                eng.wait_ge(pT_ps, h + 1)
                if h >= 2:
                    eng.wait_ge(att_ps, h - 1)
                eng.activation(pT[k][:, :], bank[k * 4 + 2][:, 0:3 * P], ACT.Copy).then_inc(pT_done, 1)

            for h in range(FX_H + 1):
                if h < FX_H:
                    soft(h)
                if h >= 1:
                    take(h - 1)
            for c in range(DC):
                eng.wait_ge(turned, c // 2 + 1)
                at = (c % 2) * T
                eng.activation(yT[:, c, :], bank[c // 2][:, at:at + T], ACT.Copy).then_inc(yT_done, 1)
            split_hi(eng, yT, xhl, yT_done, yT_hi)
            pj.act(eng, U_OUT + 2)
            pj.act(eng, U_OUT + 3)
            res.act(eng)

        @block.vector
        def _(eng):
            n = Count()
            norm_kv.dve(eng)
            norm_kv.dve_lo(eng)
            pj.dve(eng, 0)
            pj.dve(eng, 1)
            eng.wait_ge(act_step, 1)
            eng.tensor_scalar(mn[:, :], bank[0][0:FX_H, 0:T], bf[:, 0:1], 0.0, ALU.add, ALU.min
                              ).then_inc(gate_read, 1)
            eng.wait_ge(gate_read, 1)
            eng.wait_ge(logf_done, 1)
            eng.tensor_tensor(lf[:, :], mn[:, :], az[:, :], ALU.subtract).then_inc(dve_step, 1)
            eng.wait_ge(dve_step, n.up())
            eng.tensor_tensor_scan(F[:, :], chip_ones(chip, FX_H), lf[:, :], 0.0, ALU.mult, ALU.add
                                   ).then_inc(dve_step, 1)
            eng.wait_ge(dve_step, n.up())
            eng.tensor_copy(F3[:, 0, :], F[:, 0:P])
            eng.tensor_copy(F3[:, 1:3, :], F[:, :].rearrange("h (g t) -> h g t", g=G)).then_inc(F_done, 1)

            def rms_diag(i):
                k = i % 2
                eng.wait_ge(ss_ps, i + 1)
                eng.tensor_scalar(rcol[k][:, :], bank[3][:, 0:4], 1.0 / FX_D, EPS, ALU.mult, ALU.add
                                  ).then_inc(mean_done, 1)
                eng.wait_ge(root_done, i + 1)
                if i >= 2:
                    eng.wait_ge(spread, i - 1)
                for m in range(4):
                    eng.tensor_scalar(rdiag[k][:, m, :], chip.ident[:, :], rcol[k][:, m:m + 1], None, ALU.mult
                                      ).then_inc(rdiag_done, 1)

            def normalise(i):
                u = head_units[i]
                gain, dst, at = (K_NORM, kT, 2 * (u - U_K)) if u < U_V else (Q_NORM, qT, 2 * (u - U_Q))
                eng.wait_ge(rb_done, i + 1)
                eng.scalar_tensor_tensor(out=dst[:, at:at + 2, :],
                                         in0=unit_bank(u)[:, :].rearrange("p (h t) -> p h t", h=2),
                                         scalar=chip.gains[:, gain:gain + 1],
                                         in1=rb[i % 2][:, :].rearrange("p (h t) -> p h t", h=2),
                                         op0=ALU.mult, op1=ALU.mult).then_inc(dve_evac, 1)

            for u in range(U_K, U_OUT):
                if u == U_Q:
                    norm_q.dve(eng)
                    norm_q.dve_lo(eng)
                pj.dve(eng, u + 2)
                if u - 1 in head_units:
                    rms_diag(head_units.index(u - 1))
                if u - 2 in head_units:
                    normalise(head_units.index(u - 2))
                ada.dve(eng, u, 1)
            eng.wait_ge(cols_ps, 1)
            eng.tensor_copy(Fcol[:, :, :], bank[0][:, 0:G * FX_H]).then_inc(cols_done, 1)
            eng.wait_ge(cols_done, 1)

            def logits(h):
                k = h % 2
                ps, sc = bank[k * 4], bank[k * 4 + 1]
                eng.wait_ge(row_ps, h + 1)
                eng.scalar_tensor_tensor(out=bias[k][:, 0, :], in0=ps[:, 0:P], scalar=Fcol[:, 0, h:h + 1],
                                         in1=mask[:, 0, :], op0=ALU.subtract, op1=ALU.add).then_inc(bias_done, 1)
                eng.scalar_tensor_tensor(out=bias[k][:, 1:3, :], in0=ps[:, P:3 * P].rearrange("p (a s) -> p a s", a=2),
                                         scalar=Fcol[:, 1, h:h + 1], in1=mask[:, 1:3, :],
                                         op0=ALU.subtract, op1=ALU.add).then_inc(bias_done, 1)
                eng.wait_ge(bias_done, 2 * (h + 1))
                eng.wait_ge(score_ps, h + 1)
                if h >= 2:
                    eng.wait_ge(pr_done, G * (h - 1))
                eng.scalar_tensor_tensor(out=lg[k][:, :], in0=sc[:, 0:3 * P], scalar=FX_D ** -0.5,
                                         in1=bias[k][:, :, :].rearrange("p a s -> p (a s)"),
                                         op0=ALU.mult, op1=ALU.subtract).then_inc(lg_done, 1)
                eng.wait_ge(lg_done, h + 1)
                eng.tensor_reduce(nmax[:, h, 0:1], lg[k][:, 0:P], AX.X, ALU.max, negate=True).then_inc(max_done, 1)
                eng.tensor_reduce(nmax[:, h, 1:2], lg[k][:, P:3 * P], AX.X, ALU.max, negate=True
                                  ).then_inc(max_done, 1)

            def gate(h):
                k = h % 2
                cols = slice(h * FX_D, (h + 1) * FX_D)
                eng.wait_ge(att_ps, h + 1)
                eng.reciprocal(rsum[:, h, :], rsum[:, h, :]).then_inc(dve_step, 1)
                eng.wait_ge(dve_step, n.up())
                for g in range(G):
                    eng.scalar_tensor_tensor(out=y[:, g, cols], in0=bank[k * 4 + 3][:, g * FX_D:(g + 1) * FX_D],
                                             scalar=rsum[:, h, g:g + 1], in1=so[:, g, cols],
                                             op0=ALU.mult, op1=ALU.mult).then_inc(y_done, 1)

            for h in range(FX_H + 2):
                if h < FX_H:
                    logits(h)
                if h >= 2:
                    gate(h - 2)

            ada.dve_finish(eng, bank[4], mod_done)
            eng.wait_ge(mod_done, 1)
            res.dve_diag(eng)
            split_lo(eng, yT, xhl, yT_hi, yT_lo)
            pj.dve(eng, U_OUT + 2)
            pj.dve(eng, U_OUT + 3)
            res.dve_add(eng, [(lambda n=n: eng.wait_ge(pj.done, U_OUT + n + 1), bank[4 + n][:, :], 0, G, n * T, T)
                              for n in range(4)])



class PeerState:

    def __init__(self, ph):
        self.xhl = ph.sb("xhl", [P, DC, 2, T], F32R)
        self.iT = ph.sb("iT", [SEL, T])
        self.jT = ph.sb("jT", [SEL, T])
        self.gT = ph.sb("gT", [SEL, T])


def peer_route(nc, chip, a, layer, st):
    with ExitStack() as ctx:
        ph = Phase(nc, ctx, f"rt{layer}")
        bank = chip.bank
        norm = Norm(ph, chip, mod_col(layer, SH2), mod_col(layer, SC2), FFN_NORM + layer * DC)
        blocks = [(a["peer_wq"][layer], n * WCOLS, WCOLS, True) for n in range(4)]
        VEC = 8
        if layer == 0:
            blocks += [(m, n * WCOLS, WCOLS, VECTOR) for m in (a["ada_w"][1], a["kv_ada_w"])
                       for n in range(2 * D // WCOLS)]
        pj = Project(ph, blocks)
        vectors = len(pj.units) - VEC
        sk = ph.sb("sk", [PR_KEYS, 2, P])
        skT = ph.sb("skT", [P, 2, PR_KEYS])
        qT = [ph.sb(f"qT{k}", [P, 4, T]) for k in range(2)]
        sc = ph.sb("sc", [P, G, PR_ROWS, PR_KEYS])
        left = ph.sb("left", [P, 2, T])
        top = ph.sb("top", [P, G, PR_ROWS, PR_K])
        topi = ph.sb("topi", [P, G, PR_ROWS, PR_K], U32)
        topf = ph.sb("topf", [P, G, PR_ROWS, PR_K])
        cand = ph.sb("cand", [P, PR_H, PR_K, PR_K])
        eq = ph.sb("eq", [P, PR_H, PR_K, PR_K])
        best = ph.sb("best", [P, G, PR_H, PR_K])
        pos = ph.sb("pos", [P, G, PR_H, PR_K], U32)
        posk = ph.sb("posk", [P, 2, PR_H, PR_K], U32)
        posf = ph.sb("posf", [P, 2, PR_H, PR_K])
        key = ph.sb("key", [P, G, 2, SEL])
        gate = ph.sb("gate", [P, G, SEL])
        gsum = ph.sb("gsum", [P, G, PR_H])
        row = ph.sb("row", [1, vectors * WCOLS]) if vectors else None

        row_done, vec_ps = ph.sem("row_done"), ph.sem("vec_ps")
        sk_in, sk_ps, sk_done = ph.sem("sk_in"), ph.sem("sk_ps"), ph.sem("sk_done")
        hi_done, dve_step = ph.sem("hi_done"), ph.sem("dve_step")
        q_done, sc_ps, sc_done = ph.sem("q_done"), ph.sem("sc_ps"), ph.sem("sc_done")
        diff_done, exp_done, sel_done, turned, taken = (
            ph.sem(n) for n in ("diff_done", "exp_done", "sel_done", "turned", "taken"))
        block = ctx.enter_context(nc.Block())

        @block.sync
        def _(eng):
            eng.dma_start(sk[:, :, :], a["peer_subkeys"][layer].rearrange("h k d -> k h d")).then_inc(sk_in, 16)
            pj.load(eng)

        @block.gpsimd
        def _(eng):
            norm.pool(eng)

        @block.tensor
        def _(eng):
            eng.wait_ge(sk_in, 16)
            for n in range(2):
                mm = eng.transpose(bank[4][:, n * P:(n + 1) * P], sk[:, n, :], chip.ident[:, :])
            mm.then_inc(sk_ps, 1)
            norm.pe(eng)
            eng.wait_ge(norm.done, DC)
            eng.wait_ge(sk_done, 1)

            def queries(b):
                if b >= 2:
                    eng.wait_ge(q_done, 2 * (b - 1))
                for n in range(2):
                    pj.unit(eng, 2 * b + n, bank[4 + (2 * b + n) % 4], norm.xnT)

            def scores(b):
                eng.wait_ge(q_done, 2 * (b + 1))
                for g in range(G):
                    if b >= 2:
                        eng.wait_ge(sc_done, G * (b - 2) + g + 1)
                    for j in range(4):
                        mm = eng.matmul(bank[(G * b + g) % 4][:, j * P:(j + 1) * P], qT[b % 2][:, j, g * P:(g + 1) * P],
                                        skT[:, j % 2, :], start=True, stop=True)
                    mm.then_inc(sc_ps, 1)

            for b in range(5):
                if b < 4:
                    queries(b)
                if b >= 1:
                    scores(b - 1)
            eng.wait_ge(sc_done, 4 * G)
            if vectors:
                for u in range(vectors):
                    if u >= 2:
                        eng.wait_ge(row_done, u - 1)
                    pj.unit(eng, VEC + u, bank[4 + u % 2], chip.cs)
                eng.wait_ge(row_done, vectors)
                for j in range(4 * vectors):
                    mm = eng.matmul(bank[6][:, j:j + 1], row[0:1, j * P:(j + 1) * P], chip.ones[0:1, 0:1],
                                    start=True, stop=True)
                mm.then_inc(vec_ps, 1)
            for g in range(G):
                eng.wait_ge(sel_done, g + 1)
                for n in range(3):
                    src = gate[:, g, :] if n == 2 else key[:, g, n, :]
                    mm = eng.transpose(bank[g][:, n * P:(n + 1) * P], src, chip.ident[:, :])
                mm.then_inc(turned, 1)

        @block.scalar
        def _(eng):
            norm.act(eng)
            eng.wait_ge(sk_ps, 1)
            eng.activation(skT[:, :, :], bank[4][:, 0:2 * P], ACT.Copy).then_inc(sk_done, 1)
            eng.wait_ge(norm.done, DC)
            eng.activation(st.xhl[:, :, 0, :], norm.xnT[:, :, :], ACT.Copy).then_inc(hi_done, 1)

            def take_q(b):
                for n in range(2):
                    eng.wait_ge(pj.done, 2 * b + n + 1)
                    if b >= 2:
                        eng.wait_ge(sc_ps, G * (b - 1))
                    eng.activation(qT[b % 2][:, 2 * n:2 * n + 2, :], bank[4 + (2 * b + n) % 4][:, :], ACT.Copy
                                   ).then_inc(q_done, 1)

            def take_s(b):
                for g in range(G):
                    eng.wait_ge(sc_ps, G * b + g + 1)
                    eng.activation(sc[:, g, 4 * b:4 * b + 4, :], bank[(G * b + g) % 4][:, :], ACT.Copy
                                   ).then_inc(sc_done, 1)

            for b in range(5):
                if b < 4:
                    take_q(b)
                if b >= 1:
                    take_s(b - 1)
            for u in range(vectors):
                eng.wait_ge(pj.done, VEC + u + 1)
                eng.activation(row[0:1, u * WCOLS:(u + 1) * WCOLS], bank[4 + u % 2][0:1, :], ACT.Copy
                               ).then_inc(row_done, 1)
            for g in range(G):
                eng.wait_ge(diff_done, g + 1)
                eng.activation(gate[:, g, :], gate[:, g, :], ACT.Exp).then_inc(exp_done, 1)
            for g in range(G):
                eng.wait_ge(turned, g + 1)
                for n, dst in enumerate((st.iT, st.jT, st.gT)):
                    eng.activation(dst[:, g * P:(g + 1) * P], bank[g][:, n * P:(n + 1) * P], ACT.Copy
                                   ).then_inc(taken, 1)
            eng.wait_ge(taken, 3 * G)


        @block.vector
        def _(eng):
            n = Count()
            norm.dve(eng)
            eng.wait_ge(hi_done, 1)
            eng.tensor_tensor(st.xhl[:, :, 1, :], norm.xnT[:, :, :], st.xhl[:, :, 0, :].bitcast(F32), ALU.subtract)

            def top16(values, out, index, spare):
                eng.max(out[..., 0:8], values).then_inc(dve_step, 1)
                eng.wait_ge(dve_step, n.up())
                eng.max_index(index[..., 0:8], out[..., 0:8], values)
                eng.match_replace(spare, out[..., 0:8], values, LOWEST).then_inc(dve_step, 1)
                eng.wait_ge(dve_step, n.up())
                eng.max(out[..., 8:16], spare).then_inc(dve_step, 1)
                eng.wait_ge(dve_step, n.up())
                eng.max_index(index[..., 8:16], out[..., 8:16], spare).then_inc(dve_step, 1)
                n.up()

            for b in range(4):
                for g in range(G):
                    eng.wait_ge(sc_done, G * b + g + 1)
                    for r in range(4 * b, 4 * b + 4):
                        top16(sc[:, g, r, :], top[:, g, r, :], topi[:, g, r, :], left[:, r % 2, 0:PR_KEYS])
            for g in range(G):
                eng.wait_ge(dve_step, n.n)
                eng.tensor_copy(topf[:, g, :, :], topi[:, g, :, :])
                pair = top[:, g, :, :].rearrange("p (h two) k -> p h two k", two=2)
                eng.tensor_tensor(cand[:, :, :, :],
                                  pair[:, :, 0, :].unsqueeze(3).to_broadcast([P, PR_H, PR_K, PR_K]),
                                  pair[:, :, 1, :].unsqueeze(2).to_broadcast([P, PR_H, PR_K, PR_K]), ALU.add
                                  ).then_inc(dve_step, 1)
                eng.wait_ge(dve_step, n.up())
                for h in range(PR_H):
                    top16(cand[:, h, :, :].rearrange("p a b -> p (a b)"), best[:, g, h, :], pos[:, g, h, :],
                          left[:, h % 2, :])
                eng.wait_ge(dve_step, n.n)
                eng.tensor_tensor(gate[:, g, :].rearrange("p (h k) -> p h k", h=PR_H), best[:, g, :, :],
                                  best[:, g, :, 0:1].to_broadcast([P, PR_H, PR_K]), ALU.subtract
                                  ).then_inc(diff_done, 1)
                eng.tensor_scalar(posk[:, 0, :, :], pos[:, g, :, :], 4, None, ALU.logical_shift_right
                                  ).then_inc(dve_step, 1)
                eng.wait_ge(dve_step, n.up())
                eng.tensor_scalar(posk[:, 1, :, :], pos[:, g, :, :], 15, None, ALU.bitwise_and).then_inc(dve_step, 1)
                eng.wait_ge(dve_step, n.up())
                eng.tensor_copy(posf[:, :, :, :], posk[:, :, :, :]).then_inc(dve_step, 1)
                eng.wait_ge(dve_step, n.up())
                for half in range(2):
                    wide = [P, PR_H, PR_K, PR_K]
                    eng.tensor_tensor(eq[:, :, :, :], posf[:, half, :, :].unsqueeze(3).to_broadcast(wide),
                                      chip.iota[:, 0:PR_K].unsqueeze(1).unsqueeze(1).to_broadcast(wide), ALU.is_equal
                                      ).then_inc(dve_step, 1)
                    eng.wait_ge(dve_step, n.up())
                    tf = topf[:, g, :, :].rearrange("p (h two) k -> p h two k", two=2)[:, :, half, :]
                    eng.tensor_tensor(eq[:, :, :, :], eq[:, :, :, :], tf.unsqueeze(2).to_broadcast(wide), ALU.mult
                                      ).then_inc(dve_step, 1)
                    eng.wait_ge(dve_step, n.up())
                    eng.tensor_reduce(key[:, g, half, :].rearrange("p (h k) -> p h k", h=PR_H), eq[:, :, :, :],
                                      AX.X, ALU.add).then_inc(dve_step, 1)
                    eng.wait_ge(dve_step, n.up())
                eng.wait_ge(exp_done, g + 1)
                gv = gate[:, g, :].rearrange("p (h k) -> p h k", h=PR_H)
                eng.tensor_reduce(gsum[:, g, :], gv, AX.X, ALU.add).then_inc(dve_step, 1)
                eng.wait_ge(dve_step, n.up())
                eng.reciprocal(gsum[:, g, :], gsum[:, g, :]).then_inc(dve_step, 1)
                eng.wait_ge(dve_step, n.up())
                eng.tensor_tensor(gv, gv, gsum[:, g, :].unsqueeze(2).to_broadcast([P, PR_H, PR_K]), ALU.mult
                                  ).then_inc(sel_done, 1)
                eng.wait_ge(sel_done, g + 1)
            if vectors:
                eng.wait_ge(vec_ps, 1)
                for at, first in ((0, mod_col(1, SH1)), (2 * DC, KV_SH)):
                    later = chip.mod[:, first:first + 2 * DC]
                    eng.tensor_tensor(later, later, bank[6][:, at:at + 2 * DC], ALU.add).then_inc(dve_step, 1)
                    n.up()
                eng.wait_ge(dve_step, n.n)



def peer_experts(nc, chip, a, layer, st):
    TILES = PR_EXPERTS // P
    SLOTS = 4
    TOK = 4
    with ExitStack() as ctx:
        ph = Phase(nc, ctx, f"ex{layer}")
        bank = chip.bank
        act = ph.sb("act", [P, TILES, T])
        stream = [ph.sb(f"stream{k}", [P, D]) for k in range(SLOTS)]
        hi = [ph.sb(f"hi{k}", [P, D], F32R) for k in range(2)]
        lo = [ph.sb(f"lo{k}", [P, D], F32R) for k in range(2)]
        whi = [ph.sb(f"whi{k}", [P, T], F32R) for k in range(2)]
        wlo = [ph.sb(f"wlo{k}", [P, T], F32R) for k in range(2)]
        oj = [ph.sb(f"oj{k}", [SEL, TOK, P]) for k in range(2)]
        oi = [ph.sb(f"oi{k}", [SEL, TOK, P]) for k in range(2)]
        res = Residual(ph, chip, mod_col(layer, G2), [bank[4], bank[5]], diag=stream[0], row=stream[1])

        loaded = [ph.sem(f"loaded{k}") for k in range(SLOTS)]
        slot_free = ph.sem("slot_free")
        turned = ph.sem("turned")
        hi_done, lo_done = ph.sem("hi_done"), ph.sem("lo_done")
        half_free = ph.sem("half_free")
        parts_free = ph.sem("parts_free")
        dot_ps, dot_free = ph.sem("dot_ps"), ph.sem("dot_free")
        dj_done, abs_done, oj_done, oi_done, hot_free, gate_ps, gate_free = (
            ph.sem(n) for n in ("dj_done", "abs_done", "oj_done", "oi_done", "hot_free", "gate_ps", "gate_free"))
        vhi, vlo, wparts, wl_done, v_free = (ph.sem(n) for n in ("vhi", "vlo", "wparts", "wl_done", "v_free"))
        y_ps = ph.sem("y_ps")
        block = ctx.enter_context(nc.Block())

        def tiles(eng, body, ahead=None, skip=0):
            if ahead:
                ahead(0, 0)
            first = skip
            for k in range(first):
                if ahead:
                    ahead(k + 1, (k + 1) % SLOTS)
                body(k, k % SLOTS)
            with eng.Fori(first // SLOTS, TILES // SLOTS - 1) as i:
                for k in range(SLOTS):
                    t = i * SLOTS + k
                    if ahead:
                        ahead(i * SLOTS + (k + 1), (k + 1) % SLOTS)
                    body(t, k)
            for k in range(SLOTS):
                t = TILES - SLOTS + k
                if ahead and k < SLOTS - 1:
                    ahead(t + 1, k + 1)
                body(t, k)

        @block.sync
        def _(eng):
            def load_u(t, k):
                eng.wait_ge(slot_free, t + 1)
                eng.dma_start(stream[k][:, :], a["peer_u"][layer][bass.ds(t * P, P), :]).then_inc(loaded[k], 16)

            def load_v(t, k):
                eng.wait_ge(slot_free, t + (TILES + 1))
                eng.dma_start(stream[k][:, :], a["peer_v"][layer][bass.ds(t * P, P), :]).then_inc(loaded[k], 16)

            tiles(eng, load_u)
            tiles(eng, load_v)

        @block.tensor
        def _(eng):
            eng.sem_inc(slot_free, SLOTS)

            def turn(t, k):
                p = k % 2
                eng.wait_ge(loaded[k], (t - k) * (16 // SLOTS) + 16)
                for half in range(2):
                    eng.wait_ge(half_free, t * 2 + (half + 1))
                    for c in range(4):
                        col = half * 512 + c * P
                        mm = eng.transpose(bank[2 * p + half][:, c * P:(c + 1) * P], stream[k][:, col:col + P],
                                           chip.ident[:, :])
                    mm.then_inc(turned, 1)

            def dots(t, k):
                p = k % 2
                eng.wait_ge(lo_done, t * 2 + 2)
                eng.wait_ge(dot_free, t + 1)
                out = bank[4 + p][:, 0:T]
                for c in range(DC):
                    col = slice(c * P, (c + 1) * P)
                    eng.matmul(out, hi[p][:, col], st.xhl[:, c, 0, :], start=(c == 0), stop=False)
                    eng.matmul(out, hi[p][:, col], st.xhl[:, c, 1, :], start=False, stop=False)
                    mm = eng.matmul(out, lo[p][:, col], st.xhl[:, c, 0, :], start=False, stop=(c == DC - 1))
                mm.then_inc(dot_ps, 1)

            tiles(eng, dots, ahead=turn)

            def gates(q, k):
                eng.wait_ge(oj_done, q + 1)
                eng.wait_ge(oi_done, q + 1)
                eng.wait_ge(gate_free, q + 1)
                for n in range(TOK):
                    mm = eng.matmul(bank[6 + k][:, n * P:(n + 1) * P], oj[k][:, n, :], oi[k][:, n, :],
                                    start=True, stop=True)
                mm.then_inc(gate_ps, 1)

            with eng.Fori(0, T // TOK // 2) as i:
                for k in range(2):
                    gates(i * 2 + k, k)

            def sums(t, k, first=False, last=False):
                p = k % 2
                eng.wait_ge(wl_done, t + 1)
                for half in range(2):
                    cols = slice(half * 512, (half + 1) * 512)
                    eng.wait_ge(vlo, t * 2 + (half + 1))
                    for g in range(G):
                        tok = slice(g * P, (g + 1) * P)
                        for n, (w, v) in enumerate(((whi, hi), (whi, lo), (wlo, hi))):
                            mm = eng.matmul(bank[2 * g + half][:, :], w[p][:, tok], v[p][:, cols],
                                            start=(first and n == 0), stop=(last and n == 2))
                mm.then_inc(v_free, 1)

            for k in range(SLOTS):
                sums(k, k, first=(k == 0))
            with eng.Fori(1, TILES // SLOTS - 1) as i:
                for k in range(SLOTS):
                    sums(i * SLOTS + k, k)
            for k in range(SLOTS):
                sums(TILES - SLOTS + k, k, last=(k == SLOTS - 1))
            res.pe(eng)

        @block.scalar
        def _(eng):
            nc.scalar.preload_act_table(ACT.Gelu)

            def split(t, k):
                p = k % 2
                for half in range(2):
                    eng.wait_ge(turned, t * 2 + (half + 1))
                    if half == 0:
                        eng.wait_ge(dot_ps, t + 1)
                    eng.activation(hi[p][:, half * 512:(half + 1) * 512], bank[2 * p + half][:, :], ACT.Copy
                                   ).then_inc(hi_done, 1)

            def gelu(t, k):
                eng.wait_ge(dot_ps, t + 3)
                eng.activation(act[:, bass.ds(t, 1), :], bank[4 + k % 2][:, 0:T], ACT.Gelu).then_inc(dot_free, 1)

            eng.sem_inc(dot_ps, 2)
            eng.sem_inc(dot_free, 2)
            tiles(eng, gelu, ahead=split)

            def parts(t, k):
                p = k % 2
                eng.wait_ge(loaded[k], (t - k) * (16 // SLOTS) + (16 + 16 * TILES // SLOTS))
                eng.wait_ge(v_free, t + 1)
                eng.activation(whi[p][:, :], act[:, bass.ds(t, 1), :], ACT.Copy).then_inc(wparts, 1)
                for half in range(2):
                    cols = slice(half * 512, (half + 1) * 512)
                    eng.activation(hi[p][:, cols], stream[k][:, cols], ACT.Copy).then_inc(vhi, 1)

            def hot(q, k):
                eng.wait_ge(dj_done, q + 1)
                eng.activation(oj[k][:, :, :], oj[k][:, :, :], ACT.Abs).then_inc(abs_done, 1)
                eng.wait_ge(abs_done, q + 1)
                eng.activation(oj[k][:, :, :], oj[k][:, :, :], ACT.Relu, bias=1.0, scale=-1.0).then_inc(oj_done, 1)

            with eng.Fori(0, T // TOK // 2) as i:
                for k in range(2):
                    hot(i * 2 + k, k)

            eng.sem_inc(v_free, 2)
            eng.wait_ge(gate_free, T // TOK + 2)
            tiles(eng, parts)
            res.act(eng)

        @block.gpsimd
        def _(eng):
            def hot(q, k):
                eng.wait_ge(hot_free, q + 1)
                eng.tensor_tensor(oj[k][:, :, :], chip.iota[:, :].unsqueeze(1).to_broadcast([SEL, TOK, P]),
                                  st.jT[:, bass.ds(q * TOK, TOK)].unsqueeze(2).to_broadcast([SEL, TOK, P]),
                                  ALU.subtract).then_inc(dj_done, 1)

            with eng.Fori(0, T // TOK // 2) as i:
                for k in range(2):
                    hot(i * 2 + k, k)

        @block.vector
        def _(eng):
            eng.sem_inc(half_free, 4)

            def low(t, k):
                p = k % 2
                for half in range(2):
                    cols = slice(half * 512, (half + 1) * 512)
                    eng.wait_ge(hi_done, t * 2 + (half + 1))
                    eng.tensor_tensor(lo[p][:, cols], bank[2 * p + half][:, :], hi[p][:, cols].bitcast(F32),
                                      ALU.subtract).then_inc(lo_done, 1)
                    eng.wait_ge(lo_done, t * 2 + (half + 1))
                    eng.sem_inc(half_free, 1)
                eng.sem_inc(slot_free, 1)

            with eng.Fori(0, TILES // SLOTS) as i:
                for k in range(SLOTS):
                    low(i * SLOTS + k, k)

            eng.sem_inc(hot_free, 2)
            eng.sem_inc(gate_free, 2)

            def hot(q, k):
                eng.wait_ge(gate_ps, q + 1)
                for n in range(TOK):
                    t = q * TOK + n
                    mm = eng.tensor_scalar(oi[k][:, n, :], chip.iota[:, :], st.iT[:, bass.ds(t, 1)],
                                           st.gT[:, bass.ds(t, 1)], ALU.is_equal, ALU.mult)
                mm.then_inc(oi_done, 1)

            def apply(q, k):
                eng.wait_ge(gate_ps, q + 3)
                eng.sem_inc(hot_free, 1)
                cell = act[:, :, bass.ds(q * TOK, TOK)]
                eng.tensor_tensor(cell, bank[6 + k][:, :].rearrange("p (t i) -> p i t", t=TOK), cell, ALU.mult
                                  ).then_inc(gate_free, 1)

            eng.sem_inc(gate_ps, 2)
            eng.wait_ge(dot_free, TILES + 2)
            hot(0, 0)
            with eng.Fori(0, T // TOK // 2 - 1) as i:
                for k in range(2):
                    hot(i * 2 + (k + 1), (k + 1) % 2)
                    apply(i * 2 + k, k)
            last = T // TOK
            hot(last - 1, 1)
            apply(last - 2, 0)
            apply(last - 1, 1)

            def low_parts(t, k):
                p = k % 2
                eng.wait_ge(wparts, t + 1)
                eng.tensor_tensor(wlo[p][:, :], act[:, bass.ds(t, 1), :], whi[p][:, :].bitcast(F32), ALU.subtract
                                  ).then_inc(wl_done, 1)
                for half in range(2):
                    cols = slice(half * 512, (half + 1) * 512)
                    eng.wait_ge(vhi, t * 2 + (half + 1))
                    eng.tensor_tensor(lo[p][:, cols], stream[k][:, cols], hi[p][:, cols].bitcast(F32), ALU.subtract
                                      ).then_inc(vlo, 1)
                eng.wait_ge(vlo, t * 2 + 2)
                eng.sem_inc(slot_free, 1)

            eng.wait_ge(gate_free, last + 2)
            with eng.Fori(0, TILES // SLOTS) as i:
                for k in range(SLOTS):
                    low_parts(i * SLOTS + k, k)

            res.dve_diag(eng)

            res.dve_add(eng, [(lambda: eng.wait_ge(v_free, TILES + 2), bank[2 * g + half][:, :], g, 1,
                               half * WCOLS, WCOLS) for g in range(G) for half in range(2)])


def store(nc, chip, out):
    with ExitStack() as ctx:
        stored = ctx.enter_context(nc.semaphore("stored"))
        block = ctx.enter_context(nc.Block())

        @block.sync
        def _(eng):
            for g in range(G):
                eng.dma_start(out[g * P:(g + 1) * P, :], chip.x[:, g, :]).then_inc(stored, 16)
            eng.wait_ge(stored, 16 * G)


def program(nc, a, out):
    with ExitStack() as ctx:
        chip = Chip(nc, ctx)
        adaln_vectors(nc, chip, a)
        mixers = (mlstm, fox)
        for layer, mixer in enumerate(mixers):
            mixer(nc, chip, a)
            with ExitStack() as inner:
                st = PeerState(Phase(nc, inner, f"peer{layer}"))
                peer_route(nc, chip, a, layer, st)
                peer_experts(nc, chip, a, layer, st)
        store(nc, chip, out)


_INS = ["x", "c", "ada_w", "ada_b", "mix_norm", "ffn_norm", "a_w_in", "a_b_i", "a_b_f", "a_h_norm", "a_w_out",
        "kv_ada_w", "kv_ada_b", "kv_norm", "kv_w", "kv_b_f", "kv_k_norm", "b_w_qo", "b_q_norm", "b_w_out",
        "peer_wq", "peer_subkeys", "peer_u", "peer_v"]


def kernel(**inputs):
    import numpy as np
    import concourse.bacc as bacc
    from concourse.bass_utils import run_bass_kernel_spmd

    nc = bacc.Bacc("TRN2", target_bir_lowering=False, num_devices=1)
    arrays, args = {}, {}
    for name in _INS:
        v = np.ascontiguousarray(inputs[name])
        if name == "x":
            v = v.reshape(T, D)
        arrays[f"in_{name}"] = v
        args[name] = nc.dram_tensor(f"in_{name}", v.shape, mybir.dt.from_np(v.dtype), kind="ExternalInput").ap()
    out = nc.dram_tensor("out_x", (T, D), F32, kind="ExternalOutput").ap()
    program(nc, args, out)
    r = run_bass_kernel_spmd(nc, [arrays], core_ids=[0])
    return r.results[0]["out_x"].reshape(1, T, D)
```

```python
from contextlib import ExitStack

import concourse.bass as bass
from concourse import mybir

F32 = mybir.dt.float32
F32R = mybir.dt.float32r
U32 = mybir.dt.uint32
ALU = mybir.AluOpType
ACT = mybir.ActivationFunctionType
AX = mybir.AxisListType

P = 128
D = 1024
DC = D // P
T = 256
G = T // P
EPS = 1e-6
NEG = -1e30
LOWEST = -3.0e38
N_ADA = 6

ML_H = 4
ML_DK = D // (2 * ML_H)
ML_DV = D // ML_H
CAP = 15.0

FX_H = 8
FX_D = D // FX_H

PR_H = 8
PR_KEYS = 128
PR_EXPERTS = PR_KEYS * PR_KEYS
PR_K = 16
PR_ROWS = 2 * PR_H
SEL = PR_H * PR_K

WCOLS = 512
MODS = 2 * N_ADA * DC + 2 * DC

def mod_col(layer, what):
    return (layer * N_ADA + what) * DC
SH1, SC1, G1, SH2, SC2, G2 = range(N_ADA)
KV_SH = 2 * N_ADA * DC
KV_SC = KV_SH + DC
MIX_NORM, FFN_NORM, KV_NORM, H_NORM, K_NORM, Q_NORM = 0, 2 * DC, 4 * DC, 5 * DC, 6 * DC, 6 * DC + 1
GAINS = 6 * DC + 2


class Count:

    def __init__(self):
        self.n = 0

    def up(self):
        self.n += 1
        return self.n


class Chip:

    def __init__(self, nc, ctx):
        self.nc = nc
        sb = lambda name, shape, dt=F32: ctx.enter_context(nc.sbuf_tensor(name, shape, dt))
        self.x = sb("x_res", [P, G, D])
        self.mod = sb("mod", [P, MODS])
        self.gains = sb("gains", [P, GAINS])
        self.ident = sb("ident", [P, P])
        self.ones = sb("ones", [P, P])
        self.cs = sb("silu_c", [P, DC])
        self.minus_half = sb("minus_half", [P, 1])
        self.iota = sb("iota", [P, P])
        self.minus_ident_r = sb("minus_ident_r", [P, P], F32R)
        self.iota_r = sb("iota_r", [1, P], F32R)
        self.ones_r = sb("ones_r", [1, P], F32R)
        self.bank = [ctx.enter_context(nc.psum_tensor(f"bank{k}", [P, 512], F32)) for k in range(8)]


class Phase:

    def __init__(self, nc, ctx, tag):
        self.nc, self.ctx, self.tag = nc, ctx, tag
        self.sems = []
        ctx.callback(self.close)

    def close(self):
        if self.sems:
            self.nc.clear_and_free_semaphores(self.sems)
            self.nc.all_engine_barrier()

    def sb(self, name, shape, dt=F32):
        return self.ctx.enter_context(self.nc.sbuf_tensor(f"{self.tag}_{name}", shape, dt))

    def sem(self, name):
        self.sems.append(self.nc.alloc_semaphore(f"{self.tag}_{name}"))
        return self.sems[-1]



class AdaSum:

    def __init__(self, ph, chip, mats, slots=3, wide=2 * D, tag="ada"):
        self.chip, self.mats, self.n_slots = chip, mats, slots
        self.slots = [ph.sb(f"{tag}_w{k}", [P, wide]) for k in range(self.n_slots)]
        self.acc = [ph.sb(f"{tag}_acc{m}", [P, cols]) for m, (_, _, cols, _) in enumerate(mats)]
        self.loaded = [ph.sem(f"{tag}_loaded{k}") for k in range(self.n_slots)]
        self.added, self.reduced = ph.sem(f"{tag}_added"), ph.sem(f"{tag}_reduced")
        self.pieces, self.last = [], []
        for m, (_, _, cols, _) in enumerate(mats):
            width = min(wide, cols)
            self.pieces += [(m, k, col, width) for k in range(DC) for col in range(0, cols, width)]
            self.last.append(len(self.pieces))

    def load(self, eng, first_piece=0, pieces=None):
        for n in range(first_piece, len(self.pieces))[:pieces]:
            m, k, col, width = self.pieces[n]
            if n >= self.n_slots:
                eng.wait_ge(self.added, n - self.n_slots + 1)
            w, first = self.mats[m][0:2]
            eng.dma_start(self.slots[n % self.n_slots][:, 0:width],
                          w.rearrange("(p k) n -> p k n", k=DC)[:, k, first + col:first + col + width]
                          ).then_inc(self.loaded[n % self.n_slots], 16)

    def dve(self, eng, first_piece=0, pieces=None):
        for n in range(first_piece, len(self.pieces))[:pieces]:
            m, k, col, width = self.pieces[n]
            src, dst = self.slots[n % self.n_slots][:, 0:width], self.acc[m][:, col:col + width]
            factor = self.chip.cs[:, k:k + 1]
            eng.wait_ge(self.loaded[n % self.n_slots], 16 * (n // self.n_slots + 1))
            if k == 0:
                eng.tensor_scalar(dst, src, factor, None, ALU.mult).then_inc(self.added, 1)
            else:
                eng.wait_ge(self.added, n - self.mats[m][2] // width + 1)
                eng.scalar_tensor_tensor(out=dst, in0=src, scalar=factor, in1=dst, op0=ALU.mult, op1=ALU.add
                                         ).then_inc(self.added, 1)

    def pe(self, eng, ps):
        at = 0
        for m, (_, _, cols, _) in enumerate(self.mats):
            eng.wait_ge(self.added, self.last[m])
            for j in range(cols // P):
                mm = eng.matmul(ps[:, at:at + 1], self.acc[m][:, j * P:(j + 1) * P], self.chip.ones[:, 0:1],
                                start=True, stop=True)
                at += 1
        mm.then_inc(self.reduced, 1)

    def dve_finish(self, eng, ps, done):
        eng.wait_ge(self.reduced, 1)
        at = 0
        for _, _, cols, col in self.mats:
            n = cols // P
            eng.tensor_tensor(self.chip.mod[:, col:col + n], self.chip.mod[:, col:col + n], ps[:, at:at + n],
                              ALU.add).then_inc(done, 1)
            at += n


def adaln_vectors(nc, chip, a):
    with ExitStack() as ctx:
        ph = Phase(nc, ctx, "ada")
        ada = AdaSum(ph, chip, [(a["ada_w"][0], 0, 2 * D, mod_col(0, SH1))])
        cs = chip.cs
        sig = ph.sb("sig", [P, DC])
        vb = ph.sb("vb", [MODS, P])
        vg = ph.sb("vg", [GAINS, P])
        c_in, rows_in, x_in = ph.sem("c_in"), ph.sem("rows_in"), ph.sem("x_in")
        const_done, sig_done, cs_done = ph.sem("const_done"), ph.sem("sig_done"), ph.sem("cs_done")
        vec_ps, mod_done, gains_done, pool_step = (
            ph.sem(n) for n in ("vec_ps", "mod_done", "gains_done", "pool_step"))
        mps, bps, gps = chip.bank[0], chip.bank[1], chip.bank[2]
        block = ctx.enter_context(nc.Block())

        @block.sync
        def _(eng):
            eng.dma_start(cs[:, :], a["c"].rearrange("o (p k) -> (o p) k", k=DC)).then_inc(c_in, 16)
            ada.load(eng)
            eng.wait_ge(x_in, 16 * G)

        @block.scalar
        def _(eng):
            rows = [(vb, a["ada_b"].rearrange("l (j p) -> (l j) p", p=P), 0, 2 * N_ADA * DC),
                    (vb, a["kv_ada_b"].rearrange("(j p) -> j p", p=P), KV_SH, 2 * DC),
                    (vg, a["mix_norm"].rearrange("l (j p) -> (l j) p", p=P), MIX_NORM, 2 * DC),
                    (vg, a["ffn_norm"].rearrange("l (j p) -> (l j) p", p=P), FFN_NORM, 2 * DC),
                    (vg, a["kv_norm"].rearrange("(j p) -> j p", p=P), KV_NORM, DC),
                    (vg, a["a_h_norm"].rearrange("l (j p) -> (l j) p", p=P), H_NORM, DC),
                    (vg, a["kv_k_norm"].rearrange("(j p) -> j p", p=P), K_NORM, 1),
                    (vg, a["b_q_norm"].rearrange("l (j p) -> (l j) p", p=P), Q_NORM, 1)]
            for dst, src, at, n in rows:
                eng.dma_start(dst[at:at + n, :], src).then_inc(rows_in, 16)
            for g in range(G):
                eng.dma_start(chip.x[:, g, :], a["x"][g * P:(g + 1) * P, :]).then_inc(x_in, 16)
            eng.wait_ge(c_in, 16)
            eng.activation(sig[:, :], cs[:, :], ACT.Sigmoid).then_inc(sig_done, 1)
            eng.wait_ge(const_done, 4)
            eng.activation(chip.minus_ident_r[:, :], chip.ident[:, :], ACT.Copy, scale=-1.0)
            eng.activation(chip.iota_r[:, :], chip.iota[0:1, :], ACT.Copy)
            eng.activation(chip.ones_r[:, :], chip.ones[0:1, :], ACT.Copy)
            eng.wait_ge(vec_ps, 2)
            eng.activation(chip.gains[:, :], gps[:, 0:GAINS], ACT.Copy).then_inc(gains_done, 1)
            eng.wait_ge(gains_done, 1)

        @block.gpsimd
        def _(eng):
            eng.memset(chip.ident[:, :], 0.0).then_inc(pool_step, 1)
            eng.memset(chip.ones[:, :], 1.0).then_inc(const_done, 1)
            eng.memset(chip.minus_half[:, :], -0.5).then_inc(const_done, 1)
            eng.wait_ge(pool_step, 1)
            eng.affine_select(out=chip.ident[:, :], in_=chip.ident[:, :], compare_op=ALU.not_equal, fill=1.0,
                              base=0, pattern=[[-1, P]], channel_multiplier=1).then_inc(const_done, 1)
            eng.iota(chip.iota[:, :], [[1, P]], base=0, channel_multiplier=0,
                     allow_small_or_imprecise_dtypes=True).then_inc(const_done, 1)

        @block.vector
        def _(eng):
            eng.wait_ge(sig_done, 1)
            eng.tensor_tensor(cs[:, :], cs[:, :], sig[:, :], ALU.mult).then_inc(cs_done, 1)
            eng.wait_ge(cs_done, 1)
            ada.dve(eng)
            eng.wait_ge(vec_ps, 1)
            eng.tensor_copy(chip.mod[:, :], bps[:, 0:MODS]).then_inc(mod_done, 1)
            eng.wait_ge(mod_done, 1)
            ada.dve_finish(eng, mps, mod_done)
            eng.wait_ge(mod_done, 2)

        @block.tensor
        def _(eng):
            eng.wait_ge(const_done, 4)
            eng.wait_ge(rows_in, 16 * 8)
            eng.transpose(bps[:, 0:MODS], vb[:, :], chip.ident[0:MODS, 0:MODS]).then_inc(vec_ps, 1)
            eng.transpose(gps[:, 0:GAINS], vg[:, :], chip.ident[0:GAINS, 0:GAINS]).then_inc(vec_ps, 1)
            ada.pe(eng, mps)



class Norm:

    def __init__(self, ph, chip, shift, scale, gain, tag="", xhl=None, like=None):
        self.chip, self.shift, self.scale, self.gain, self.like = chip, shift, scale, gain, like
        self.xs = like.xs if like else ph.sb(f"xs{tag}", [P, G, D])
        self.xnT = like.xnT if like else ph.sb(f"xnT{tag}", [P, DC, T])
        self.xhl = xhl
        if xhl is not None:
            self.hi, self.lo = ph.sem(f"norm_hi{tag}"), ph.sem(f"norm_lo{tag}")
        self.ss = ph.sb(f"ss{tag}", [P, G])
        self.coef = ph.sb(f"coef{tag}", [P, DC])
        self.squared, self.scaled, self.turned, self.done = (
            ph.sem(f"norm_{n}{tag}") for n in ("squared", "scaled", "turned", "done"))
        self.step, self.mean, self.root = (ph.sem(f"norm_{n}{tag}") for n in ("step", "mean", "root"))

    def act(self, eng):
        for g in range(G):
            eng.activation(self.xs[:, g, :], self.chip.x[:, g, :], ACT.Square,
                           accum_out=self.ss[:, g:g + 1]).then_inc(self.squared, 1)

    def act_hi(self, eng):
        split_hi(eng, self.xnT, self.xhl, self.done, self.hi)

    def dve_lo(self, eng):
        split_lo(eng, self.xnT, self.xhl, self.hi, self.lo)

    def dve(self, eng):
        n = Count()
        chip = self.chip
        eng.scalar_tensor_tensor(out=self.coef[:, :], in0=chip.mod[:, self.scale:self.scale + DC], scalar=1.0,
                                 in1=chip.gains[:, self.gain:self.gain + DC], op0=ALU.add, op1=ALU.mult
                                 ).then_inc(self.step, 1)
        eng.wait_ge(self.step, n.up())
        if not self.like:
            eng.wait_ge(self.squared, G)
            eng.tensor_scalar(self.ss[:, :], self.ss[:, :], 1.0 / D, EPS, ALU.mult, ALU.add).then_inc(self.mean, 1)
            eng.wait_ge(self.root, 1)
            for g in range(G):
                eng.tensor_scalar(self.xs[:, g, :], chip.x[:, g, :], self.ss[:, g:g + 1], None,
                                  ALU.mult).then_inc(self.scaled, 1)
        for c in range(DC):
            eng.wait_ge(self.turned, c // 2 + 1)
            at = (c % 2) * T
            eng.tensor_scalar(self.xnT[:, c, :], chip.bank[c // 2][:, at:at + T], self.coef[:, c:c + 1],
                              chip.mod[:, self.shift + c:self.shift + c + 1], ALU.mult, ALU.add
                              ).then_inc(self.done, 1)

    def pool(self, eng):
        eng.wait_ge(self.mean, 1)
        rsqrt(eng, self.chip, self.ss[:, :], [P, G]).then_inc(self.root, 1)

    def pe(self, eng):
        if not self.like:
            eng.wait_ge(self.scaled, G)
        turn_to_features(eng, self.chip, self.xs, self.turned)


def split_hi(eng, src, parts, ready, hi_done):
    for half in range(2):
        c = slice(half * DC // 2, (half + 1) * DC // 2)
        eng.wait_ge(ready, (half + 1) * DC // 2)
        eng.activation(parts[:, c, 0, :], src[:, c, :], ACT.Copy).then_inc(hi_done, 1)


def split_lo(eng, src, parts, hi_done, lo_done):
    for half in range(2):
        c = slice(half * DC // 2, (half + 1) * DC // 2)
        eng.wait_ge(hi_done, half + 1)
        eng.tensor_tensor(parts[:, c, 1, :], src[:, c, :], parts[:, c, 0, :].bitcast(F32), ALU.subtract
                          ).then_inc(lo_done, 1)


def rsqrt(eng, chip, values, shape):
    return eng.tensor_tensor(values, values, chip.minus_half[:, 0:1].to_broadcast(shape), ALU.pow)


def turn_to_features(eng, chip, src, turned):
    for c in range(DC):
        for g in range(G):
            at = (c % 2) * T + g * P
            mm = eng.transpose(chip.bank[c // 2][:, at:at + P], src[:, g, c * P:(c + 1) * P], chip.ident[:, :])
        if c % 2:
            mm.then_inc(turned, 1)


VECTOR = "vector"


class Project:

    SLOTS = 3

    def __init__(self, ph, blocks, tag="", slots=None):
        self.blocks = blocks
        self.slots = slots or [ph.sb(f"wst{tag}{k}", [P, DC, WCOLS]) for k in range(self.SLOTS)]
        self.loaded = [ph.sem(f"w_loaded{tag}{k}") for k in range(self.SLOTS)]
        self.done = ph.sem(f"projected{tag}")
        self.units, self.last = [], []
        for b, (_, _, width, fm) in enumerate(blocks):
            self.units += [(b, n) for n in range(1 if fm == VECTOR else width // T if fm else G)]
            self.last.append(len(self.units))

    def load(self, eng):
        for b, (w, col, width, fm) in enumerate(self.blocks):
            if b >= self.SLOTS:
                eng.wait_ge(self.done, self.last[b - self.SLOTS])
            rows = "(p c) n -> p c n" if fm == VECTOR else "(c p) n -> p c n"
            eng.dma_start(self.slots[b % self.SLOTS][:, :, 0:width],
                          w.rearrange(rows, p=P)[:, :, col:col + width]
                          ).then_inc(self.loaded[b % self.SLOTS], 16)

    def unit(self, eng, u, out, xT):
        b, n = self.units[u]
        _, _, width, fm = self.blocks[b]
        w = self.slots[b % self.SLOTS]
        eng.wait_ge(self.loaded[b % self.SLOTS], 16 * (b // self.SLOTS + 1))
        if fm == VECTOR:
            for c in range(DC):
                mm = eng.matmul(out[0:1, 0:width], xT[:, c:c + 1], w[:, c, 0:width],
                                start=(c == 0), stop=(c == DC - 1))
        elif fm:
            for half in range(2):
                f = n * T + half * P
                for c in range(DC):
                    mm = eng.matmul(out[:, half * T:(half + 1) * T], w[:, c, f:f + P], xT[:, c, :],
                                    start=(c == 0), stop=(c == DC - 1))
        else:
            for c in range(DC):
                mm = eng.matmul(out[:, 0:width], xT[:, c, n * P:(n + 1) * P], w[:, c, 0:width],
                                start=(c == 0), stop=(c == DC - 1))
        mm.then_inc(self.done, 1)


class SplitProject:

    def __init__(self, ph, blocks, slots=3):
        self.blocks, self.n_slots = blocks, slots
        self.slots = [ph.sb(f"wst{k}", [P, DC, WCOLS]) for k in range(slots)]
        self.wh = [ph.sb(f"w_hi{k}", [P, DC, T], F32R) for k in range(2)]
        self.wl = [ph.sb(f"w_lo{k}", [P, DC, T], F32R) for k in range(2)]
        self.loaded = [ph.sem(f"w_loaded{k}") for k in range(slots)]
        self.hi, self.lo, self.done = ph.sem("w_hi_done"), ph.sem("w_lo_done"), ph.sem("projected")
        self.units = 2 * len(blocks)

    def load(self, eng, first_block=0, blocks=None):
        for b in range(first_block, len(self.blocks))[:blocks]:
            w, col, _ = self.blocks[b]
            if b >= self.n_slots:
                eng.wait_ge(self.lo, 2 * (b - self.n_slots + 1))
            eng.dma_start(self.slots[b % self.n_slots][:, :, :],
                          w.rearrange("(c p) n -> p c n", p=P)[:, :, col:col + WCOLS]
                          ).then_inc(self.loaded[b % self.n_slots], 16)

    def source(self, u):
        return self.slots[u // 2 % self.n_slots][:, :, u % 2 * T:(u % 2 + 1) * T]

    def act(self, eng, u):
        if u >= self.units:
            return
        b = u // 2
        eng.wait_ge(self.loaded[b % self.n_slots], 16 * (b // self.n_slots + 1))
        if u >= 2:
            eng.wait_ge(self.done, u - 1)
        eng.activation(self.wh[u % 2][:, :, :], self.source(u), ACT.Copy).then_inc(self.hi, 1)

    def dve(self, eng, u):
        if u >= self.units:
            return
        eng.wait_ge(self.hi, u + 1)
        eng.tensor_tensor(self.wl[u % 2][:, :, :], self.source(u), self.wh[u % 2][:, :, :].bitcast(F32),
                          ALU.subtract).then_inc(self.lo, 1)

    def pe(self, eng, u, out, xhl):
        wh, wl = self.wh[u % 2], self.wl[u % 2]
        eng.wait_ge(self.lo, u + 1)
        for n in range(2):
            at = slice(n * P, (n + 1) * P)
            dst = out[:, n * T:(n + 1) * T]
            for c in range(DC):
                if self.blocks[u // 2][2]:
                    terms = ((wh[:, c, at], xhl[:, c, 0, :]), (wh[:, c, at], xhl[:, c, 1, :]),
                             (wl[:, c, at], xhl[:, c, 0, :]))
                else:
                    terms = ((xhl[:, c, 0, at], wh[:, c, :]), (xhl[:, c, 0, at], wl[:, c, :]),
                             (xhl[:, c, 1, at], wh[:, c, :]))
                for i, (lhsT, rhs) in enumerate(terms):
                    mm = eng.matmul(dst, lhsT, rhs, start=(c == 0 and i == 0), stop=(c == DC - 1 and i == 2))
        mm.then_inc(self.done, 1)


class Residual:

    def __init__(self, ph, chip, gate, banks, diag=None, row=None):
        self.chip, self.gate, self.banks = chip, gate, banks
        self.diag = diag if diag is not None else ph.sb("gate_diag", [P, D])
        self.row = row if row is not None else ph.sb("gate_row", [P, D])
        self.diag_done, self.spread, self.row_done, self.step = (
            ph.sem(n) for n in ("gate_diag_done", "gate_spread", "gate_row_done", "residual_step"))

    def dve_diag(self, eng):
        for c in range(DC):
            eng.tensor_scalar(self.diag[:, c * P:(c + 1) * P], self.chip.ident[:, :],
                              self.chip.mod[:, self.gate + c:self.gate + c + 1], None, ALU.mult
                              ).then_inc(self.diag_done, 1)

    def pe(self, eng):
        eng.wait_ge(self.diag_done, DC)
        for half in range(2):
            eng.matmul(self.banks[half][:, :], self.chip.ones[:, :], self.diag[:, half * 512:(half + 1) * 512],
                       start=True, stop=True).then_inc(self.spread, 1)

    def act(self, eng):
        for half in range(2):
            eng.wait_ge(self.spread, half + 1)
            eng.activation(self.row[:, half * 512:(half + 1) * 512], self.banks[half][:, :], ACT.Copy
                           ).then_inc(self.row_done, 1)

    def dve_add(self, eng, pieces):
        n = Count()
        eng.wait_ge(self.row_done, 2)
        for wait, y, g, groups, col, width in pieces:
            wait()
            shape = [P, groups, width]
            row = self.row[:, col:col + width].unsqueeze(1).to_broadcast(shape)
            tmp = self.diag[:, 0:groups * width].rearrange("p (g d) -> p g d", g=groups)
            eng.tensor_tensor(tmp, y.rearrange("p (g d) -> p g d", g=groups), row, ALU.mult).then_inc(self.step, 1)
            eng.wait_ge(self.step, n.up())
            x = self.chip.x[:, g:g + groups, col:col + width]
            eng.tensor_tensor(x, x, tmp, ALU.add).then_inc(self.step, 1)
            eng.wait_ge(self.step, n.up())



def mlstm(nc, chip, a):
    with ExitStack() as ctx:
        ph = Phase(nc, ctx, "ml")
        bank = chip.bank
        w = a["a_w_in"][0]
        qk, vw = ML_H * ML_DK, ML_H * ML_DV
        norm = Norm(ph, chip, mod_col(0, SH1), mod_col(0, SC1), MIX_NORM)
        GATES = 2 * qk + vw + D
        blocks = [(w, GATES, 2 * ML_H, None), (w, 0, WCOLS, True), (w, qk, WCOLS, True)]
        blocks += [(w, 2 * qk + n * WCOLS, WCOLS, False) for n in range(4)]
        blocks += [(a["a_w_out"][0], n * WCOLS, WCOLS, False) for n in range(2)]
        pj = Project(ph, blocks)
        pj.units = [(b, n) for b, n in pj.units if not (b == 0 and n == 1)]
        pj.last = [n - 1 for n in pj.last]
        U_Q, U_K, U_V, U_O, U_OUT = 1, 3, 5, 9, 13
        qT = ph.sb("qT", [P, ML_H, T])
        kT = ph.sb("kT", [P, ML_H, T])
        vx = ph.sb("vx", [P, G, ML_H, ML_DV + 1])
        so = ph.sb("so", [P, G, D])
        num = ph.sb("num", [P, G, ML_H, ML_DV + 1])
        y, yT = norm.xs, norm.xnT
        bi, bf = ph.sb("bi", [ML_H, 1]), ph.sb("bf", [ML_H, 1])
        ti, tf = ph.sb("ti", [ML_H, T]), ph.sb("tf", [ML_H, T])
        soft = ph.sb("soft", [ML_H, T])
        B, ai, M, em = (ph.sb(n, [ML_H, T]) for n in ("B", "ai", "M", "em"))
        sel = ph.sb("sel", [ML_H, ML_H, P])
        tri = ph.sb("tri", [P, P])
        acol = ph.sb("acol", [P, G, ML_H])
        ecol = ph.sb("ecol", [P, G, ML_H])
        arg = [ph.sb(f"arg{k}", [P, G, P]) for k in range(2)]
        pw = [ph.sb(f"pw{k}", [P, 3, P]) for k in range(2)]
        sd = [ph.sb(f"sd{k}", [P, 3, P]) for k in range(2)]
        junk = ph.sb("junk", [P, ML_DV])
        ssq, den, rr = (ph.sb(n, [P, G, ML_H]) for n in ("ssq", "den", "rr"))
        res = Residual(ph, chip, mod_col(0, G1), [bank[2], bank[3]])
        ada = AdaSum(ph, chip, [(a["ada_w"][0], 2 * D, 4 * D, mod_col(0, G1))])
        ada1 = AdaSum(ph, chip, [(a["ada_w"][1], 0, 2 * D, mod_col(1, SH1))], slots=2, wide=D, tag="ada1")
        mod_done = ph.sem("mod_done")

        b_in, bias_ready, const_done = ph.sem("b_in"), ph.sem("bias_ready"), ph.sem("const_done")
        pool_step, dve_step, act_step = ph.sem("pool_step"), ph.sem("dve_step"), ph.sem("act_step")
        evac = ph.sem("evacuated")
        tanh_done, logf_done = ph.sem("tanh_done"), ph.sem("logf_done")
        em_done, cols_ps, cols_done = ph.sem("em_done"), ph.sem("cols_ps"), ph.sem("cols_done")
        em_arg, mean_done, root_done = ph.sem("em_arg"), ph.sem("mean_done"), ph.sem("root_done")
        row_ps, score_ps, arg_done, pw_done, sd_done = (
            ph.sem(n) for n in ("row_ps", "score_ps", "arg_done", "pw_done", "sd_done"))
        num_ps, num_done, y_done, turned, yT_done = (
            ph.sem(n) for n in ("num_ps", "num_done", "y_done", "turned", "yT_done"))
        block = ctx.enter_context(nc.Block())

        def unit_bank(u):
            return bank[(4 + u) % 8]

        @block.sync
        def _(eng):
            eng.dma_start(bi[:, :], a["a_b_i"].rearrange("o h -> h o")).then_inc(b_in, 16)
            eng.dma_start(bf[:, :], a["a_b_f"].rearrange("o h -> h o")).then_inc(b_in, 16)
            pj.load(eng)

        @block.gpsimd
        def _(eng):
            eng.memset(sel[:, :, :], 0.0).then_inc(pool_step, 1)
            eng.memset(tri[:, :], 0.0).then_inc(pool_step, 1)
            eng.memset(vx[:, :, :, ML_DV:ML_DV + 1], 1.0).then_inc(const_done, 1)
            eng.wait_ge(pool_step, 2)
            eng.affine_select(out=sel[:, :, :], in_=sel[:, :, :], compare_op=ALU.not_equal, fill=1.0, base=0,
                              pattern=[[-1, ML_H], [0, P]], channel_multiplier=1).then_inc(const_done, 1)
            eng.affine_select(out=tri[:, :], in_=tri[:, :], compare_op=ALU.is_ge, fill=NEG, base=0,
                              pattern=[[1, P]], channel_multiplier=-1).then_inc(const_done, 1)
            norm.pool(eng)
            ada.load(eng)
            ada1.load(eng, 0, 2)
            eng.wait_ge(mean_done, 1)
            rsqrt(eng, chip, rr[:, :, :].rearrange("p g h -> p (g h)"), [P, G * ML_H]).then_inc(root_done, 1)
            ada1.load(eng, 2)

        @block.tensor
        def _(eng):
            norm.pe(eng)
            eng.wait_ge(norm.done, DC)
            eng.wait_ge(pj.loaded[0], 16)
            for n in range(2):
                for c in range(DC):
                    mm = eng.matmul(unit_bank(0)[0:ML_H, n * T:(n + 1) * T],
                                    pj.slots[0][:, c, n * ML_H:(n + 1) * ML_H], norm.xnT[:, c, :],
                                    start=(c == 0), stop=(c == DC - 1))
            mm.then_inc(pj.done, 1)
            for u in range(U_Q, U_OUT):
                if u >= 8:
                    eng.wait_ge(evac, u - 8 + 1)
                pj.unit(eng, u, unit_bank(u), norm.xnT)
            eng.wait_ge(evac, U_OUT)
            eng.wait_ge(em_done, 1)
            for n, src in enumerate((ai, em)):
                for g in range(G):
                    at = (n * G + g) * ML_H
                    mm = eng.transpose(bank[4][:, at:at + ML_H], src[:, g * P:(g + 1) * P],
                                       chip.ident[0:ML_H, 0:ML_H])
            mm.then_inc(cols_ps, 1)
            eng.wait_ge(cols_done, 2)
            eng.wait_ge(const_done, 3)

            def scores(h):
                base = (h % 2) * 4
                if h >= 2:
                    eng.wait_ge(sd_done, h - 1)
                    eng.wait_ge(pw_done, h - 1)
                eng.matmul(bank[base][:, 0:T], sel[:, h, :], M[:, :], start=True, stop=True).then_inc(row_ps, 1)
                eng.matmul(bank[base + 1][:, 0:T], kT[:, h, 0:P], qT[:, h, :], start=True, stop=True)
                eng.matmul(bank[base + 1][:, T:T + P], kT[:, h, P:T], qT[:, h, P:T], start=True, stop=True
                           ).then_inc(score_ps, 1)

            def sums(h):
                base = (h % 2) * 4
                if h >= 2:
                    eng.wait_ge(num_done, G * (h - 1))
                eng.wait_ge(sd_done, h + 1)
                s = sd[h % 2]
                eng.matmul(bank[base + 2][:, 0:ML_DV + 1], s[:, 0, :], vx[:, 0, h, :], start=True, stop=True
                           ).then_inc(num_ps, 1)
                eng.matmul(bank[base + 3][:, 0:ML_DV + 1], s[:, 1, :], vx[:, 0, h, :], start=True, stop=False)
                eng.matmul(bank[base + 3][:, 0:ML_DV + 1], s[:, 2, :], vx[:, 1, h, :], start=False, stop=True
                           ).then_inc(num_ps, 1)

            for h in range(ML_H + 1):
                if h < ML_H:
                    scores(h)
                if h >= 1:
                    sums(h - 1)
            eng.wait_ge(num_done, G * ML_H)
            ada.pe(eng, bank[7])
            eng.wait_ge(y_done, G * ML_H)
            turn_to_features(eng, chip, y, turned)
            eng.wait_ge(yT_done, DC)
            for n in range(2 * G):
                if n == 3:
                    eng.wait_ge(mod_done, 1)
                pj.unit(eng, U_OUT + n, bank[4 + n], yT)
            res.pe(eng)
            ada1.pe(eng, bank[0])

        @block.scalar
        def _(eng):
            norm.act(eng)
            eng.wait_ge(bias_ready, 2)
            eng.wait_ge(pj.done, 1)
            eng.activation(ti[:, :], unit_bank(0)[0:ML_H, 0:T], ACT.Tanh, bias=bi[:, 0:1], scale=1.0 / CAP
                           ).then_inc(tanh_done, 1)
            eng.activation(tf[:, :], unit_bank(0)[0:ML_H, T:2 * T], ACT.Tanh, bias=bf[:, 0:1], scale=1.0 / CAP
                           ).then_inc(evac, 1)
            eng.wait_ge(evac, 1)
            eng.activation(soft[:, :], tf[:, :], ACT.Exp, scale=-CAP).then_inc(act_step, 1)
            eng.wait_ge(act_step, 1)
            eng.activation(soft[:, :], soft[:, :], ACT.Ln, bias=1.0).then_inc(logf_done, 1)
            for u in range(U_Q, U_OUT):
                eng.wait_ge(pj.done, u + 1)
                ps = unit_bank(u)
                if u < U_K:
                    i = 2 * (u - U_Q)
                    eng.activation(qT[:, i:i + 2, :], ps[:, :], ACT.Copy).then_inc(evac, 1)
                elif u < U_V:
                    i = 2 * (u - U_K)
                    eng.activation(kT[:, i:i + 2, :], ps[:, :], ACT.Copy).then_inc(evac, 1)
                elif u < U_O:
                    b, g = divmod(u - U_V, G)
                    eng.activation(vx[:, g, 2 * b:2 * b + 2, 0:ML_DV],
                                   ps[:, :].rearrange("p (h d) -> p h d", h=2), ACT.Copy).then_inc(evac, 1)
                else:
                    b, g = divmod(u - U_O, G)
                    eng.activation(so[:, g, b * WCOLS:(b + 1) * WCOLS], ps[:, :], ACT.Sigmoid).then_inc(evac, 1)
            eng.wait_ge(em_arg, 1)
            eng.activation(em[:, :], em[:, :], ACT.Exp, scale=-1.0).then_inc(em_done, 1)
            eng.wait_ge(cols_done, 2)

            def weights(h):
                k = h % 2
                if h >= 2:
                    eng.wait_ge(sd_done, h - 1)
                eng.wait_ge(arg_done, h + 1)
                eng.activation(pw[k][:, 0, :], arg[k][:, 0, :], ACT.Exp, bias=acol[:, 0, h:h + 1])
                eng.activation(pw[k][:, 1, :], bank[(h % 2) * 4][:, P:T], ACT.Exp, bias=acol[:, 0, h:h + 1],
                               scale=-1.0)
                eng.activation(pw[k][:, 2, :], arg[k][:, 1, :], ACT.Exp, bias=acol[:, 1, h:h + 1]
                               ).then_inc(pw_done, 1)

            def take(h):
                for g in range(G):
                    ps = bank[(h % 2) * 4 + 2 + g]
                    eng.wait_ge(num_ps, G * h + g + 1)
                    if h + g:
                        eng.wait_ge(num_done, G * h + g)
                    eng.activation(junk[:, :], ps[:, 0:ML_DV], ACT.Square, accum_out=ssq[:, g, h:h + 1])
                    eng.activation(num[:, g, h, :], ps[:, 0:ML_DV + 1], ACT.Copy).then_inc(num_done, 1)

            for h in range(ML_H + 1):
                if h < ML_H:
                    weights(h)
                if h >= 1:
                    take(h - 1)
            for c in range(DC):
                eng.wait_ge(turned, c // 2 + 1)
                at = (c % 2) * T
                eng.activation(yT[:, c, :], bank[c // 2][:, at:at + T], ACT.Copy,
                               scale=chip.gains[:, H_NORM + c:H_NORM + c + 1]).then_inc(yT_done, 1)
            res.act(eng)

        @block.vector
        def _(eng):
            n = Count()
            eng.wait_ge(b_in, 32)
            eng.tensor_scalar(bi[:, :], bi[:, :], 1.0 / CAP, None, ALU.mult).then_inc(bias_ready, 1)
            eng.tensor_scalar(bf[:, :], bf[:, :], 1.0 / CAP, None, ALU.mult).then_inc(bias_ready, 1)
            norm.dve(eng)
            eng.wait_ge(logf_done, 1)
            eng.tensor_tensor_scan(B[:, :], chip_ones(chip, ML_H), soft[:, :], 0.0, ALU.mult, ALU.subtract
                                   ).then_inc(dve_step, 1)
            eng.wait_ge(dve_step, n.up())
            eng.wait_ge(tanh_done, 1)
            eng.scalar_tensor_tensor(out=ai[:, :], in0=ti[:, :], scalar=CAP, in1=B[:, :], op0=ALU.mult,
                                     op1=ALU.subtract).then_inc(dve_step, 1)
            eng.wait_ge(dve_step, n.up())
            eng.tensor_tensor_scan(M[:, :], chip_ones(chip, ML_H), ai[:, :], 0.0, ALU.mult, ALU.max
                                   ).then_inc(dve_step, 1)
            eng.wait_ge(dve_step, n.up())
            eng.tensor_tensor(em[:, :], B[:, :], M[:, :], ALU.add).then_inc(em_arg, 1)
            ada.dve(eng)
            eng.wait_ge(cols_ps, 1)
            eng.tensor_copy(acol[:, :, :], bank[4][:, 0:G * ML_H]).then_inc(cols_done, 1)
            eng.tensor_copy(ecol[:, :, :], bank[4][:, G * ML_H:2 * G * ML_H]).then_inc(cols_done, 1)

            def args(h):
                k = h % 2
                if h >= 2:
                    eng.wait_ge(pw_done, h - 1)
                eng.wait_ge(row_ps, h + 1)
                eng.tensor_tensor(arg[k][:, :, :], tri[:, :].unsqueeze(1).to_broadcast([P, G, P]),
                                  bank[k * 4][:, 0:T].rearrange("p (g t) -> p g t", g=G), ALU.subtract
                                  ).then_inc(arg_done, 1)

            def weigh(h):
                k = h % 2
                if h >= 2:
                    eng.wait_ge(num_ps, G * (h - 1))
                eng.wait_ge(score_ps, h + 1)
                eng.wait_ge(pw_done, h + 1)
                eng.scalar_tensor_tensor(out=sd[k][:, :, :], in0=bank[k * 4 + 1][:, 0:3 * P].rearrange("p (a t) -> p a t", a=3),
                                         scalar=ML_DK ** -0.5, in1=pw[k][:, :, :], op0=ALU.mult, op1=ALU.mult
                                         ).then_inc(sd_done, 1)

            for h in range(ML_H + 1):
                if h < ML_H:
                    args(h)
                if h >= 1:
                    weigh(h - 1)
            eng.wait_ge(num_done, G * ML_H)
            d = num[:, :, :, ML_DV:ML_DV + 1].rearrange("p g h o -> p g (h o)")
            eng.scalar_tensor_tensor(out=den[:, :, :], in0=d, scalar=-1.0, in1=d, op0=ALU.mult,
                                     op1=ALU.max).then_inc(dve_step, 1)
            eng.wait_ge(dve_step, n.up())
            eng.tensor_tensor(den[:, :, :], den[:, :, :], ecol[:, :, :], ALU.max).then_inc(dve_step, 1)
            eng.wait_ge(dve_step, n.up())
            eng.reciprocal(den[:, :, :], den[:, :, :]).then_inc(dve_step, 1)
            eng.wait_ge(dve_step, n.up())
            eng.tensor_tensor(rr[:, :, :], ssq[:, :, :], den[:, :, :], ALU.mult).then_inc(dve_step, 1)
            eng.wait_ge(dve_step, n.up())
            eng.tensor_tensor(rr[:, :, :], rr[:, :, :], den[:, :, :], ALU.mult).then_inc(dve_step, 1)
            eng.wait_ge(dve_step, n.up())
            eng.tensor_scalar(rr[:, :, :], rr[:, :, :], 1.0 / ML_DV, EPS, ALU.mult, ALU.add).then_inc(mean_done, 1)
            eng.wait_ge(root_done, 1)
            eng.tensor_tensor(rr[:, :, :], rr[:, :, :], den[:, :, :], ALU.mult).then_inc(dve_step, 1)
            eng.wait_ge(dve_step, n.up())
            for g in range(G):
                for h in range(ML_H):
                    cols = slice(h * ML_DV, (h + 1) * ML_DV)
                    eng.scalar_tensor_tensor(out=y[:, g, cols], in0=num[:, g, h, 0:ML_DV], scalar=rr[:, g, h:h + 1],
                                             in1=so[:, g, cols], op0=ALU.mult, op1=ALU.mult).then_inc(y_done, 1)
            ada1.dve(eng, 0, 8)
            ada.dve_finish(eng, bank[7], mod_done)
            eng.wait_ge(mod_done, 1)
            res.dve_diag(eng)
            ada1.dve(eng, 8)
            res.dve_add(eng, [(lambda n=n: eng.wait_ge(pj.done, U_OUT + n + 1), bank[4 + n][:, :], n % G, 1,
                               n // G * WCOLS, WCOLS) for n in range(2 * G)])
            ada1.dve_finish(eng, bank[0], mod_done)
            eng.wait_ge(mod_done, 2)


def chip_ones(chip, rows):
    return chip.ones[0:rows, 0:1].to_broadcast([rows, T])



def fox(nc, chip, a):
    with ExitStack() as ctx:
        ph = Phase(nc, ctx, "fx")
        bank = chip.bank
        xhl = ph.sb("xhl", [P, DC, 2, T], F32R)
        norm_kv = Norm(ph, chip, KV_SH, KV_SC, KV_NORM, "kv", xhl=xhl)
        norm_q = Norm(ph, chip, mod_col(1, SH1), mod_col(1, SC1), MIX_NORM + DC, "q", xhl=xhl, like=norm_kv)
        wk, wq = a["kv_w"], a["b_w_qo"][0]
        wf = ph.sb("wf", [P, DC, FX_H])
        blocks = [(wk, 0, True), (wk, WCOLS, True), (wk, D, False), (wk, D + WCOLS, False),
                  (wq, 0, True), (wq, WCOLS, True), (wq, D, False), (wq, D + WCOLS, False),
                  (a["b_w_out"][0], 0, False), (a["b_w_out"][0], WCOLS, False)]
        pj = SplitProject(ph, blocks)
        U_K, U_V, U_Q, U_O, U_OUT = 0, 4, 8, 12, 16
        ada = AdaSum(ph, chip, [(a["ada_w"][1], 2 * D, 3 * D, mod_col(1, G1))], slots=2, wide=D)
        kT = ph.sb("kT", [P, FX_H, T])
        qT = ph.sb("qT", [P, FX_H, T])
        v = ph.sb("v", [P, G, D])
        so = ph.sb("so", [P, G, D])
        y = norm_kv.xs
        yT = norm_kv.xnT
        bf = ph.sb("bf", [FX_H, 1])
        az, lf, mn = (ph.sb(n, [FX_H, T]) for n in ("az", "lf", "mn"))
        F3 = ph.sb("F3", [FX_H, 3, P])
        F = ph.sb("F", [FX_H, T])
        Fcol = ph.sb("Fcol", [P, G, FX_H])
        sel = ph.sb("sel", [FX_H, FX_H, P])
        mask = ph.sb("mask", [P, 3, P])
        with ExitStack() as projections:
            pr_sb = lambda name, shape: projections.enter_context(nc.sbuf_tensor(f"fx_{name}", shape, F32))
            sq = [pr_sb(f"sq{k}", [P, 4, P]) for k in range(2)]
            rdiag = [pr_sb(f"rdiag{k}", [P, 4, P]) for k in range(2)]
            rb = [pr_sb(f"rb{k}", [P, 512]) for k in range(2)]
        bias = [ph.sb(f"bias{k}", [P, 3, P]) for k in range(2)]
        lg = [ph.sb(f"lg{k}", [P, 3 * P]) for k in range(2)]
        pr = [ph.sb(f"pr{k}", [P, 3 * P]) for k in range(2)]
        pT = [ph.sb(f"pT{k}", [P, 3 * P]) for k in range(2)]
        rcol = [ph.sb(f"rcol{k}", [P, 4]) for k in range(2)]
        nmax = ph.sb("nmax", [P, FX_H, G])
        rsum = ph.sb("rsum", [P, FX_H, G])
        res = Residual(ph, chip, mod_col(1, G1), [bank[2], bank[3]], diag=so[:, 0, :], row=so[:, 1, :])

        f_ps, mod_done = ph.sem("f_ps"), ph.sem("mod_done")
        yT_hi, yT_lo = ph.sem("yT_hi"), ph.sem("yT_lo")
        b_in, const_done, pool_step, dve_step, act_step = (
            ph.sem(n) for n in ("b_in", "const_done", "pool_step", "dve_step", "act_step"))
        evac, sq_done, ss_ps, logf_done, gate_read = (
            ph.sem(n) for n in ("evacuated", "sq_done", "ss_ps", "logf_done", "gate_read"))
        mean_done, root_done = ph.sem("mean_done"), ph.sem("root_done")
        rdiag_done, spread, rb_done = ph.sem("rdiag_done"), ph.sem("rms_spread"), ph.sem("rb_done")
        F_done, cols_ps, cols_done = ph.sem("F_done"), ph.sem("cols_ps"), ph.sem("cols_done")
        dve_evac = ph.sem("dve_evac")
        row_ps, bias_done, score_ps, lg_done, max_done, pr_done, pT_ps, pT_done, att_ps, y_done = (
            ph.sem(n) for n in ("row_ps", "bias_done", "score_ps", "lg_done", "max_done", "pr_done",
                                "pT_ps", "pT_done", "att_ps", "y_done"))
        turned, yT_done = ph.sem("turned"), ph.sem("yT_done")
        block = ctx.enter_context(nc.Block())

        head_units = list(range(U_K, U_V)) + list(range(U_Q, U_O))
        plain_units = list(range(U_V, U_Q)) + list(range(U_O, U_OUT))

        def unit_bank(u):
            return bank[(4, 5, 6, 1, 2, 0)[u % 6]]

        def wait_left(eng, u):
            if u == 5:
                eng.wait_ge(gate_read, 1)
            if u - 6 in head_units:
                eng.wait_ge(dve_evac, head_units.index(u - 6) + 1)
            elif u >= 6:
                eng.wait_ge(evac, plain_units.index(u - 6) + 1)

        @block.sync
        def _(eng):
            pj.load(eng, 0, 1)
            eng.dma_start(bf[:, :], a["kv_b_f"].rearrange("(h o) -> h o", o=1)).then_inc(b_in, 16)
            eng.dma_start(wf[:, :, :], wk.rearrange("(c p) n -> p c n", p=P)[:, :, 2 * D:2 * D + FX_H]
                          ).then_inc(b_in, 16)
            pj.load(eng, 1, 3)
            for b in range(4, len(blocks)):
                pj.load(eng, b, 1)
                ada.load(eng, 4 * (b - 4), 4)

        @block.gpsimd
        def _(eng):
            eng.memset(sel[:, :, :], 0.0).then_inc(pool_step, 1)
            eng.memset(mask[:, :, :], 0.0).then_inc(pool_step, 1)
            eng.wait_ge(pool_step, 2)
            eng.affine_select(out=sel[:, :, :], in_=sel[:, :, :], compare_op=ALU.not_equal, fill=1.0, base=0,
                              pattern=[[-1, FX_H], [0, P]], channel_multiplier=1).then_inc(const_done, 1)
            for n in (0, 2):
                eng.affine_select(out=mask[:, n, :], in_=mask[:, n, :], compare_op=ALU.is_ge, fill=-NEG, base=0,
                                  pattern=[[-1, P]], channel_multiplier=1).then_inc(const_done, 1)

            def root(i):
                eng.wait_ge(mean_done, i + 1)
                rsqrt(eng, chip, rcol[i % 2][:, :], [P, 4]).then_inc(root_done, 1)

            norm_kv.pool(eng)
            for i in range(len(head_units)):
                root(i)

        @block.tensor
        def _(eng):
            norm_kv.pe(eng)
            eng.wait_ge(norm_kv.done, DC)
            eng.wait_ge(b_in, 32)
            for c in range(DC):
                mm = eng.matmul(bank[0][0:FX_H, 0:T], wf[:, c, :], norm_kv.xnT[:, c, :],
                                start=(c == 0), stop=(c == DC - 1))
            mm.then_inc(f_ps, 1)
            eng.wait_ge(norm_kv.lo, 2)

            def squares(u):
                i = head_units.index(u)
                eng.wait_ge(sq_done, i + 1)
                if i >= 1:
                    eng.wait_ge(mean_done, i)
                for n in range(4):
                    mm = eng.matmul(bank[3][:, n:n + 1], sq[i % 2][:, n, :], chip.ones[:, 0:1], start=True, stop=True)
                mm.then_inc(ss_ps, 1)

            def spread_rms(u):
                i = head_units.index(u)
                eng.wait_ge(rdiag_done, 4 * (i + 1))
                if i >= 1:
                    eng.wait_ge(rb_done, i)
                eng.matmul(bank[7][:, :], chip.ones[:, :], rdiag[i % 2][:, :, :], start=True, stop=True
                           ).then_inc(spread, 1)

            def rms_behind(u):
                if u - 1 in head_units:
                    squares(u - 1)
                if u - 2 in head_units:
                    spread_rms(u - 2)

            for u in range(U_K, U_Q):
                wait_left(eng, u)
                pj.pe(eng, u, unit_bank(u), xhl)
                rms_behind(u)
            eng.wait_ge(dve_evac, U_V - U_K)
            eng.wait_ge(evac, U_Q - U_V)
            norm_q.pe(eng)
            eng.wait_ge(norm_q.lo, 2)
            for u in range(U_Q, U_OUT):
                wait_left(eng, u)
                pj.pe(eng, u, unit_bank(u), xhl)
                rms_behind(u)
            eng.wait_ge(F_done, 1)
            eng.wait_ge(evac, len(plain_units))
            eng.wait_ge(dve_evac, len(head_units))
            for g in range(G):
                mm = eng.transpose(bank[0][:, g * FX_H:(g + 1) * FX_H], F[:, g * P:(g + 1) * P],
                                   chip.ident[0:FX_H, 0:FX_H])
            mm.then_inc(cols_ps, 1)
            eng.wait_ge(cols_done, 1)
            eng.wait_ge(const_done, 3)

            def scores(h):
                base = (h % 2) * 4
                if h >= 2:
                    eng.wait_ge(lg_done, h - 1)
                eng.matmul(bank[base][:, 0:3 * P], sel[:, h, :], F3[:, :, :], start=True, stop=True
                           ).then_inc(row_ps, 1)
                eng.matmul(bank[base + 1][:, 0:P], qT[:, h, 0:P], kT[:, h, 0:P], start=True, stop=True)
                eng.matmul(bank[base + 1][:, P:3 * P], qT[:, h, P:T], kT[:, h, :], start=True, stop=True
                           ).then_inc(score_ps, 1)

            def turn(h):
                base = (h % 2) * 4
                eng.wait_ge(pr_done, G * (h + 1))
                if h >= 2:
                    eng.wait_ge(pT_done, h - 1)
                for n in range(3):
                    mm = eng.transpose(bank[base + 2][:, n * P:(n + 1) * P], pr[h % 2][:, n * P:(n + 1) * P],
                                       chip.ident[:, :])
                mm.then_inc(pT_ps, 1)

            def attend(h):
                base = (h % 2) * 4
                cols = slice(h * FX_D, (h + 1) * FX_D)
                eng.wait_ge(pT_done, h + 1)
                if h >= 2:
                    eng.wait_ge(y_done, G * (h - 1))
                p = pT[h % 2]
                eng.matmul(bank[base + 3][:, 0:FX_D], p[:, 0:P], v[:, 0, cols], start=True, stop=True)
                eng.matmul(bank[base + 3][:, FX_D:2 * FX_D], p[:, P:2 * P], v[:, 0, cols], start=True, stop=False)
                eng.matmul(bank[base + 3][:, FX_D:2 * FX_D], p[:, 2 * P:3 * P], v[:, 1, cols], start=False,
                           stop=True).then_inc(att_ps, 1)

            for h in range(FX_H + 2):
                if h < FX_H:
                    scores(h)
                if 1 <= h <= FX_H:
                    turn(h - 1)
                if h >= 2:
                    attend(h - 2)
            eng.wait_ge(y_done, G * FX_H)
            turn_to_features(eng, chip, y, turned)
            ada.pe(eng, bank[7])
            eng.wait_ge(yT_lo, 2)
            for n in range(4):
                if n == 3:
                    eng.wait_ge(mod_done, 1)
                pj.pe(eng, U_OUT + n, bank[4 + n], xhl)
            res.pe(eng)

        @block.scalar
        def _(eng):
            norm_kv.act(eng)
            pj.act(eng, 0)
            pj.act(eng, 1)
            norm_kv.act_hi(eng)
            eng.wait_ge(f_ps, 1)
            eng.wait_ge(b_in, 32)
            eng.activation(az[:, :], bank[0][0:FX_H, 0:T], ACT.Abs, bias=bf[:, 0:1]).then_inc(act_step, 1)
            eng.wait_ge(act_step, 1)
            eng.activation(az[:, :], az[:, :], ACT.Exp, scale=-1.0).then_inc(act_step, 1)
            eng.wait_ge(act_step, 2)
            eng.activation(az[:, :], az[:, :], ACT.Ln, bias=1.0).then_inc(logf_done, 1)
            for u in range(U_K, U_OUT):
                if u == U_Q:
                    norm_q.act_hi(eng)
                pj.act(eng, u + 2)
                eng.wait_ge(pj.done, u + 1)
                ps = unit_bank(u)
                if u in head_units:
                    i = head_units.index(u)
                    if i >= 2:
                        eng.wait_ge(ss_ps, i - 1)
                    eng.activation(sq[i % 2][:, :, :], ps[:, :], ACT.Square).then_inc(sq_done, 1)
                elif u < U_Q:
                    cols = slice((u - U_V) * T, (u - U_V + 1) * T)
                    eng.activation(v[:, :, cols], ps[:, :].rearrange("p (g d) -> p g d", g=G), ACT.Copy
                                   ).then_inc(evac, 1)
                else:
                    cols = slice((u - U_O) * T, (u - U_O + 1) * T)
                    eng.activation(so[:, :, cols], ps[:, :].rearrange("p (g d) -> p g d", g=G), ACT.Sigmoid
                                   ).then_inc(evac, 1)
                if u - 2 in head_units:
                    i = head_units.index(u - 2)
                    eng.wait_ge(spread, i + 1)
                    if i >= 2:
                        eng.wait_ge(dve_evac, i - 1)
                    eng.activation(rb[i % 2][:, :], bank[7][:, :], ACT.Copy).then_inc(rb_done, 1)

            def soft(h):
                k = h % 2
                eng.wait_ge(max_done, G * (h + 1))
                if h >= 2:
                    eng.wait_ge(pT_ps, h - 1)
                eng.activation(pr[k][:, 0:P], lg[k][:, 0:P], ACT.Exp, bias=nmax[:, h, 0:1],
                               accum_out=rsum[:, h, 0:1]).then_inc(pr_done, 1)
                eng.activation(pr[k][:, P:3 * P], lg[k][:, P:3 * P], ACT.Exp, bias=nmax[:, h, 1:2],
                               accum_out=rsum[:, h, 1:2]).then_inc(pr_done, 1)

            def take(h):
                k = h % 2
                eng.wait_ge(pT_ps, h + 1)
                if h >= 2:
                    eng.wait_ge(att_ps, h - 1)
                eng.activation(pT[k][:, :], bank[k * 4 + 2][:, 0:3 * P], ACT.Copy).then_inc(pT_done, 1)

            for h in range(FX_H + 1):
                if h < FX_H:
                    soft(h)
                if h >= 1:
                    take(h - 1)
            for c in range(DC):
                eng.wait_ge(turned, c // 2 + 1)
                at = (c % 2) * T
                eng.activation(yT[:, c, :], bank[c // 2][:, at:at + T], ACT.Copy).then_inc(yT_done, 1)
            split_hi(eng, yT, xhl, yT_done, yT_hi)
            pj.act(eng, U_OUT + 2)
            pj.act(eng, U_OUT + 3)
            res.act(eng)

        @block.vector
        def _(eng):
            n = Count()
            norm_kv.dve(eng)
            norm_kv.dve_lo(eng)
            pj.dve(eng, 0)
            pj.dve(eng, 1)
            eng.wait_ge(act_step, 1)
            eng.tensor_scalar(mn[:, :], bank[0][0:FX_H, 0:T], bf[:, 0:1], 0.0, ALU.add, ALU.min
                              ).then_inc(gate_read, 1)
            eng.wait_ge(gate_read, 1)
            eng.wait_ge(logf_done, 1)
            eng.tensor_tensor(lf[:, :], mn[:, :], az[:, :], ALU.subtract).then_inc(dve_step, 1)
            eng.wait_ge(dve_step, n.up())
            eng.tensor_tensor_scan(F[:, :], chip_ones(chip, FX_H), lf[:, :], 0.0, ALU.mult, ALU.add
                                   ).then_inc(dve_step, 1)
            eng.wait_ge(dve_step, n.up())
            eng.tensor_copy(F3[:, 0, :], F[:, 0:P])
            eng.tensor_copy(F3[:, 1:3, :], F[:, :].rearrange("h (g t) -> h g t", g=G)).then_inc(F_done, 1)

            def rms_diag(i):
                k = i % 2
                eng.wait_ge(ss_ps, i + 1)
                eng.tensor_scalar(rcol[k][:, :], bank[3][:, 0:4], 1.0 / FX_D, EPS, ALU.mult, ALU.add
                                  ).then_inc(mean_done, 1)
                eng.wait_ge(root_done, i + 1)
                if i >= 2:
                    eng.wait_ge(spread, i - 1)
                for m in range(4):
                    eng.tensor_scalar(rdiag[k][:, m, :], chip.ident[:, :], rcol[k][:, m:m + 1], None, ALU.mult
                                      ).then_inc(rdiag_done, 1)

            def normalise(i):
                u = head_units[i]
                gain, dst, at = (K_NORM, kT, 2 * (u - U_K)) if u < U_V else (Q_NORM, qT, 2 * (u - U_Q))
                eng.wait_ge(rb_done, i + 1)
                eng.scalar_tensor_tensor(out=dst[:, at:at + 2, :],
                                         in0=unit_bank(u)[:, :].rearrange("p (h t) -> p h t", h=2),
                                         scalar=chip.gains[:, gain:gain + 1],
                                         in1=rb[i % 2][:, :].rearrange("p (h t) -> p h t", h=2),
                                         op0=ALU.mult, op1=ALU.mult).then_inc(dve_evac, 1)

            for u in range(U_K, U_OUT):
                if u == U_Q:
                    norm_q.dve(eng)
                    norm_q.dve_lo(eng)
                pj.dve(eng, u + 2)
                if u - 1 in head_units:
                    rms_diag(head_units.index(u - 1))
                if u - 2 in head_units:
                    normalise(head_units.index(u - 2))
                if u >= U_V:
                    ada.dve(eng, 2 * (u - U_V), 2)
            eng.wait_ge(cols_ps, 1)
            eng.tensor_copy(Fcol[:, :, :], bank[0][:, 0:G * FX_H]).then_inc(cols_done, 1)
            eng.wait_ge(cols_done, 1)

            def logits(h):
                k = h % 2
                ps, sc = bank[k * 4], bank[k * 4 + 1]
                eng.wait_ge(row_ps, h + 1)
                eng.scalar_tensor_tensor(out=bias[k][:, 0, :], in0=ps[:, 0:P], scalar=Fcol[:, 0, h:h + 1],
                                         in1=mask[:, 0, :], op0=ALU.subtract, op1=ALU.add).then_inc(bias_done, 1)
                eng.scalar_tensor_tensor(out=bias[k][:, 1:3, :], in0=ps[:, P:3 * P].rearrange("p (a s) -> p a s", a=2),
                                         scalar=Fcol[:, 1, h:h + 1], in1=mask[:, 1:3, :],
                                         op0=ALU.subtract, op1=ALU.add).then_inc(bias_done, 1)
                eng.wait_ge(bias_done, 2 * (h + 1))
                eng.wait_ge(score_ps, h + 1)
                if h >= 2:
                    eng.wait_ge(pr_done, G * (h - 1))
                eng.scalar_tensor_tensor(out=lg[k][:, :], in0=sc[:, 0:3 * P], scalar=FX_D ** -0.5,
                                         in1=bias[k][:, :, :].rearrange("p a s -> p (a s)"),
                                         op0=ALU.mult, op1=ALU.subtract).then_inc(lg_done, 1)
                eng.wait_ge(lg_done, h + 1)
                eng.tensor_reduce(nmax[:, h, 0:1], lg[k][:, 0:P], AX.X, ALU.max, negate=True).then_inc(max_done, 1)
                eng.tensor_reduce(nmax[:, h, 1:2], lg[k][:, P:3 * P], AX.X, ALU.max, negate=True
                                  ).then_inc(max_done, 1)

            def gate(h):
                k = h % 2
                cols = slice(h * FX_D, (h + 1) * FX_D)
                eng.wait_ge(att_ps, h + 1)
                eng.reciprocal(rsum[:, h, :], rsum[:, h, :]).then_inc(dve_step, 1)
                eng.wait_ge(dve_step, n.up())
                for g in range(G):
                    eng.scalar_tensor_tensor(out=y[:, g, cols], in0=bank[k * 4 + 3][:, g * FX_D:(g + 1) * FX_D],
                                             scalar=rsum[:, h, g:g + 1], in1=so[:, g, cols],
                                             op0=ALU.mult, op1=ALU.mult).then_inc(y_done, 1)

            for h in range(FX_H + 2):
                if h < FX_H:
                    logits(h)
                if h >= 2:
                    gate(h - 2)

            split_lo(eng, yT, xhl, yT_hi, yT_lo)
            ada.dve_finish(eng, bank[7], mod_done)
            eng.wait_ge(mod_done, 1)
            eng.wait_ge(y_done, G * FX_H)
            res.dve_diag(eng)
            pj.dve(eng, U_OUT + 2)
            pj.dve(eng, U_OUT + 3)
            res.dve_add(eng, [(lambda n=n: eng.wait_ge(pj.done, U_OUT + n + 1), bank[4 + n][:, :], 0, G, n * T, T)
                              for n in range(4)])



class PeerState:

    def __init__(self, ph):
        self.xhl = ph.sb("xhl", [P, DC, 2, T], F32R)
        self.i = ph.sb("i", [P, G, SEL], F32R)
        self.jT = ph.sb("jT", [SEL, T])
        self.gT = ph.sb("gT", [SEL, T])


def peer_route(nc, chip, a, layer, st):
    with ExitStack() as ctx:
        ph = Phase(nc, ctx, f"rt{layer}")
        bank = chip.bank
        norm = Norm(ph, chip, mod_col(layer, SH2), mod_col(layer, SC2), FFN_NORM + layer * DC)
        blocks = [(a["peer_wq"][layer], n * WCOLS, WCOLS, True) for n in range(4)]
        VEC = 8
        vec_w, vec_from, vec_cols, vec_to = ((a["kv_ada_w"], 0, 2 * D, KV_SH),
                                             (a["ada_w"][1], G2 * D, D, mod_col(1, G2)))[layer]
        blocks += [(vec_w, vec_from + n * WCOLS, WCOLS, VECTOR) for n in range(vec_cols // WCOLS)]
        pj = Project(ph, blocks)
        vectors = len(pj.units) - VEC
        sk = ph.sb("sk", [PR_KEYS, 2, P])
        skT = ph.sb("skT", [P, 2, PR_KEYS])
        qT = [ph.sb(f"qT{k}", [P, 2, T]) for k in range(3)]
        sc = ph.sb("sc", [P, G, PR_ROWS, PR_KEYS])
        left = ph.sb("left", [P, 4, T])
        top = ph.sb("top", [P, G, PR_ROWS, PR_K])
        topi = ph.sb("topi", [P, G, PR_ROWS, PR_K], U32)
        topf = ph.sb("topf", [P, G, PR_ROWS, PR_K])
        cand = ph.sb("cand", [P, G, 2, PR_K, PR_K])
        eq = ph.sb("eq", [P, G, 2, 2, PR_K, PR_K])
        best = ph.sb("best", [P, G, PR_H, PR_K])
        pos = ph.sb("pos", [P, G, PR_H, PR_K], U32)
        posk = ph.sb("posk", [P, 2, G, 2, PR_K], U32)
        posf = ph.sb("posf", [P, 2, G, 2, PR_K])
        key = ph.sb("key", [P, G, 2, SEL])
        gate = ph.sb("gate", [P, G, SEL])
        gsum = ph.sb("gsum", [P, G, PR_H])
        row = ph.sb("row", [1, vec_cols])

        row_done, vec_ps = ph.sem("row_done"), ph.sem("vec_ps")
        sk_in, sk_ps, sk_done = ph.sem("sk_in"), ph.sem("sk_ps"), ph.sem("sk_done")
        hi_done, lo_done, dve_step = ph.sem("hi_done"), ph.sem("lo_done"), ph.sem("dve_step")
        eq_done, key_done = ph.sem("eq_done"), ph.sem("key_done")
        q_done, sc_ps, sc_done = ph.sem("q_done"), ph.sem("sc_ps"), ph.sem("sc_done")
        diff_done, exp_done, sel_done, turned, taken = (
            ph.sem(n) for n in ("diff_done", "exp_done", "sel_done", "turned", "taken"))
        block = ctx.enter_context(nc.Block())

        @block.sync
        def _(eng):
            eng.dma_start(sk[:, :, :], a["peer_subkeys"][layer].rearrange("h k d -> k h d")).then_inc(sk_in, 16)
            pj.load(eng)

        @block.gpsimd
        def _(eng):
            norm.pool(eng)
            eng.wait_ge(hi_done, 1)
            eng.tensor_tensor(st.xhl[:, :, 1, :], norm.xnT[:, :, :], st.xhl[:, :, 0, :].bitcast(F32), ALU.subtract
                              ).then_inc(lo_done, 1)
            for b in range(4):
                for g in range(G):
                    for half in range(2):
                        eng.wait_ge(eq_done, 4 * b + 2 * g + half + 1)
                        cell = eq[:, g, half, :, :, :]
                        keys = topf[:, g, 4 * b:4 * b + 4, :].rearrange("p (h two) k -> p h two k", two=2)[:, :, half, :]
                        eng.tensor_tensor(cell, cell, keys.unsqueeze(2).to_broadcast([P, 2, PR_K, PR_K]), ALU.mult
                                          ).then_inc(key_done, 1)
            eng.wait_ge(lo_done, 1)

        @block.tensor
        def _(eng):
            eng.wait_ge(sk_in, 16)
            for n in range(2):
                mm = eng.transpose(bank[4][:, n * P:(n + 1) * P], sk[:, n, :], chip.ident[:, :])
            mm.then_inc(sk_ps, 1)
            norm.pe(eng)
            eng.wait_ge(norm.done, DC)
            eng.wait_ge(sk_done, 1)

            def queries(u):
                if u >= 4:
                    eng.wait_ge(q_done, u - 3)
                pj.unit(eng, u, bank[4 + u % 4], norm.xnT)

            def scores(u):
                eng.wait_ge(q_done, u + 1)
                if u >= 4:
                    eng.wait_ge(sc_done, u - 3)
                for g in range(G):
                    for half in range(2):
                        at = (2 * g + half) * P
                        mm = eng.matmul(bank[u % 4][:, at:at + P], qT[u % 3][:, half, g * P:(g + 1) * P],
                                        skT[:, half, :], start=True, stop=True)
                mm.then_inc(sc_ps, 1)

            for u in range(PR_H + 1):
                if u < PR_H:
                    queries(u)
                if u >= 1:
                    scores(u - 1)
            eng.wait_ge(sc_done, PR_H)
            for u in range(vectors):
                if u >= 2:
                    eng.wait_ge(row_done, u - 1)
                pj.unit(eng, VEC + u, bank[4 + u % 2], chip.cs)
            eng.wait_ge(row_done, vectors)
            for j in range(vec_cols // P):
                mm = eng.matmul(bank[6][:, j:j + 1], row[0:1, j * P:(j + 1) * P], chip.ones[0:1, 0:1],
                                start=True, stop=True)
            mm.then_inc(vec_ps, 1)
            eng.wait_ge(sel_done, 1)
            for g in range(G):
                for n, src in enumerate((key[:, g, 1, :], gate[:, g, :])):
                    mm = eng.transpose(bank[g][:, n * P:(n + 1) * P], src, chip.ident[:, :])
                mm.then_inc(turned, 1)

        @block.scalar
        def _(eng):
            norm.act(eng)
            eng.wait_ge(sk_ps, 1)
            eng.activation(skT[:, :, :], bank[4][:, 0:2 * P], ACT.Copy).then_inc(sk_done, 1)
            eng.wait_ge(norm.done, DC)
            eng.activation(st.xhl[:, :, 0, :], norm.xnT[:, :, :], ACT.Copy).then_inc(hi_done, 1)

            def take_q(u):
                eng.wait_ge(pj.done, u + 1)
                if u >= 3:
                    eng.wait_ge(sc_ps, u - 2)
                eng.activation(qT[u % 3][:, :, :], bank[4 + u % 4][:, :], ACT.Copy).then_inc(q_done, 1)

            def take_s(u):
                eng.wait_ge(sc_ps, u + 1)
                eng.activation(sc[:, :, 2 * u:2 * u + 2, :], bank[u % 4][:, :].rearrange("p (g r k) -> p g r k", g=G, r=2),
                               ACT.Copy).then_inc(sc_done, 1)

            for u in range(PR_H + 1):
                if u < PR_H:
                    take_q(u)
                if u >= 1:
                    take_s(u - 1)
            for u in range(vectors):
                eng.wait_ge(pj.done, VEC + u + 1)
                eng.activation(row[0:1, u * WCOLS:(u + 1) * WCOLS], bank[4 + u % 2][0:1, :], ACT.Copy
                               ).then_inc(row_done, 1)
            for b in range(4):
                eng.wait_ge(diff_done, b + 1)
                cell = gate[:, :, 2 * b * PR_K:2 * (b + 1) * PR_K]
                eng.activation(cell, cell, ACT.Exp).then_inc(exp_done, 1)
            for g in range(G):
                eng.wait_ge(turned, g + 1)
                for n, dst in enumerate((st.jT, st.gT)):
                    eng.activation(dst[:, g * P:(g + 1) * P], bank[g][:, n * P:(n + 1) * P], ACT.Copy
                                   ).then_inc(taken, 1)
                eng.activation(st.i[:, g, :], key[:, g, 0, :], ACT.Copy).then_inc(taken, 1)
            eng.wait_ge(taken, 3 * G)


        @block.vector
        def _(eng):
            n = Count()
            norm.dve(eng)

            def top16(rows):
                for values, out, _, _ in rows:
                    eng.max(out[..., 0:8], values).then_inc(dve_step, 1)
                    n.up()
                first = n.n - len(rows)
                for k, (values, out, index, spare) in enumerate(rows):
                    eng.wait_ge(dve_step, first + k + 1)
                    eng.max_index(index[..., 0:8], out[..., 0:8], values)
                    eng.match_replace(spare, out[..., 0:8], values, LOWEST).then_inc(dve_step, 1)
                    n.up()
                for k, (_, out, _, spare) in enumerate(rows):
                    eng.wait_ge(dve_step, first + len(rows) + k + 1)
                    eng.max(out[..., 8:16], spare).then_inc(dve_step, 1)
                    n.up()
                for k, (_, out, index, spare) in enumerate(rows):
                    eng.wait_ge(dve_step, first + 2 * len(rows) + k + 1)
                    eng.max_index(index[..., 8:16], out[..., 8:16], spare).then_inc(dve_step, 1)
                    n.up()

            def best_keys(b):
                for u in (2 * b, 2 * b + 1):
                    eng.wait_ge(sc_done, u + 1)
                    top16([(sc[:, g, r, :], top[:, g, r, :], topi[:, g, r, :], left[:, 2 * g + r % 2, 0:PR_KEYS])
                           for g in range(G) for r in (2 * u, 2 * u + 1)])
                eng.wait_ge(dve_step, n.n)
                rows = slice(4 * b, 4 * b + 4)
                eng.tensor_copy(topf[:, :, rows, :], topi[:, :, rows, :]).then_inc(dve_step, 1)
                n.up()

            def best_pairs(b):
                for g in range(G):
                    pair = top[:, g, 4 * b:4 * b + 4, :].rearrange("p (h two) k -> p h two k", two=2)
                    eng.tensor_tensor(cand[:, g, :, :, :],
                                      pair[:, :, 0, :].unsqueeze(3).to_broadcast([P, 2, PR_K, PR_K]),
                                      pair[:, :, 1, :].unsqueeze(2).to_broadcast([P, 2, PR_K, PR_K]), ALU.add
                                      ).then_inc(dve_step, 1)
                    n.up()
                eng.wait_ge(dve_step, n.n)
                top16([(cand[:, g, h, :, :].rearrange("p a b -> p (a b)"), best[:, g, 2 * b + h, :],
                        pos[:, g, 2 * b + h, :], left[:, 2 * g + h, :]) for g in range(G) for h in range(2)])
                eng.wait_ge(dve_step, n.n)
                heads = slice(2 * b, 2 * b + 2)
                eng.tensor_tensor(gate[:, :, 2 * b * PR_K:2 * (b + 1) * PR_K].rearrange("p g (h k) -> p g h k", h=2),
                                  best[:, :, heads, :],
                                  best[:, :, heads, 0:1].to_broadcast([P, G, 2, PR_K]), ALU.subtract
                                  ).then_inc(diff_done, 1)
                eng.tensor_scalar(posk[:, 0, :, :, :], pos[:, :, heads, :], 4, None, ALU.logical_shift_right
                                  ).then_inc(dve_step, 1)
                n.up()
                eng.tensor_scalar(posk[:, 1, :, :, :], pos[:, :, heads, :], 15, None, ALU.bitwise_and
                                  ).then_inc(dve_step, 1)
                eng.wait_ge(dve_step, n.up())
                eng.tensor_copy(posf[:, :, :, :, :], posk[:, :, :, :, :]).then_inc(dve_step, 1)
                n.up()

            def compare(b):
                eng.wait_ge(dve_step, n.n)
                for g in range(G):
                    for half in range(2):
                        wide = [P, 2, PR_K, PR_K]
                        eng.tensor_tensor(eq[:, g, half, :, :, :], posf[:, half, g, :, :].unsqueeze(3).to_broadcast(wide),
                                          chip.iota[:, 0:PR_K].unsqueeze(1).unsqueeze(1).to_broadcast(wide),
                                          ALU.is_equal).then_inc(eq_done, 1)

            def take_keys(b):
                for g in range(G):
                    for half in range(2):
                        eng.wait_ge(key_done, 4 * b + 2 * g + half + 1)
                        eng.tensor_reduce(key[:, g, half, 2 * b * PR_K:2 * (b + 1) * PR_K].rearrange("p (h k) -> p h k", h=2),
                                          eq[:, g, half, :, :, :], AX.X, ALU.add).then_inc(dve_step, 1)
                        n.up()

            for b in range(4):
                best_keys(b)
                best_pairs(b)
                if b >= 1:
                    take_keys(b - 1)
                compare(b)
            eng.wait_ge(exp_done, 4)
            gv = gate[:, :, :].rearrange("p g (h k) -> p (g h) k", h=PR_H)
            gs = gsum[:, :, :].rearrange("p g h -> p (g h)")
            eng.tensor_reduce(gs, gv, AX.X, ALU.add).then_inc(dve_step, 1)
            eng.wait_ge(dve_step, n.up())
            eng.reciprocal(gs, gs).then_inc(dve_step, 1)
            eng.wait_ge(dve_step, n.up())
            eng.tensor_tensor(gv, gv, gs.unsqueeze(2).to_broadcast([P, G * PR_H, PR_K]), ALU.mult
                              ).then_inc(dve_step, 1)
            n.up()
            take_keys(3)
            eng.wait_ge(dve_step, n.n)
            eng.sem_inc(sel_done, 1)
            eng.wait_ge(vec_ps, 1)
            later = chip.mod[:, vec_to:vec_to + vec_cols // P]
            eng.tensor_tensor(later, later, bank[6][:, 0:vec_cols // P], ALU.add).then_inc(dve_step, 1)
            eng.wait_ge(dve_step, n.up())



def peer_experts(nc, chip, a, layer, st):
    TILES = PR_EXPERTS // P
    SLOTS = 4
    TOK = 4
    HOT = 4
    AHEAD = 2
    with ExitStack() as ctx:
        ph = Phase(nc, ctx, f"ex{layer}")
        bank = chip.bank
        act = ph.sb("act", [P, TILES, T])
        stream = [ph.sb(f"stream{k}", [P, D]) for k in range(SLOTS)]
        hi = [ph.sb(f"hi{k}", [P, D], F32R) for k in range(2)]
        lo = [ph.sb(f"lo{k}", [P, D], F32R) for k in range(2)]
        with ExitStack() as step2:
            hot_sb = lambda name: step2.enter_context(nc.sbuf_tensor(f"ex{layer}_{name}", [SEL, TOK, P], F32))
            oj = [hot_sb(f"oj{k}") for k in range(HOT)]
            oi = [hot_sb(f"oi{k}") for k in range(HOT)]
        whi = [ph.sb(f"whi{k}", [P, T], F32R) for k in range(2)]
        wlo = [ph.sb(f"wlo{k}", [P, T], F32R) for k in range(2)]
        res = Residual(ph, chip, mod_col(layer, G2), [bank[4], bank[5]])
        if 4 * T + 2 * D < 2 * HOT * TOK * P:
            ph.sb("rest_of_hot", [P, 2 * HOT * TOK * P - 4 * T - 2 * D])
        diff_bank = [bank[2 + k] for k in range(HOT)]
        gate_bank = [bank[(6 + k) % 8] for k in range(HOT)]

        loaded = [ph.sem(f"loaded{k}") for k in range(SLOTS)]
        slot_free = ph.sem("slot_free")
        turned = ph.sem("turned")
        hi_done, lo_done = ph.sem("hi_done"), ph.sem("lo_done")
        half_free = ph.sem("half_free")
        parts_free = ph.sem("parts_free")
        dot_ps, dot_free = ph.sem("dot_ps"), ph.sem("dot_free")
        dj_done, abs_done, oj_done, oi_done, hot_free, gate_ps, gate_free = (
            ph.sem(n) for n in ("dj_done", "abs_done", "oj_done", "oi_done", "hot_free", "gate_ps", "gate_free"))
        vhi, vlo, wparts, wl_done, v_free = (ph.sem(n) for n in ("vhi", "vlo", "wparts", "wl_done", "v_free"))
        diff_ps = ph.sem("diff_ps")
        block = ctx.enter_context(nc.Block())

        def tiles(eng, body, ahead=None, skip=0):
            if ahead:
                ahead(0, 0)
            first = skip
            for k in range(first):
                if ahead:
                    ahead(k + 1, (k + 1) % SLOTS)
                body(k, k % SLOTS)
            with eng.Fori(first // SLOTS, TILES // SLOTS - 1) as i:
                for k in range(SLOTS):
                    t = i * SLOTS + k
                    if ahead:
                        ahead(i * SLOTS + (k + 1), (k + 1) % SLOTS)
                    body(t, k)
            for k in range(SLOTS):
                t = TILES - SLOTS + k
                if ahead and k < SLOTS - 1:
                    ahead(t + 1, k + 1)
                body(t, k)

        @block.sync
        def _(eng):
            def load_u(t, k):
                eng.wait_ge(slot_free, t + 1)
                eng.dma_start(stream[k][:, :], a["peer_u"][layer][bass.ds(t * P, P), :]).then_inc(loaded[k], 16)

            def load_v(t, k):
                eng.wait_ge(slot_free, t + (TILES + 1))
                eng.dma_start(stream[k][:, :], a["peer_v"][layer][bass.ds(t * P, P), :]).then_inc(loaded[k], 16)

            tiles(eng, load_u)
            tiles(eng, load_v)

        @block.tensor
        def _(eng):
            eng.sem_inc(slot_free, SLOTS)

            def turn(t, k):
                p = k % 2
                eng.wait_ge(loaded[k], (t - k) * (16 // SLOTS) + 16)
                for half in range(2):
                    eng.wait_ge(half_free, t * 2 + (half + 1))
                    for c in range(4):
                        col = half * 512 + c * P
                        mm = eng.transpose(bank[2 * p + half][:, c * P:(c + 1) * P], stream[k][:, col:col + P],
                                           chip.ident[:, :])
                    mm.then_inc(turned, 1)

            def dots(t, k):
                p = k % 2
                eng.wait_ge(lo_done, t * 2 + 2)
                eng.wait_ge(dot_free, t + 1)
                out = bank[4 + p][:, 0:T]
                for c in range(DC):
                    col = slice(c * P, (c + 1) * P)
                    eng.matmul(out, hi[p][:, col], st.xhl[:, c, 0, :], start=(c == 0), stop=False)
                    eng.matmul(out, hi[p][:, col], st.xhl[:, c, 1, :], start=False, stop=False)
                    mm = eng.matmul(out, lo[p][:, col], st.xhl[:, c, 0, :], start=False, stop=(c == DC - 1))
                mm.then_inc(dot_ps, 1)

            tiles(eng, dots, ahead=turn)

            def diffs(q, k, g):
                eng.wait_ge(oi_done, q + 1)
                out = diff_bank[k][:, :].rearrange("p (t n) -> p t n", t=TOK)
                pick = chip.minus_ident_r[:, bass.ds(q * TOK - g * P, TOK)]
                eng.matmul(out, st.i[:, g, :], pick.unsqueeze(2).to_broadcast([P, TOK, P]), start=True, stop=False)
                eng.matmul(out, chip.ones_r[:, :], chip.iota_r[:, :].unsqueeze(1).to_broadcast([1, TOK, P]),
                           start=False, stop=True).then_inc(diff_ps, 1)

            def gates(q, k):
                eng.wait_ge(oj_done, q + 1)
                eng.wait_ge(oi_done, q + HOT + 1)
                eng.wait_ge(gate_free, q + 1)
                for n in range(TOK):
                    mm = eng.matmul(gate_bank[k][:, n * P:(n + 1) * P], oj[k][:, n, :], oi[k][:, n, :],
                                    start=True, stop=True)
                mm.then_inc(gate_ps, 1)

            eng.wait_ge(half_free, 2 * TILES + 4)
            eng.wait_ge(dot_free, TILES + 2)
            steps = P // TOK // HOT
            for g in range(G):
                for k in range(AHEAD):
                    diffs(g * P // TOK + k, k, g)
                with eng.Fori(g * steps, (g + 1) * steps - 1) as i:
                    for k in range(HOT):
                        diffs(i * HOT + (k + AHEAD), (k + AHEAD) % HOT, g)
                        gates(i * HOT + k, k)
                for k in range(HOT):
                    q = (g + 1) * P // TOK - HOT + k
                    if k + AHEAD < HOT:
                        diffs(q + AHEAD, k + AHEAD, g)
                    gates(q, k)

            def sums(t, k, first=False, last=False):
                p = k % 2
                eng.wait_ge(wl_done, t + 1)
                for half in range(2):
                    cols = slice(half * 512, (half + 1) * 512)
                    eng.wait_ge(vlo, t * 2 + (half + 1))
                    for g in range(G):
                        tok = slice(g * P, (g + 1) * P)
                        for n, (w, v) in enumerate(((whi, hi), (whi, lo), (wlo, hi))):
                            mm = eng.matmul(bank[2 * g + half][:, :], w[p][:, tok], v[p][:, cols],
                                            start=(first and n == 0), stop=(last and n == 2))
                mm.then_inc(v_free, 1)

            res.pe(eng)
            for k in range(SLOTS):
                sums(k, k, first=(k == 0))
            with eng.Fori(1, TILES // SLOTS - 1) as i:
                for k in range(SLOTS):
                    sums(i * SLOTS + k, k)
            for k in range(SLOTS):
                sums(TILES - SLOTS + k, k, last=(k == SLOTS - 1))

        @block.scalar
        def _(eng):
            nc.scalar.preload_act_table(ACT.Gelu)

            def split(t, k):
                p = k % 2
                for half in range(2):
                    eng.wait_ge(turned, t * 2 + (half + 1))
                    if half == 0:
                        eng.wait_ge(dot_ps, t + 1)
                    eng.activation(hi[p][:, half * 512:(half + 1) * 512], bank[2 * p + half][:, :], ACT.Copy
                                   ).then_inc(hi_done, 1)

            def gelu(t, k):
                eng.wait_ge(dot_ps, t + 3)
                eng.activation(act[:, bass.ds(t, 1), :], bank[4 + k % 2][:, 0:T], ACT.Gelu).then_inc(dot_free, 1)

            eng.sem_inc(dot_ps, 2)
            eng.sem_inc(dot_free, 2)
            tiles(eng, gelu, ahead=split)

            def parts(t, k):
                p = k % 2
                eng.wait_ge(loaded[k], (t - k) * (16 // SLOTS) + (16 + 16 * TILES // SLOTS))
                eng.wait_ge(v_free, t + 1)
                eng.activation(whi[p][:, :], act[:, bass.ds(t, 1), :], ACT.Copy).then_inc(wparts, 1)
                for half in range(2):
                    cols = slice(half * 512, (half + 1) * 512)
                    eng.activation(hi[p][:, cols], stream[k][:, cols], ACT.Copy).then_inc(vhi, 1)

            def hot(q, k):
                eng.wait_ge(dj_done, q + 1)
                eng.activation(oj[k][:, :, :], oj[k][:, :, :], ACT.Abs).then_inc(abs_done, 1)
                eng.wait_ge(abs_done, q + 1)
                eng.activation(oj[k][:, :, :], oj[k][:, :, :], ACT.Relu, bias=1.0, scale=-1.0).then_inc(oj_done, 1)

            with eng.Fori(0, T // TOK // HOT) as i:
                for k in range(HOT):
                    hot(i * HOT + k, k)

            eng.sem_inc(v_free, 2)
            eng.wait_ge(gate_free, T // TOK + HOT)
            for k in range(2):
                parts(k, k)
            res.act(eng)
            for k in range(2, SLOTS):
                parts(k, k)
            with eng.Fori(1, TILES // SLOTS) as i:
                for k in range(SLOTS):
                    parts(i * SLOTS + k, k)

        @block.gpsimd
        def _(eng):
            def hot(q, k):
                eng.wait_ge(hot_free, q + 1)
                eng.tensor_tensor(oj[k][:, :, :], chip.iota[:, :].unsqueeze(1).to_broadcast([SEL, TOK, P]),
                                  st.jT[:, bass.ds(q * TOK, TOK)].unsqueeze(2).to_broadcast([SEL, TOK, P]),
                                  ALU.subtract).then_inc(dj_done, 1)

            with eng.Fori(0, T // TOK // HOT) as i:
                for k in range(HOT):
                    hot(i * HOT + k, k)

        @block.vector
        def _(eng):
            eng.sem_inc(half_free, 4)

            def low(t, k):
                p = k % 2
                for half in range(2):
                    cols = slice(half * 512, (half + 1) * 512)
                    eng.wait_ge(hi_done, t * 2 + (half + 1))
                    eng.tensor_tensor(lo[p][:, cols], bank[2 * p + half][:, :], hi[p][:, cols].bitcast(F32),
                                      ALU.subtract).then_inc(lo_done, 1)
                    eng.wait_ge(lo_done, t * 2 + (half + 1))
                    eng.sem_inc(half_free, 1)
                eng.sem_inc(slot_free, 1)

            with eng.Fori(0, TILES // SLOTS) as i:
                for k in range(SLOTS):
                    low(i * SLOTS + k, k)

            eng.sem_inc(hot_free, HOT)
            eng.sem_inc(oi_done, HOT)
            eng.sem_inc(gate_free, HOT)

            def hot(q, k):
                eng.wait_ge(gate_ps, q + 1)
                eng.wait_ge(diff_ps, q + 1)
                gate = st.gT[:, bass.ds(q * TOK, TOK)].unsqueeze(2).to_broadcast([SEL, TOK, P])
                eng.scalar_tensor_tensor(out=oi[k][:, :, :], in0=diff_bank[k][:, :].rearrange("p (t n) -> p t n", t=TOK),
                                         scalar=0.0, in1=gate, op0=ALU.is_equal, op1=ALU.mult).then_inc(oi_done, 1)

            def apply(q, k):
                eng.wait_ge(gate_ps, q + HOT + 1)
                eng.sem_inc(hot_free, 1)
                cell = act[:, :, bass.ds(q * TOK, TOK)]
                eng.tensor_tensor(cell, gate_bank[k][:, :].rearrange("p (t i) -> p i t", t=TOK), cell, ALU.mult
                                  ).then_inc(gate_free, 1)

            eng.sem_inc(gate_ps, HOT)
            eng.wait_ge(dot_free, TILES + 2)
            for k in range(AHEAD):
                hot(k, k)
            last = T // TOK
            with eng.Fori(0, last // HOT - 1) as i:
                for k in range(HOT):
                    hot(i * HOT + (k + AHEAD), (k + AHEAD) % HOT)
                    apply(i * HOT + k, k)
            for k in range(HOT):
                if k + AHEAD < HOT:
                    hot(last - HOT + k + AHEAD, k + AHEAD)
                apply(last - HOT + k, k)

            def low_parts(t, k):
                p = k % 2
                eng.wait_ge(wparts, t + 1)
                eng.tensor_tensor(wlo[p][:, :], act[:, bass.ds(t, 1), :], whi[p][:, :].bitcast(F32), ALU.subtract
                                  ).then_inc(wl_done, 1)
                for half in range(2):
                    cols = slice(half * 512, (half + 1) * 512)
                    eng.wait_ge(vhi, t * 2 + (half + 1))
                    eng.tensor_tensor(lo[p][:, cols], stream[k][:, cols], hi[p][:, cols].bitcast(F32), ALU.subtract
                                      ).then_inc(vlo, 1)
                eng.wait_ge(vlo, t * 2 + 2)
                eng.sem_inc(slot_free, 1)

            eng.wait_ge(gate_free, last + HOT)
            res.dve_diag(eng)
            with eng.Fori(0, TILES // SLOTS) as i:
                for k in range(SLOTS):
                    low_parts(i * SLOTS + k, k)

            res.dve_add(eng, [(lambda: eng.wait_ge(v_free, TILES + 2), bank[2 * g + half][:, :], g, 1,
                               half * WCOLS, WCOLS) for g in range(G) for half in range(2)])


def store(nc, chip, out):
    with ExitStack() as ctx:
        stored = ctx.enter_context(nc.semaphore("stored"))
        block = ctx.enter_context(nc.Block())

        @block.sync
        def _(eng):
            for g in range(G):
                eng.dma_start(out[g * P:(g + 1) * P, :], chip.x[:, g, :]).then_inc(stored, 16)
            eng.wait_ge(stored, 16 * G)


def program(nc, a, out):
    with ExitStack() as ctx:
        chip = Chip(nc, ctx)
        adaln_vectors(nc, chip, a)
        mixers = (mlstm, fox)
        for layer, mixer in enumerate(mixers):
            mixer(nc, chip, a)
            with ExitStack() as inner:
                st = PeerState(Phase(nc, inner, f"peer{layer}"))
                peer_route(nc, chip, a, layer, st)
                peer_experts(nc, chip, a, layer, st)
        store(nc, chip, out)


_INS = ["x", "c", "ada_w", "ada_b", "mix_norm", "ffn_norm", "a_w_in", "a_b_i", "a_b_f", "a_h_norm", "a_w_out",
        "kv_ada_w", "kv_ada_b", "kv_norm", "kv_w", "kv_b_f", "kv_k_norm", "b_w_qo", "b_q_norm", "b_w_out",
        "peer_wq", "peer_subkeys", "peer_u", "peer_v"]


def kernel(**inputs):
    import numpy as np
    import concourse.bacc as bacc
    from concourse.bass_utils import run_bass_kernel_spmd

    nc = bacc.Bacc("TRN2", target_bir_lowering=False, num_devices=1)
    arrays, args = {}, {}
    for name in _INS:
        v = np.ascontiguousarray(inputs[name])
        if name == "x":
            v = v.reshape(T, D)
        arrays[f"in_{name}"] = v
        args[name] = nc.dram_tensor(f"in_{name}", v.shape, mybir.dt.from_np(v.dtype), kind="ExternalInput").ap()
    out = nc.dram_tensor("out_x", (T, D), F32, kind="ExternalOutput").ap()
    program(nc, args, out)
    r = run_bass_kernel_spmd(nc, [arrays], core_ids=[0])
    return r.results[0]["out_x"].reshape(1, T, D)
```
